# Optimizing a Trainium2 kernel written in Bass

```python
import math
import jax, jax.numpy as jnp
from jax import lax
import numpy as np

D_MODEL = 1024
BATCH = 1
SEQ = 512
DEPTH = 2

CHUNK = 64
NORM_EPS = 1e-6

RWKV_HEAD_SIZE = 64
RWKV_WIDTH = D_MODEL
RWKV_HEADS = RWKV_WIDTH // RWKV_HEAD_SIZE
DECAY_LORA = 64
ICLR_LORA = 64
VRES_LORA = 32
GATE_LORA = 160
RWKV_GN_EPS = 64e-5

SSD_WIDTH = 2 * D_MODEL
SSD_HEAD_DIM = 64
SSD_HEADS = SSD_WIDTH // SSD_HEAD_DIM
SSD_STATE = 128
SSD_GROUPS = 4
SSD_CONV = 4
SSD_CONV_CH = SSD_WIDTH + 2 * SSD_GROUPS * SSD_STATE

PEER_HEADS = 8
PEER_NKEYS = 128
PEER_EXPERTS = PEER_NKEYS * PEER_NKEYS
PEER_TOPK = 16
PEER_QDIM = 256
PEER_TOKEN_BLOCK = 128

RWKV_SPLITS = (RWKV_WIDTH, RWKV_WIDTH, RWKV_WIDTH, DECAY_LORA, ICLR_LORA, GATE_LORA)
RWKV_PROJ = sum(RWKV_SPLITS)
SSD_SPLITS = (SSD_WIDTH, SSD_CONV_CH, SSD_HEADS)
SSD_PROJ = sum(SSD_SPLITS)
GATE_PROJ = 2 * D_MODEL
IN_PROJ = RWKV_PROJ + SSD_PROJ + GATE_PROJ

kernel_name = 'hybrid_rwkv7_ssd_peer_block'

def rmsnorm(x, g):
    xf = x.astype(jnp.float32)
    y = xf * lax.rsqrt(jnp.mean(xf * xf, axis=-1, keepdims=True) + NORM_EPS)
    return (y * g.astype(jnp.float32)).astype(x.dtype)

def split_last(t, sizes):
    out, start = [], 0
    for s in sizes:
        out.append(t[..., start:start + s])
        start += s
    return out

def shift_prev(x):
    return jnp.pad(x, ((0, 0), (1, 0), (0, 0)))[:, :-1]

def causal_depthwise_conv(x, w, b):
    T = x.shape[1]
    xp = jnp.pad(x, ((0, 0), (SSD_CONV - 1, 0), (0, 0)))
    y = b
    for j in range(SSD_CONV):
        y = y + xp[:, j:j + T] * w[j]
    return y

def rwkv7_recurrence(r, w, k, v, a, b):
    Bsz, T, H, N = r.shape

    def step(S, inp):
        r_t, w_t, k_t, v_t, a_t, b_t = inp
        sa = jnp.einsum('bhvk,bhk->bhv', S, a_t)
        S = S * w_t[:, :, None, :] + sa[..., None] * b_t[:, :, None, :] + v_t[..., None] * k_t[:, :, None, :]
        return S, jnp.einsum('bhvk,bhk->bhv', S, r_t)

    xs = tuple(jnp.moveaxis(t.astype(jnp.float32), 1, 0) for t in (r, w, k, v, a, b))
    _, ys = lax.scan(step, jnp.zeros((Bsz, H, N, N), jnp.float32), xs)
    return jnp.moveaxis(ys, 0, 1)

def rwkv7_time_mix(p, v_first, vres, mu, w0, w2, a0, a2, g2, k_k, k_a, r_k, ln_w, ln_b, w_branch):
    Bsz, T, _ = p.shape
    H, N = RWKV_HEADS, RWKV_HEAD_SIZE
    p = p + (shift_prev(p) - p) * mu
    r, k, v, wd, ad, gd = split_last(p, RWKV_SPLITS)
    w_log = -jax.nn.softplus(-(w0 + jnp.tanh(wd) @ w2).astype(jnp.float32)) - 0.5
    decay = jnp.exp(-jnp.exp(w_log))
    a = jax.nn.sigmoid(a0 + ad @ a2)
    g = jax.nn.sigmoid(gd) @ g2
    if vres is None:
        v_first = v
    else:
        v0, v1, v2 = vres
        v = v + (v_first - v) * jax.nn.sigmoid(v0 + (v @ v1) @ v2)
    heads = lambda t: t.reshape(Bsz, T, H, N)
    r, k, v, a, decay = heads(r), heads(k), heads(v), heads(a), heads(decay)
    kk = (k * k_k.reshape(H, N)).astype(jnp.float32)
    kk = kk * lax.rsqrt(jnp.sum(kk * kk, axis=-1, keepdims=True) + 1e-12)
    k = k * (1.0 + (a - 1.0) * k_a.reshape(H, N))
    y = rwkv7_recurrence(r, decay, k, v, -kk, kk * a)
    mean = jnp.mean(y, axis=-1, keepdims=True)
    var = jnp.mean(jnp.square(y - mean), axis=-1, keepdims=True)
    y = (y - mean) * lax.rsqrt(var + RWKV_GN_EPS) * ln_w.reshape(H, N) + ln_b.reshape(H, N)
    y = y + jnp.sum(r * k * r_k, axis=-1, keepdims=True) * v
    y = y.reshape(Bsz, T, RWKV_WIDTH).astype(p.dtype) * g
    return y @ w_branch, v_first

def ssd_chunked_scan(X, a, Bm, Cm):
    Bsz, T, H, P = X.shape
    G, N = Bm.shape[2], Bm.shape[3]
    Hg = H // G
    nc = T // CHUNK
    to_chunks = lambda t: jnp.moveaxis(t.reshape(Bsz, nc, CHUNK, *t.shape[2:]), 1, 0)
    Xc = to_chunks(X.reshape(Bsz, T, G, Hg, P))
    ac = to_chunks(a.reshape(Bsz, T, G, Hg))
    Bc, Cc = to_chunks(Bm), to_chunks(Cm)
    causal = jnp.tril(jnp.ones((CHUNK, CHUNK), dtype=bool))[None, :, :, None, None]

    def step(state, inp):
        x_c, a_c, b_c, c_c = inp
        acs = jnp.cumsum(a_c.astype(jnp.float32), axis=1)
        seg = acs[:, :, None] - acs[:, None, :]
        Lmat = jnp.exp(jnp.where(causal, seg, -jnp.inf))
        cb = jnp.einsum('bign,bjgn->bijg', c_c, b_c)
        y_diag = jnp.einsum('bijgh,bjghp->bighp', Lmat * cb[..., None], x_c)
        y_off = jnp.einsum('bign,bghpn->bighp', c_c, state) * jnp.exp(acs)[..., None]
        decay_to_end = jnp.exp(acs[:, -1:] - acs)
        state = state * jnp.exp(acs[:, -1])[..., None, None] + jnp.einsum('bjgn,bjgh,bjghp->bghpn', b_c, decay_to_end, x_c)
        return state, y_diag + y_off

    state0 = jnp.zeros((Bsz, G, Hg, P, N), jnp.float32)
    _, ys = lax.scan(step, state0, (Xc, ac, Bc, Cc))
    return jnp.moveaxis(ys, 0, 1).reshape(Bsz, T, H, P)

def ssd_mixer(p, conv_w, conv_b, dt_bias, A_log, D_skip, norm_g, w_branch):
    Bsz, T, _ = p.shape
    z, xbc, dt_raw = split_last(p, SSD_SPLITS)
    xbc = jax.nn.silu(causal_depthwise_conv(xbc, conv_w, conv_b))
    xs, Bm, Cm = split_last(xbc, (SSD_WIDTH, SSD_GROUPS * SSD_STATE, SSD_GROUPS * SSD_STATE))
    dt = jax.nn.softplus((dt_raw + dt_bias).astype(jnp.float32))
    A = -jnp.exp(A_log.astype(jnp.float32))
    xh = xs.reshape(Bsz, T, SSD_HEADS, SSD_HEAD_DIM)
    y = ssd_chunked_scan(xh * dt[..., None], dt * A,
                         Bm.reshape(Bsz, T, SSD_GROUPS, SSD_STATE),
                         Cm.reshape(Bsz, T, SSD_GROUPS, SSD_STATE))
    y = y + xh * D_skip[:, None]
    y = y.reshape(Bsz, T, SSD_WIDTH) * jax.nn.silu(z)
    gs = SSD_WIDTH // SSD_GROUPS
    y = rmsnorm(y.reshape(Bsz, T, SSD_GROUPS, gs), norm_g.reshape(SSD_GROUPS, gs))
    return y.reshape(Bsz, T, SSD_WIDTH).astype(p.dtype) @ w_branch

def peer_ffn(u, w_q, sub_keys, expert_down, expert_up):
    Bsz, T, D = u.shape
    half = PEER_QDIM // 2
    blocks = u.reshape(-1, PEER_TOKEN_BLOCK, D)

    def block_fn(xb):
        q = (xb @ w_q).reshape(PEER_TOKEN_BLOCK, PEER_HEADS, 2, half)
        s = jnp.einsum('thcd,hckd->thck', q, sub_keys).astype(jnp.float32)
        top_s, top_i = lax.top_k(s, PEER_TOPK)
        cand_s = (top_s[:, :, 0, :, None] + top_s[:, :, 1, None, :]).reshape(PEER_TOKEN_BLOCK, PEER_HEADS, -1)
        cand_i = (top_i[:, :, 0, :, None] * PEER_NKEYS + top_i[:, :, 1, None, :]).reshape(PEER_TOKEN_BLOCK, PEER_HEADS, -1)
        best_s, best_pos = lax.top_k(cand_s, PEER_TOPK)
        idx = jnp.take_along_axis(cand_i, best_pos, axis=-1)
        gate = jax.nn.softmax(best_s, axis=-1)
        act = jax.nn.gelu(jnp.einsum('td,thkd->thk', xb, expert_down[idx]).astype(jnp.float32))
        return jnp.einsum('thk,thkd->td', (gate * act).astype(xb.dtype), expert_up[idx])

    return lax.map(block_fn, blocks).reshape(Bsz, T, D)

def setup_inputs(seed: int = 0) -> dict:
    key = jax.random.key(seed)
    ks = iter(jax.random.split(key, 40))
    nrm = lambda shape, scale: jax.random.normal(next(ks), shape, jnp.float32) * scale
    uni = lambda shape, lo, hi: jax.random.uniform(next(ks), shape, jnp.float32, lo, hi)
    L, D = DEPTH, D_MODEL
    dt_init = jnp.exp(uni((L, SSD_HEADS), math.log(1e-3), math.log(1e-1)))
    dt_bias = dt_init + jnp.log(-jnp.expm1(-dt_init))
    return {
        'x': nrm((BATCH, SEQ, D), 1.0),
        'norm_mix_g': 1.0 + nrm((L, D), 0.02),
        'w_in': nrm((L, D, IN_PROJ), D ** -0.5),
        'rwkv_mu': uni((L, RWKV_PROJ), 0.0, 1.0),
        'rwkv_w0': uni((L, RWKV_WIDTH), -5.0, 1.0),
        'rwkv_w2': nrm((L, DECAY_LORA, RWKV_WIDTH), 0.1 * DECAY_LORA ** -0.5),
        'rwkv_a0': nrm((L, RWKV_WIDTH), 0.1),
        'rwkv_a2': nrm((L, ICLR_LORA, RWKV_WIDTH), 0.1 * ICLR_LORA ** -0.5),
        'rwkv_g2': nrm((L, GATE_LORA, RWKV_WIDTH), GATE_LORA ** -0.5),
        'rwkv_v0': 1.0 + nrm((L - 1, RWKV_WIDTH), 0.1),
        'rwkv_v1': nrm((L - 1, RWKV_WIDTH, VRES_LORA), RWKV_WIDTH ** -0.5),
        'rwkv_v2': nrm((L - 1, VRES_LORA, RWKV_WIDTH), VRES_LORA ** -0.5),
        'rwkv_k_k': 0.85 + nrm((L, RWKV_WIDTH), 0.05),
        'rwkv_k_a': 1.0 + nrm((L, RWKV_WIDTH), 0.05),
        'rwkv_r_k': nrm((L, RWKV_HEADS, RWKV_HEAD_SIZE), 0.1),
        'rwkv_ln_w': 1.0 + nrm((L, RWKV_WIDTH), 0.02),
        'rwkv_ln_b': nrm((L, RWKV_WIDTH), 0.02),
        'w_rwkv_branch': nrm((L, RWKV_WIDTH, D), RWKV_WIDTH ** -0.5),
        'ssd_conv_w': nrm((L, SSD_CONV, SSD_CONV_CH), 0.5),
        'ssd_conv_b': nrm((L, SSD_CONV_CH), 0.02),
        'ssd_dt_bias': dt_bias,
        'ssd_A_log': jnp.log(uni((L, SSD_HEADS), 1.0, 16.0)),
        'ssd_D': 1.0 + nrm((L, SSD_HEADS), 0.1),
        'ssd_norm_g': 1.0 + nrm((L, SSD_WIDTH), 0.02),
        'w_ssd_branch': nrm((L, SSD_WIDTH, D), SSD_WIDTH ** -0.5),
        'w_out': nrm((L, D, D), D ** -0.5),
        'norm_ffn_g': 1.0 + nrm((L, D), 0.02),
        'peer_w_q': nrm((L, D, PEER_HEADS * PEER_QDIM), D ** -0.5),
        'peer_sub_keys': nrm((L, PEER_HEADS, 2, PEER_NKEYS, PEER_QDIM // 2), (PEER_QDIM // 2) ** -0.5),
        'peer_down': nrm((L, PEER_EXPERTS, D), D ** -0.5),
        'peer_up': nrm((L, PEER_EXPERTS, D), PEER_HEADS ** -0.5),
        'norm_final_g': 1.0 + nrm((D,), 0.02),
    }

def reference(x, norm_mix_g, w_in, rwkv_mu, rwkv_w0, rwkv_w2, rwkv_a0, rwkv_a2, rwkv_g2,
              rwkv_v0, rwkv_v1, rwkv_v2, rwkv_k_k, rwkv_k_a, rwkv_r_k, rwkv_ln_w, rwkv_ln_b,
              w_rwkv_branch, ssd_conv_w, ssd_conv_b, ssd_dt_bias, ssd_A_log, ssd_D, ssd_norm_g,
              w_ssd_branch, w_out, norm_ffn_g, peer_w_q, peer_sub_keys, peer_down, peer_up,
              norm_final_g):
    h = x
    v_first = None
    for l in range(DEPTH):
        u = rmsnorm(h, norm_mix_g[l])
        proj = u @ w_in[l]
        p_rwkv, p_ssd, gates = split_last(proj, (RWKV_PROJ, SSD_PROJ, GATE_PROJ))
        vres = None if l == 0 else (rwkv_v0[l - 1], rwkv_v1[l - 1], rwkv_v2[l - 1])
        y_a, v_first = rwkv7_time_mix(p_rwkv, v_first, vres, rwkv_mu[l], rwkv_w0[l], rwkv_w2[l],
                                      rwkv_a0[l], rwkv_a2[l], rwkv_g2[l], rwkv_k_k[l], rwkv_k_a[l],
                                      rwkv_r_k[l], rwkv_ln_w[l], rwkv_ln_b[l], w_rwkv_branch[l])
        y_b = ssd_mixer(p_ssd, ssd_conv_w[l], ssd_conv_b[l], ssd_dt_bias[l], ssd_A_log[l], ssd_D[l],
                        ssd_norm_g[l], w_ssd_branch[l])
        g_a, g_b = split_last(gates, (D_MODEL, D_MODEL))
        mixed = jax.nn.sigmoid(g_a) * y_a + jax.nn.sigmoid(g_b) * y_b
        h = h + mixed @ w_out[l]
        h = h + peer_ffn(rmsnorm(h, norm_ffn_g[l]), peer_w_q[l], peer_sub_keys[l], peer_down[l], peer_up[l])
    return rmsnorm(h, norm_final_g)


_drawn_inputs = setup_inputs


def setup_inputs(seed=0):
    import zlib

    import numpy as np

    out = dict(_drawn_inputs(seed))
    spreads = {}
    factors = {'rwkv_w2': 4.321,
     'rwkv_v0': 19.85,
     'norm_final_g': 8.421,
     'rwkv_v1': 3.492,
     'rwkv_v2': 3.508}
    for name, (base, spread) in spreads.items():
        noise = np.random.default_rng([zlib.crc32(name.encode()), seed]).standard_normal(out[name].shape)
        drawn = base * np.exp(spread * noise) if base else spread * noise
        out[name] = __import__('jax').numpy.asarray(drawn.astype(out[name].dtype))
    for name, factor in factors.items():
        out[name] = (out[name] * factor).astype(out[name].dtype)
    return out
```

```python
from contextlib import ExitStack

import numpy as np
import concourse.bass as bass
from concourse import mybir

F32 = mybir.dt.float32
F16 = mybir.dt.float16
U32 = mybir.dt.uint32
ALU = mybir.AluOpType
ACT = mybir.ActivationFunctionType
AX = mybir.AxisListType
ds = bass.ds

P = 128
LAYERS, T, D = 2, 512, 1024
KT = D // P
HS = 64
RWKV_TILES = D // P
CH = 64
NC = T // CH
SSD_HEADS, SSD_GROUPS, GROUP_HEADS = 32, 4, 8
SCH = 128
SNC = T // SCH
TB = T // P
HEADS, NKEYS, TOPK = 8, 128, 16
HK = HEADS * TOPK
NORM_EPS, GN_EPS, KK_EPS = 1e-6, 64e-5, 1e-12
DECAY_SCALE = float(np.exp(np.float64(-0.5)))

R0, K0, V0, WA, GD, GDT, Z0, X0, B0, C0, GA, GB = 0, 8, 16, 24, 25, 26, 27, 43, 59, 63, 67, 75
IN_TILES = 84
SLOTS = 4
W_SCALE = 64.0

PARAMS = {}
_at = 0
for _name, _n in (("norm_mix", 8), ("mu", 27), ("w0", 8), ("a0", 8), ("v0", 8), ("k_k", 8), ("k_a", 8),
                  ("r_k", 8), ("ln_w", 8), ("ln_b", 8), ("conv_w", 96), ("conv_b", 24), ("ssd_norm", 16),
                  ("D", 16), ("dt_bias", 1), ("A_log", 1), ("norm_ffn", 8), ("norm_final", 8)):
    PARAMS[_name] = _at
    _at += _n
N_PARAMS = _at

CONSTS = {}
_at = 0
for _name, _n in (("ident", 128), ("mean", 128), ("head_ones", 128), ("head_mean", 128), ("scores", 128),
                  ("levels_q", 6 * 64), ("level0_n", 64), ("eye64", 64), ("ssd_mask", 128),
                  ("chunk_start", 512), ("ssd_start", 512), ("iota128", 128), ("iota16", 16), ("eps", 3)):
    CONSTS[_name] = _at
    _at += _n
N_CONSTS = _at


def make_consts():
    c = np.zeros((P, N_CONSTS), np.float32)

    def put(name, a):
        c[:a.shape[0], CONSTS[name]:CONSTS[name] + a.shape[1]] = a

    i = np.arange(P)
    put("ident", np.eye(P, dtype=np.float32))
    put("mean", np.full((P, P), 1.0 / D, np.float32))
    same_head = (i[:, None] // HS == i[None, :] // HS).astype(np.float32)
    put("head_ones", same_head)
    put("head_mean", same_head / HS)
    j, q = i[:, None] % CH, i[None, :] % CH
    put("scores", np.where(i[None, :] < CH, j < q, j <= q).astype(np.float32))
    j, q = i[:, None] % CH, np.arange(CH)[None, :]
    for s in range(6):
        b = 1 << s
        m = (j // (2 * b) == q // (2 * b)) & (j % (2 * b) < b) & (q % (2 * b) >= b)
        c[:, CONSTS["levels_q"] + s * 64:CONSTS["levels_q"] + (s + 1) * 64] = m
    put("level0_n", ((j // 2 == q // 2) & (j % 2 == 1) & (q % 2 == 0)).astype(np.float32))
    put("eye64", (j == q).astype(np.float32))
    put("ssd_mask", np.where(i[:, None] <= i[None, :], 0.0, -1e30).astype(np.float32))
    t = np.arange(T)
    put("chunk_start", np.broadcast_to((t % CH != 0).astype(np.float32), (P, T)))
    put("ssd_start", np.broadcast_to((t % SCH != 0).astype(np.float32), (P, T)))
    put("iota128", np.broadcast_to(i.astype(np.float32), (P, P)))
    put("eps", np.broadcast_to(np.array([NORM_EPS, GN_EPS, KK_EPS], np.float32), (P, 3)))
    put("iota16", np.broadcast_to(np.arange(16, dtype=np.float32), (P, 16)))
    return c


def phase_sems(nc, phase, names):
    out = {}
    for name in names.split():
        name, _, n = name.partition("*")
        out[name] = [nc.alloc_semaphore(f"{phase}_{name}{i}") for i in range(int(n))] if n else nc.alloc_semaphore(f"{phase}_{name}")
    return out


def end_phase(nc, sems):
    flat = [s for v in sems.values() for s in (v if isinstance(v, list) else [v])]
    nc.clear_and_free_semaphores(flat)
    nc.all_engine_barrier()


def norm_phase(nc, bufs, name, gain_column, act_hi, act_lo, to_dram=None):
    hT, consts, params = bufs["hT"], bufs["consts"], bufs["params"]
    mean = consts[:, CONSTS["mean"]:CONSTS["mean"] + P]
    S = phase_sems(nc, name, "squared summed root_ready rstd_ready scaled high_done low_done stored")
    with nc.sbuf_tensor(name + "_sq", [P, 2, T], F32) as sq, nc.sbuf_tensor(name + "_rstd", [P, T], F32) as rstd, \
            nc.sbuf_tensor(name + "_root", [P, T], F32) as root, \
            nc.sbuf_tensor(name + "_u", [P, KT, T], F32) as u, nc.psum_tensor(name + "_ss", [P, 2, T], F32) as ss, \
            nc.Block() as block:

        @block.scalar
        def _(act):
            for k in range(KT):
                if k >= 2:
                    act.wait_ge(S["summed"], k - 1)
                nc.scalar.activation(sq[:, k % 2, :], hT[:, k, :], ACT.Square).then_inc(S["squared"], 1)
            act.wait_ge(S["summed"], KT)
            nc.scalar.activation(root[:], ss[:, 0, :], ACT.Sqrt, bias=consts[:, CONSTS["eps"]:CONSTS["eps"] + 1]).then_inc(S["root_ready"], 1)
            if to_dram is None:
                for k in range(KT):
                    act.wait_ge(S["scaled"], k + 1)
                    nc.scalar.activation(act_hi[:, k, :], u[:, k, :], ACT.Copy).then_inc(S["high_done"], 1)

        @block.tensor
        def _(pe):
            for k in range(KT):
                pe.wait_ge(S["squared"], k + 1)
                nc.tensor.matmul(ss[:, 0, :], mean, sq[:, k % 2, :], start=k == 0, stop=k == KT - 1).then_inc(S["summed"], 1)

        @block.vector
        def _(dve):
            dve.wait_ge(S["root_ready"], 1)
            nc.vector.reciprocal(rstd[:], root[:]).then_inc(S["rstd_ready"], 1)
            dve.wait_ge(S["rstd_ready"], 1)
            for k in range(KT):
                nc.vector.scalar_tensor_tensor(u[:, k, :], hT[:, k, :], params[:, gain_column + k:gain_column + k + 1],
                                               rstd[:], ALU.mult, ALU.mult).then_inc(S["scaled"], 1)
            if to_dram is None:
                for k in range(KT):
                    dve.wait_ge(S["high_done"], k + 1)
                    dve.wait_ge(S["scaled"], k + 1)
                    nc.vector.tensor_tensor(act_lo[:, k, :], u[:, k, :], act_hi[:, k, :], ALU.subtract).then_inc(S["low_done"], 1)

        @block.sync
        def _(sp):
            if to_dram is not None:
                for k in range(KT):
                    sp.wait_ge(S["scaled"], k + 1)
                    sp.dma_start(to_dram[:, k, :], u[:, k, :]).then_inc(S["stored"], 16)
                sp.wait_ge(S["stored"], 16 * KT)
    end_phase(nc, S)


def project_phase(nc, bufs, l, weights, tiles, act_hi, act_lo, out, name):
    S = phase_sems(nc, name, "w_loaded*4 high_ready*4 low_ready*4 product_done*4 copied*4 stored*4")
    steps = tiles // SLOTS
    with nc.sbuf_tensor(name + "_w", [P, SLOTS, KT, P], F32) as w, nc.sbuf_tensor(name + "_whi", [P, SLOTS, KT, P], F16) as w_hi, \
            nc.sbuf_tensor(name + "_wlo", [P, SLOTS, KT, P], F16) as w_lo, nc.sbuf_tensor(name + "_o", [P, SLOTS, T], F32) as o, \
            nc.psum_tensor(name + "_acc", [P, SLOTS, T], F32) as acc, nc.Block() as block:

        @block.sync
        def _(sp):
            for s in range(SLOTS):
                sp.dma_start(w[:, s].rearrange("p k n -> p (k n)"), weights[l * tiles + s]).then_inc(S["w_loaded"][s], 16)
            with sp.Fori(1, steps) as i:
                for s in range(SLOTS):
                    sp.wait_ge(S["low_ready"][s], i)
                    sp.dma_start(w[:, s].rearrange("p k n -> p (k n)"), weights[l * tiles + i * SLOTS + s]).then_inc(S["w_loaded"][s], 16)
                    sp.wait_ge(S["copied"][s], i)
                    sp.dma_start(out[(i - 1) * SLOTS + s], o[:, s]).then_inc(S["stored"][s], 16)
            for s in range(SLOTS):
                sp.wait_ge(S["copied"][s], steps)
                sp.dma_start(out[(steps - 1) * SLOTS + s], o[:, s]).then_inc(S["stored"][s], 16)
            for s in range(SLOTS):
                sp.wait_ge(S["stored"][s], 16 * steps)

        @block.scalar
        def _(act):
            def split_high(s):
                nc.scalar.activation(w_hi[:, s], w[:, s], ACT.Copy, scale=W_SCALE).then_inc(S["high_ready"][s], 1)

            for s in range(SLOTS):
                act.wait_ge(S["w_loaded"][s], 16)
                split_high(s)
            with act.Fori(1, steps) as i:
                for s in range(SLOTS):
                    act.wait_ge(S["w_loaded"][s], i * 16 + 16)
                    act.wait_ge(S["product_done"][s], i)
                    split_high(s)

        @block.tensor
        def _(pe):
            def product(s):
                for k in range(KT):
                    nc.tensor.matmul(acc[:, s], w_hi[:, s, k], act_hi[:, k], start=k == 0, stop=False)
                    nc.tensor.matmul(acc[:, s], w_hi[:, s, k], act_lo[:, k], start=False, stop=False)
                    last = nc.tensor.matmul(acc[:, s], w_lo[:, s, k], act_hi[:, k], start=False, stop=k == KT - 1)
                last.then_inc(S["product_done"][s], 1)

            for s in range(SLOTS):
                pe.wait_ge(S["low_ready"][s], 1)
                product(s)
            with pe.Fori(1, steps) as i:
                for s in range(SLOTS):
                    pe.wait_ge(S["low_ready"][s], i + 1)
                    pe.wait_ge(S["copied"][s], i)
                    product(s)

        @block.vector
        def _(dve):
            def split_rest(i, s):
                dve.wait_ge(S["high_ready"][s], i + 1)
                nc.vector.scalar_tensor_tensor(w_lo[:, s], w[:, s], W_SCALE, w_hi[:, s], ALU.mult, ALU.subtract).then_inc(S["low_ready"][s], 1)

            def copy_out(s):
                nc.vector.tensor_scalar(o[:, s], acc[:, s], 1.0 / W_SCALE, None, ALU.mult).then_inc(S["copied"][s], 1)

            for s in range(SLOTS):
                split_rest(0, s)
            for s in range(SLOTS):
                split_rest(1, s)
                dve.wait_ge(S["product_done"][s], 1)
                copy_out(s)
            with dve.Fori(2, steps) as i:
                for s in range(SLOTS):
                    split_rest(i, s)
                    dve.wait_ge(S["product_done"][s], i)
                    dve.wait_ge(S["stored"][s], i * 16 - 16)
                    copy_out(s)
            for s in range(SLOTS):
                dve.wait_ge(S["product_done"][s], steps)
                dve.wait_ge(S["stored"][s], steps * 16 - 16)
                copy_out(s)
    end_phase(nc, S)


PACK_COLS = 3 * P + 12
MU_R, MU_K, W0, A0, V0P, K_K, K_A, R_K, LN_W, LN_B = range(3 * P, 3 * P + 10)


def lora_phase(nc, bufs, l, lora, dram):
    params = bufs["params"]
    projected, v_mixed, v1 = dram["projected"], dram["v_mixed"], dram["v1"]
    low_wa, low_g, low_gv = lora
    S = phase_sems(nc, "lora", "zeroed raw_loaded v1_loaded diffed mixed ready vlow_done vlow_copied stored")
    mu = PARAMS["mu"]
    tiles = [WA, GD, GDT] + [V0 + k for k in range(KT)]
    n = len(tiles)
    with nc.sbuf_tensor("l_raw", [P, n, T + 1], F32) as raw, nc.sbuf_tensor("l_diff", [P, 2, T], F32) as diff, \
            nc.sbuf_tensor("l_mix", [P, n, T], F32) as mix, nc.sbuf_tensor("l_v1", [P, KT, 32], F32) as v1s, \
            nc.psum_tensor("l_vlow", [P, T], F32) as vlow, nc.Block() as block:

        @block.sync
        def _(sp):
            sp.dma_start(v1s[:].rearrange("p k n -> p (k n)"), v1[l]).then_inc(S["v1_loaded"], 16)
            for k in range(KT):
                sp.wait_ge(S["mixed"], 4 + k)
                sp.dma_start(v_mixed[l * KT + k], mix[:, 3 + k]).then_inc(S["stored"], 16)
            sp.wait_ge(S["stored"], 16 * KT)

        @block.scalar
        def _(act):
            for k, t in enumerate(tiles):
                act.dma_start(raw[:, k, 1:], projected[t]).then_inc(S["raw_loaded"], 16)
            act.wait_ge(S["mixed"], 3)
            nc.scalar.activation(low_wa[0:64, :], mix[0:64, 0], ACT.Tanh).then_inc(S["ready"], 1)
            nc.scalar.activation(low_wa[64:128, :], mix[64:128, 0], ACT.Copy).then_inc(S["ready"], 1)
            nc.scalar.activation(low_g[:], mix[:, 1], ACT.Sigmoid).then_inc(S["ready"], 1)
            nc.scalar.activation(low_gv[0:32, :], mix[0:32, 2], ACT.Sigmoid).then_inc(S["ready"], 1)
            act.wait_ge(S["vlow_done"], 1)
            nc.scalar.activation(low_gv[32:64, :], vlow[32:64, :], ACT.Copy).then_inc(S["vlow_copied"], 1)

        @block.gpsimd
        def _(pool):
            nc.gpsimd.memset(raw[:, :, 0:1], 0.0).then_inc(S["zeroed"], 1)

        @block.vector
        def _(dve):
            dve.wait_ge(S["zeroed"], 1)
            dve.wait_ge(S["raw_loaded"], 16 * n)
            for k, t in enumerate(tiles):
                if k >= 2:
                    dve.wait_ge(S["mixed"], k - 1)
                nc.vector.tensor_tensor(diff[:, k % 2], raw[:, k, 0:T], raw[:, k, 1:], ALU.subtract).then_inc(S["diffed"], 1)
                dve.wait_ge(S["diffed"], k + 1)
                nc.vector.scalar_tensor_tensor(mix[:, k], diff[:, k % 2], params[:, mu + t:mu + t + 1], raw[:, k, 1:],
                                               ALU.mult, ALU.add).then_inc(S["mixed"], 1)

        @block.tensor
        def _(pe):
            pe.wait_ge(S["v1_loaded"], 16)
            for k in range(KT):
                pe.wait_ge(S["mixed"], 4 + k)
                last = nc.tensor.matmul(vlow[32:64, :], v1s[:, k, :], mix[:, 3 + k], start=k == 0, stop=k == KT - 1)
            last.then_inc(S["vlow_done"], 1)
    end_phase(nc, S)


def rwkv_pair_phase(nc, bufs, l, hp, lora, dram, mixed_hi, mixed_lo):
    consts = bufs["consts"]
    projected, v_mixed, pair_pack = dram["projected"], dram["v_mixed"], dram["pair_pack"]
    low_wa, low_g, low_gv = lora
    con = lambda name, n: consts[:, CONSTS[name]:CONSTS[name] + n]
    ident, head_ones, head_mean = con("ident", P), con("head_ones", P), con("head_mean", P)
    S = phase_sems(nc, "rwkv_pair", "zeroed r_loaded k_loaded v_loaded v_first_loaded pack_loaded r_diff r_mix k_diff k_mix "
                       "gates_psum sigmoid_w a_ready sigmoid_v g_ready v_diff v_scaled v_ready log_decay decay_sum "
                       "decay_before exp_in exp_out exp_before kk_scaled kk_squared kk_norm kk_root kk_inverse kk_ready "
                       "a_less_one k_ready b_ready ar_ready bk_ready bk_end rk bonus_sum bonus_ready scores_psum "
                       "scores_masked n_psum q_psum q_masked tri_ready trit_ready bkt_psum bkt_copied vt_psum vt_copied "
                       "at_psum at_copied left_psum left_copied joined_psum tri_joined trit_joined w1_psum w1_copied "
                       "ta_psum ta_copied state_zero u_psum u_copied state_psum state_ready y_psum y_copied y_mean "
                       "y_centered y_squared y_variance y_root y_inverse y_scaled y_bonus y_gated high_done low_done")
    sb = lambda name, shape, dt=F32: nc.sbuf_tensor("r_" + name, shape, dt)
    with ExitStack() as mem:
        raw = mem.enter_context(sb("raw", [P, 2, T + 1]))
        vin = mem.enter_context(sb("vin", [P, 2, T]))
        pack = mem.enter_context(sb("pack", [P, PACK_COLS]))
        diff = mem.enter_context(sb("diff", [P, 2, T]))
        r = mem.enter_context(sb("r", [P, T]))
        kx = mem.enter_context(sb("kx", [P, T]))
        sw = mem.enter_context(sb("sw", [P, T]))
        a = mem.enter_context(sb("a", [P, T]))
        sv = mem.enter_context(sb("sv", [P, T]))
        g = mem.enter_context(sb("g", [P, T]))
        vd = mem.enter_context(sb("vd", [P, 2, T]))
        v = mem.enter_context(sb("v", [P, T]))
        ld = mem.enter_context(sb("ld", [P, T]))
        cs = mem.enter_context(sb("cs", [P, T]))
        lp = mem.enter_context(sb("lp", [P, T]))
        ein = mem.enter_context(sb("ein", [P, T]))
        eout = mem.enter_context(sb("eout", [P, T]))
        ebef = mem.enter_context(sb("ebef", [P, T]))
        kk0 = mem.enter_context(sb("kk0", [P, T]))
        kksq = mem.enter_context(sb("kksq", [P, T]))
        rn = mem.enter_context(sb("rn", [P, T]))
        kk = mem.enter_context(sb("kk", [P, T]))
        am = mem.enter_context(sb("am", [P, T]))
        k = mem.enter_context(sb("k", [P, T]))
        b = mem.enter_context(sb("b", [P, T]))
        ar = mem.enter_context(sb("ar", [P, NC, 2, CH]))
        bk = mem.enter_context(sb("bk", [P, NC, 2, CH]))
        bke = mem.enter_context(sb("bke", [P, NC, 2, CH]))
        rk = mem.enter_context(sb("rk", [P, T]))
        bonus = mem.enter_context(sb("bonus", [P, T]))
        scm = mem.enter_context(sb("scm", [P, 2, NC, P]))
        qs = mem.enter_context(sb("qs", [P, 6, NC, CH]))
        tri = mem.enter_context(sb("tri", [P, NC, CH]))
        trit = mem.enter_context(sb("trit", [P, NC, CH]))
        left = mem.enter_context(sb("left", [P, NC, CH]))
        bkt = mem.enter_context(sb("bkt", [P, NC, P]))
        uv = mem.enter_context(sb("uv", [P, NC, 2, CH]))
        at = mem.enter_context(sb("at", [P, NC, CH]))
        w1 = mem.enter_context(sb("w1", [P, NC, CH]))
        ta = mem.enter_context(sb("ta", [P, NC, CH]))
        state = mem.enter_context(sb("state", [P, NC + 1, CH]))
        ps = mem.enter_context(nc.psum_tensor("r_psum", [P, 8, T], F32))
        block = mem.enter_context(nc.Block())
        y, yc, ysq, yin, yn, y2, y3 = sw, kk0, kksq, rn, am, rk, lp
        half = lambda t, h: t[64 * h:64 * h + 64]
        p1 = lambda c: pack[:, c:c + 1]
        chunks = lambda x: x.rearrange("p (c t) -> p c t", c=NC)

        @block.sync
        def _(sp):
            sp.dma_start(raw[:, 1, 1:], projected[K0 + hp]).then_inc(S["k_loaded"], 16)
            sp.dma_start(raw[:, 0, 1:], projected[R0 + hp]).then_inc(S["r_loaded"], 16)
            sp.dma_start(vin[:, 0], v_mixed[l * KT + hp]).then_inc(S["v_loaded"], 16)

        @block.scalar
        def _(act):
            act.dma_start(pack[:], pair_pack[l * RWKV_TILES + hp]).then_inc(S["pack_loaded"], 16)
            act.dma_start(vin[:, 1], v_mixed[hp]).then_inc(S["v_first_loaded"], 16)
            act.wait_ge(S["pack_loaded"], 16)
            act.wait_ge(S["gates_psum"], 1)
            nc.scalar.activation(sw[:], ps[:, 0], ACT.Sigmoid, bias=p1(W0)).then_inc(S["sigmoid_w"], 1)
            act.wait_ge(S["gates_psum"], 2)
            nc.scalar.activation(a[:], ps[:, 1], ACT.Sigmoid, bias=p1(A0)).then_inc(S["a_ready"], 1)
            act.wait_ge(S["gates_psum"], 4)
            nc.scalar.activation(sv[:], ps[:, 3], ACT.Sigmoid, bias=p1(V0P)).then_inc(S["sigmoid_v"], 1)
            nc.scalar.activation(g[:], ps[:, 2], ACT.Copy).then_inc(S["g_ready"], 1)
            act.wait_ge(S["kk_scaled"], 1)
            nc.scalar.activation(kksq[:], kk0[:], ACT.Square).then_inc(S["kk_squared"], 1)
            act.wait_ge(S["kk_norm"], 1)
            nc.scalar.activation(rn[:], ps[:, 4], ACT.Sqrt, bias=con("eps", 3)[:, 2:3]).then_inc(S["kk_root"], 1)
            act.wait_ge(S["decay_sum"], 1)
            nc.scalar.activation(ein[:], cs[:], ACT.Exp).then_inc(S["exp_in"], 1)
            nc.scalar.activation(eout[:], cs[:], ACT.Exp, scale=-1.0).then_inc(S["exp_out"], 1)
            act.wait_ge(S["decay_before"], 1)
            nc.scalar.activation(ebef[:], lp[:], ACT.Exp).then_inc(S["exp_before"], 1)
            act.wait_ge(S["bkt_psum"], 1)
            nc.scalar.activation(bkt[:].rearrange("p c n -> p (c n)"), ps[:, 0:2].rearrange("p b n -> p (b n)"), ACT.Copy).then_inc(S["bkt_copied"], 1)
            act.wait_ge(S["vt_psum"], 1)
            nc.scalar.activation(uv[64:128].rearrange("p c h n -> p (c h n)"), ps[64:128, 2:4].rearrange("p b n -> p (b n)"), ACT.Copy).then_inc(S["vt_copied"], 1)
            act.wait_ge(S["at_psum"], 1)
            nc.scalar.activation(at[:].rearrange("p c n -> p (c n)"), ps[:, 4], ACT.Copy).then_inc(S["at_copied"], 1)
            for s in range(1, 6):
                act.wait_ge(S["left_psum"], s)
                nc.scalar.activation(left[:].rearrange("p c n -> p (c n)"), ps[:, 5], ACT.Copy).then_inc(S["left_copied"], 1)
            act.wait_ge(S["w1_psum"], 1)
            nc.scalar.activation(w1[:].rearrange("p c n -> p (c n)"), ps[:, 5], ACT.Copy).then_inc(S["w1_copied"], 1)
            act.wait_ge(S["ta_psum"], 1)
            nc.scalar.activation(ta[:].rearrange("p c n -> p (c n)"), ps[:, 6], ACT.Copy).then_inc(S["ta_copied"], 1)
            act.wait_ge(S["y_psum"], 1)
            nc.scalar.activation(y[:], ps[:, 3], ACT.Copy).then_inc(S["y_copied"], 1)
            act.wait_ge(S["y_centered"], 1)
            nc.scalar.activation(ysq[:], yc[:], ACT.Square).then_inc(S["y_squared"], 1)
            act.wait_ge(S["y_variance"], 1)
            nc.scalar.activation(yin[:], ps[:, 5], ACT.Sqrt, bias=con("eps", 3)[:, 1:2]).then_inc(S["y_root"], 1)
            act.wait_ge(S["y_gated"], 1)
            nc.scalar.activation(mixed_hi[:, ds(hp, 1)].rearrange("p a t -> p (a t)"), y3[:], ACT.Copy).then_inc(S["high_done"], 1)

        @block.gpsimd
        def _(pool):
            nc.gpsimd.memset(raw[:, :, 0:1], 0.0).then_inc(S["zeroed"], 1)
            nc.gpsimd.memset(state[:, 0], 0.0).then_inc(S["state_zero"], 1)

        @block.vector
        def _(dve):
            V = nc.vector
            dve.wait_ge(S["pack_loaded"], 16)
            dve.wait_ge(S["zeroed"], 1)
            dve.wait_ge(S["k_loaded"], 16)
            V.tensor_tensor(diff[:, 1], raw[:, 1, 0:T], raw[:, 1, 1:], ALU.subtract).then_inc(S["k_diff"], 1)
            dve.wait_ge(S["k_diff"], 1)
            V.scalar_tensor_tensor(kx[:], diff[:, 1], p1(MU_K), raw[:, 1, 1:], ALU.mult, ALU.add).then_inc(S["k_mix"], 1)
            dve.wait_ge(S["k_mix"], 1)
            V.tensor_scalar(kk0[:], kx[:], p1(K_K), None, ALU.mult).then_inc(S["kk_scaled"], 1)
            dve.wait_ge(S["sigmoid_w"], 1)
            V.tensor_scalar(ld[:], sw[:], -DECAY_SCALE, None, ALU.mult).then_inc(S["log_decay"], 1)
            dve.wait_ge(S["log_decay"], 1)
            V.tensor_tensor_scan(cs[:], con("chunk_start", T), ld[:], 0.0, ALU.mult, ALU.add).then_inc(S["decay_sum"], 1)
            dve.wait_ge(S["decay_sum"], 1)
            V.tensor_tensor(lp[:], cs[:], ld[:], ALU.subtract).then_inc(S["decay_before"], 1)
            dve.wait_ge(S["r_loaded"], 16)
            V.tensor_tensor(diff[:, 0], raw[:, 0, 0:T], raw[:, 0, 1:], ALU.subtract).then_inc(S["r_diff"], 1)
            dve.wait_ge(S["r_diff"], 1)
            V.scalar_tensor_tensor(r[:], diff[:, 0], p1(MU_R), raw[:, 0, 1:], ALU.mult, ALU.add).then_inc(S["r_mix"], 1)
            dve.wait_ge(S["kk_root"], 1)
            V.reciprocal(rn[:], rn[:]).then_inc(S["kk_inverse"], 1)
            dve.wait_ge(S["kk_inverse"], 1)
            V.tensor_tensor(kk[:], kk0[:], rn[:], ALU.mult).then_inc(S["kk_ready"], 1)
            dve.wait_ge(S["a_ready"], 1)
            V.tensor_scalar(am[:], a[:], -1.0, p1(K_A), ALU.add, ALU.mult).then_inc(S["a_less_one"], 1)
            dve.wait_ge(S["a_less_one"], 1)
            V.scalar_tensor_tensor(k[:], am[:], 1.0, kx[:], ALU.add, ALU.mult).then_inc(S["k_ready"], 1)
            dve.wait_ge(S["kk_ready"], 1)
            V.tensor_tensor(b[:], kk[:], a[:], ALU.mult).then_inc(S["b_ready"], 1)
            dve.wait_ge(S["exp_before"], 1)
            V.scalar_tensor_tensor(ar[:, :, 0], chunks(kk[:]), -1.0, chunks(ebef[:]), ALU.mult, ALU.mult).then_inc(S["ar_ready"], 1)
            dve.wait_ge(S["r_mix"], 1)
            dve.wait_ge(S["exp_in"], 1)
            V.tensor_tensor(ar[:, :, 1], chunks(r[:]), chunks(ein[:]), ALU.mult).then_inc(S["ar_ready"], 1)
            dve.wait_ge(S["b_ready"], 1)
            dve.wait_ge(S["exp_out"], 1)
            V.tensor_tensor(bk[:, :, 0], chunks(b[:]), chunks(eout[:]), ALU.mult).then_inc(S["bk_ready"], 1)
            dve.wait_ge(S["k_ready"], 1)
            V.tensor_tensor(bk[:, :, 1], chunks(k[:]), chunks(eout[:]), ALU.mult).then_inc(S["bk_ready"], 1)
            dve.wait_ge(S["v_loaded"], 16)
            dve.wait_ge(S["v_first_loaded"], 16)
            V.tensor_tensor(vd[:, 0], vin[:, 1], vin[:, 0], ALU.subtract).then_inc(S["v_diff"], 1)
            dve.wait_ge(S["sigmoid_v"], 1)
            dve.wait_ge(S["v_diff"], 1)
            V.tensor_tensor(vd[:, 1], vd[:, 0], sv[:], ALU.mult).then_inc(S["v_scaled"], 1)
            dve.wait_ge(S["v_scaled"], 1)
            V.tensor_tensor(v[:], vd[:, 1], vin[:, 0], ALU.add).then_inc(S["v_ready"], 1)
            level = lambda n, w=CH: consts[:, n:n + w].unsqueeze(1).broadcast_to([P, NC, w])
            dve.wait_ge(S["n_psum"], 1)
            V.tensor_tensor(tri[:], ps[:, 6].rearrange("p (c t) -> p c t", c=NC), level(CONSTS["level0_n"]), ALU.mult).then_inc(S["tri_ready"], 1)
            dve.wait_ge(S["tri_ready"], 1)
            V.tensor_tensor(tri[:], tri[:], level(CONSTS["eye64"]), ALU.add).then_inc(S["tri_ready"], 1)
            dve.wait_ge(S["q_psum"], 1)
            for s in range(6):
                V.tensor_tensor(qs[:, s], ps[:, 7].rearrange("p (c t) -> p c t", c=NC), level(CONSTS["levels_q"] + CH * s), ALU.mult).then_inc(S["q_masked"], 1)
            dve.wait_ge(S["q_masked"], 1)
            V.tensor_tensor(trit[:], qs[:, 0], level(CONSTS["eye64"]), ALU.add).then_inc(S["trit_ready"], 1)
            dve.wait_ge(S["bk_ready"], 2)
            end = chunks(ein[:])[:, :, CH - 1:CH].unsqueeze(2).broadcast_to([P, NC, 2, CH])
            V.tensor_tensor(bke[:], bk[:], end, ALU.mult).then_inc(S["bk_end"], 1)
            V.scalar_tensor_tensor(rk[:], r[:], p1(R_K), k[:], ALU.mult, ALU.mult).then_inc(S["rk"], 1)
            for n in range(4):
                dve.wait_ge(S["scores_psum"], n + 1)
                mask = con("scores", P).unsqueeze(1).broadcast_to([P, 4, P])
                V.tensor_tensor(scm[:, n // 2, 4 * (n % 2):4 * (n % 2) + 4], ps[:, n].rearrange("p (x q) -> p x q", x=4),
                                mask, ALU.mult).then_inc(S["scores_masked"], 1)
            dve.wait_ge(S["v_ready"], 1)
            dve.wait_ge(S["bonus_sum"], 1)
            V.tensor_tensor(bonus[:], ps[:, 5], v[:], ALU.mult).then_inc(S["bonus_ready"], 1)
            for s in range(1, 6):
                dve.wait_ge(S["joined_psum"], s)
                dve.wait_ge(S["trit_ready"], s)
                V.tensor_tensor(trit[:], trit[:], ps[:, 7].rearrange("p (c t) -> p c t", c=NC), ALU.add).then_inc(S["trit_ready"], 1)
                if s < 5:
                    dve.wait_ge(S["tri_ready"], s + 1)
                    V.tensor_tensor(tri[:], tri[:], ps[:, 6].rearrange("p (c t) -> p c t", c=NC), ALU.add).then_inc(S["tri_ready"], 1)
            dve.wait_ge(S["state_zero"], 1)
            for c in range(NC):
                dve.wait_ge(S["u_psum"], c + 1)
                V.tensor_copy(uv[0:64, c], ps[0:64, 0:2, 0:CH]).then_inc(S["u_copied"], 1)
                dve.wait_ge(S["state_psum"], c + 1)
                if c:
                    dve.wait_ge(S["state_ready"], c)
                if c < NC - 1:
                    V.scalar_tensor_tensor(state[:, c + 1], state[:, c], ein[:, c * CH + CH - 1:c * CH + CH], ps[:, 2, 0:CH],
                                           ALU.mult, ALU.add).then_inc(S["state_ready"], 1)
            dve.wait_ge(S["y_mean"], 1)
            dve.wait_ge(S["y_copied"], 1)
            V.tensor_tensor(yc[:], y[:], ps[:, 4], ALU.subtract).then_inc(S["y_centered"], 1)
            dve.wait_ge(S["y_root"], 1)
            V.reciprocal(yin[:], yin[:]).then_inc(S["y_inverse"], 1)
            dve.wait_ge(S["y_inverse"], 1)
            dve.wait_ge(S["y_centered"], 1)
            V.scalar_tensor_tensor(yn[:], yc[:], p1(LN_W), yin[:], ALU.mult, ALU.mult).then_inc(S["y_scaled"], 1)
            dve.wait_ge(S["y_scaled"], 1)
            dve.wait_ge(S["bonus_ready"], 1)
            V.scalar_tensor_tensor(y2[:], yn[:], p1(LN_B), bonus[:], ALU.add, ALU.add).then_inc(S["y_bonus"], 1)
            dve.wait_ge(S["y_bonus"], 1)
            dve.wait_ge(S["g_ready"], 1)
            V.tensor_tensor(y3[:], y2[:], g[:], ALU.mult).then_inc(S["y_gated"], 1)
            dve.wait_ge(S["high_done"], 1)
            V.tensor_tensor(mixed_lo[:, ds(hp, 1)].rearrange("p a t -> p (a t)"), y3[:],
                            mixed_hi[:, ds(hp, 1)].rearrange("p a t -> p (a t)"), ALU.subtract).then_inc(S["low_done"], 1)

        @block.tensor
        def _(pe):
            mm = nc.tensor.matmul
            pe.wait_ge(S["pack_loaded"], 16)
            mm(ps[:, 0], pack[0:64, 0:P], low_wa[0:64, :], start=True, stop=True).then_inc(S["gates_psum"], 1)
            mm(ps[:, 1], pack[64:128, 0:P], low_wa[64:128, :], start=True, stop=True).then_inc(S["gates_psum"], 1)
            mm(ps[:, 3], pack[32:64, 2 * P:3 * P], low_gv[32:64, :], start=True, stop=True).then_inc(S["gates_psum"], 1)
            mm(ps[:, 2], pack[:, P:2 * P], low_g[:], start=True, stop=False)
            mm(ps[:, 2], pack[0:32, 2 * P:3 * P], low_gv[0:32, :], start=False, stop=True).then_inc(S["gates_psum"], 1)
            pe.wait_ge(S["kk_squared"], 1)
            mm(ps[:, 4], head_ones, kksq[:], start=True, stop=True).then_inc(S["kk_norm"], 1)
            pe.wait_ge(S["ar_ready"], 2)
            pe.wait_ge(S["bk_ready"], 1)
            for c in range(NC):
                for h in range(2):
                    last = mm(half(ps, h)[:, 6, c * CH:(c + 1) * CH], half(ar, h)[:, c, 0], half(bk, h)[:, c, 0], start=True, stop=True)
            last.then_inc(S["n_psum"], 1)
            for c in range(NC):
                for h in range(2):
                    last = mm(half(ps, h)[:, 7, c * CH:(c + 1) * CH], half(bk, h)[:, c, 0], half(ar, h)[:, c, 0], start=True, stop=True)
            last.then_inc(S["q_psum"], 1)
            pe.wait_ge(S["bk_ready"], 2)
            pe.wait_ge(S["sigmoid_w"], 1)
            pe.wait_ge(S["g_ready"], 1)
            for n in range(4):
                for x in range(4):
                    c, h = 4 * (n % 2) + x, n // 2
                    last = mm(ps[:, n, x * P:(x + 1) * P], half(bk, h)[:, c].rearrange("p a t -> p (a t)"),
                              half(ar, h)[:, c].rearrange("p a t -> p (a t)"), start=True, stop=True)
                last.then_inc(S["scores_psum"], 1)
            pe.wait_ge(S["rk"], 1)
            mm(ps[:, 5], head_ones, rk[:], start=True, stop=True).then_inc(S["bonus_sum"], 1)
            pe.wait_ge(S["kk_inverse"], 1)
            for c in range(NC):
                for h in range(2):
                    last = mm(half(ps, h)[:, 4, c * CH:(c + 1) * CH], half(ar, h)[:, c, 0], half(ident, h)[:, 64 * h:64 * h + 64], start=True, stop=True)
            last.then_inc(S["at_psum"], 1)
            pe.wait_ge(S["scores_masked"], 4)
            pe.wait_ge(S["bk_end"], 1)
            for c in range(NC):
                for x in range(2):
                    last = mm(ps[64 * x:64 * x + 64, c // 4, (c % 4) * P:(c % 4 + 1) * P], bke[:, c, x], ident, start=True, stop=True)
            last.then_inc(S["bkt_psum"], 1)
            pe.wait_ge(S["v_ready"], 1)
            for c in range(NC):
                last = mm(ps[64:128, 2 + c // 4, (c % 4) * P:(c % 4 + 1) * P], v[:, c * CH:(c + 1) * CH], ident, start=True, stop=True)
            last.then_inc(S["vt_psum"], 1)
            pe.wait_ge(S["q_masked"], 6)
            pe.wait_ge(S["bonus_ready"], 1)
            for s in range(1, 6):
                pe.wait_ge(S["tri_ready"], s + 1)
                for c in range(NC):
                    for h in range(2):
                        last = mm(half(ps, h)[:, 5, c * CH:(c + 1) * CH], half(qs, h)[:, s, c], half(tri, h)[:, c], start=True, stop=True)
                last.then_inc(S["left_psum"], 1)
                pe.wait_ge(S["left_copied"], s)
                pe.wait_ge(S["trit_ready"], s)
                for c in range(NC):
                    for h in range(2):
                        if s < 5:
                            mm(half(ps, h)[:, 6, c * CH:(c + 1) * CH], half(trit, h)[:, c], half(left, h)[:, c], start=True, stop=True)
                        last = mm(half(ps, h)[:, 7, c * CH:(c + 1) * CH], half(left, h)[:, c], half(trit, h)[:, c], start=True, stop=True)
                last.then_inc(S["joined_psum"], 1)
            pe.wait_ge(S["vt_copied"], 1)
            for c in range(NC):
                for h in range(2):
                    last = mm(half(ps, h)[:, 5, c * CH:(c + 1) * CH], scm[64:128, h, c, 0:CH], uv[64:128, c, h], start=True, stop=True)
            last.then_inc(S["w1_psum"], 1)
            pe.wait_ge(S["trit_ready"], 6)
            pe.wait_ge(S["at_copied"], 1)
            for c in range(NC):
                for h in range(2):
                    last = mm(half(ps, h)[:, 6, c * CH:(c + 1) * CH], half(at, h)[:, c], half(trit, h)[:, c], start=True, stop=True)
            last.then_inc(S["ta_psum"], 1)
            pe.wait_ge(S["w1_copied"], 1)
            pe.wait_ge(S["ta_copied"], 1)
            pe.wait_ge(S["bkt_copied"], 1)
            pe.wait_ge(S["state_zero"], 1)
            for c in range(NC):
                if c:
                    pe.wait_ge(S["u_copied"], c)
                for h in range(2):
                    mm(ps[0:64, h, 0:CH], half(trit, h)[:, c], half(w1, h)[:, c], start=True, stop=False)
                if c:
                    pe.wait_ge(S["state_ready"], c)
                for h in range(2):
                    last = mm(ps[0:64, h, 0:CH], half(ta, h)[:, c], half(state, h)[:, c], start=False, stop=True)
                last.then_inc(S["u_psum"], 1)
                pe.wait_ge(S["u_copied"], c + 1)
                for h in range(2):
                    last = mm(half(ps, h)[:, 2, 0:CH], bkt[:, c, 64 * h:64 * h + 64], uv[:, c, h], start=True, stop=True)
                last.then_inc(S["state_psum"], 1)
            for c in range(NC):
                for h in range(2):
                    mm(half(ps, h)[:, 3, c * CH:(c + 1) * CH], uv[:, c, h], scm[:, h, c, CH:P], start=True, stop=False)
                    last = mm(half(ps, h)[:, 3, c * CH:(c + 1) * CH], half(state, h)[:, c], half(ar, h)[:, c, 1], start=False, stop=True)
            last.then_inc(S["y_psum"], 1)
            pe.wait_ge(S["y_copied"], 1)
            mm(ps[:, 4], head_mean, y[:], start=True, stop=True).then_inc(S["y_mean"], 1)
            pe.wait_ge(S["y_squared"], 1)
            mm(ps[:, 5], head_mean, ysq[:], start=True, stop=True).then_inc(S["y_variance"], 1)
    end_phase(nc, S)


T_DT, T_NEG, T_EXP, T_END_DT, T_END = range(5)
G_CONV, G_BIAS, G_GAIN, G_D = 0, 24, 30, 34
GROUP_COLS = 38


def dt_phase(nc, bufs, l, dram, acs, table):
    consts, params = bufs["consts"], bufs["params"]
    projected = dram["projected"]
    S = phase_sems(nc, "dt", "loaded biased negative exponent one_plus less_one is_zero log_ready log_masked den_masked "
                       "inverse ratio log1p dt_ready rate_ready decay acs_ready diagonal transposed tables_ready "
                       "end_diff end_exp")
    R = slice(32, 64)
    with nc.sbuf_tensor("d_t", [P, 14, T], F32) as t, nc.sbuf_tensor("d_diag", [P, SNC, 32], F32) as diag, \
            nc.sbuf_tensor("d_rate", [P, 1], F32) as rate, nc.sbuf_tensor("d_end", [P, SNC, 32], F32) as end_diff, \
            nc.psum_tensor("d_ps", [P, 3, SNC, 32], F32) as ps, nc.Block() as block:
        raw, x, neg, e, u, less, zero, logu, num, den, inv, ratio, lp, dt = (t[R, n] for n in range(14))
        bias = params[R, PARAMS["dt_bias"]:PARAMS["dt_bias"] + 1]
        a_log = params[R, PARAMS["A_log"]:PARAMS["A_log"] + 1]
        ident = consts[:, CONSTS["ident"]:CONSTS["ident"] + P]
        heads = lambda n: table[:, :, n].rearrange("p g c h -> p c g h")
        psum = lambda n: ps[:, n].rearrange("p c (g h) -> p c g h", g=SSD_GROUPS)

        @block.sync
        def _(sp):
            sp.dma_start(raw, projected[GDT, 32:64]).then_inc(S["loaded"], 16)

        @block.scalar
        def _(act):
            nc.scalar.activation(rate[R], a_log, ACT.Exp).then_inc(S["rate_ready"], 1)
            act.wait_ge(S["negative"], 1)
            nc.scalar.activation(e, neg, ACT.Exp).then_inc(S["exponent"], 1)
            act.wait_ge(S["one_plus"], 1)
            nc.scalar.activation(logu, u, ACT.Ln).then_inc(S["log_ready"], 1)
            act.wait_ge(S["transposed"], 1)
            nc.scalar.activation(heads(T_DT), psum(0), ACT.Copy).then_inc(S["tables_ready"], 1)
            nc.scalar.activation(heads(T_NEG), psum(1), ACT.Copy, scale=-1.0).then_inc(S["tables_ready"], 1)
            nc.scalar.activation(heads(T_EXP), psum(1), ACT.Exp).then_inc(S["tables_ready"], 1)
            nc.scalar.activation(heads(T_END), psum(2), ACT.Exp).then_inc(S["tables_ready"], 1)
            act.wait_ge(S["end_diff"], 1)
            nc.scalar.activation(end_diff[:], end_diff[:], ACT.Exp).then_inc(S["end_exp"], 1)

        @block.vector
        def _(dve):
            V = nc.vector
            dve.wait_ge(S["loaded"], 16)
            V.tensor_scalar(x, raw, bias, None, ALU.add).then_inc(S["biased"], 1)
            dve.wait_ge(S["biased"], 1)
            V.scalar_tensor_tensor(neg, x, -1.0, x, ALU.mult, ALU.min).then_inc(S["negative"], 1)
            dve.wait_ge(S["exponent"], 1)
            V.tensor_scalar(u, e, 1.0, None, ALU.add).then_inc(S["one_plus"], 1)
            dve.wait_ge(S["one_plus"], 1)
            V.tensor_scalar(less, u, -1.0, None, ALU.add).then_inc(S["less_one"], 1)
            dve.wait_ge(S["less_one"], 1)
            V.tensor_scalar(zero, less, 0.0, None, ALU.is_equal).then_inc(S["is_zero"], 1)
            dve.wait_ge(S["is_zero"], 1)
            V.tensor_tensor(den, less, zero, ALU.add).then_inc(S["den_masked"], 1)
            dve.wait_ge(S["den_masked"], 1)
            V.reciprocal(inv, den).then_inc(S["inverse"], 1)
            dve.wait_ge(S["log_ready"], 1)
            V.tensor_tensor(num, logu, zero, ALU.add).then_inc(S["log_masked"], 1)
            dve.wait_ge(S["log_masked"], 1)
            dve.wait_ge(S["inverse"], 1)
            V.tensor_tensor(ratio, num, inv, ALU.mult).then_inc(S["ratio"], 1)
            dve.wait_ge(S["ratio"], 1)
            V.tensor_tensor(lp, ratio, e, ALU.mult).then_inc(S["log1p"], 1)
            dve.wait_ge(S["log1p"], 1)
            V.scalar_tensor_tensor(dt, x, 0.0, lp, ALU.max, ALU.add).then_inc(S["dt_ready"], 1)
            dve.wait_ge(S["dt_ready"], 1)
            dve.wait_ge(S["rate_ready"], 1)
            V.tensor_scalar(raw, dt, rate[R], -1.0, ALU.mult, ALU.mult).then_inc(S["decay"], 1)
            dve.wait_ge(S["decay"], 1)
            V.tensor_tensor_scan(acs[R], consts[R, CONSTS["ssd_start"]:CONSTS["ssd_start"] + T], raw, 0.0, ALU.mult, ALU.add).then_inc(S["acs_ready"], 1)
            dve.wait_ge(S["acs_ready"], 1)
            for c in range(SNC):
                V.tensor_scalar(diag[R, c], ident[R, 32:64], acs[R, (c + 1) * SCH - 1:(c + 1) * SCH], float(D), ALU.mult, ALU.mult).then_inc(S["diagonal"], 1)
            dve.wait_ge(S["transposed"], 1)
            dve.wait_ge(S["tables_ready"], 4)
            V.tensor_tensor(end_diff[:].rearrange("p c (g h) -> p c g h", g=SSD_GROUPS), psum(2), heads(T_NEG), ALU.add).then_inc(S["end_diff"], 1)
            dve.wait_ge(S["end_exp"], 1)
            V.tensor_tensor(heads(T_END_DT), end_diff[:].rearrange("p c (g h) -> p c g h", g=SSD_GROUPS), heads(T_DT), ALU.mult).then_inc(S["tables_ready"], 1)

        @block.tensor
        def _(pe):
            mean = consts[:, CONSTS["mean"]:CONSTS["mean"] + P]
            pe.wait_ge(S["diagonal"], SNC)
            for c in range(SNC):
                cut = slice(c * SCH, (c + 1) * SCH)
                nc.tensor.matmul(ps[:, 0, c], dt[:, cut], ident[R, 32:64], start=True, stop=True)
                nc.tensor.matmul(ps[:, 1, c], acs[R, cut], ident[R, 32:64], start=True, stop=True)
                last = nc.tensor.matmul(ps[:, 2, c], mean[R, :], diag[R, c], start=True, stop=True)
            last.then_inc(S["transposed"], 1)
    end_phase(nc, S)


def ssd_group_phase(nc, bufs, l, g, dram, acs, table, mixed_hi, mixed_lo):
    consts = bufs["consts"]
    projected = dram["projected"]
    con = lambda name, n: consts[:, CONSTS[name]:CONSTS[name] + n]
    ident, mean, mask = con("ident", P), con("mean", P), con("ssd_mask", P)
    GH, W = GROUP_HEADS, GROUP_HEADS * 64
    S = phase_sems(nc, "ssd_group", "zeroed state_zero pack_loaded raw_loaded z_loaded select_loaded tab_ready tapped conv_done "
                       "silu_ready z_ready cb_psum cb_ready xt_psum xt_read bt_psum bt_ready seg_psum seg_exp scored "
                       "diag_psum off_psum off_scaled y_ready state_psum state_decayed state_ready back_psum "
                       "skipped gated squared norm_psum root_ready rstd_ready normed high_done low_done")
    sb = lambda name, shape, dt=F32: nc.sbuf_tensor("s_" + name, shape, dt)
    with ExitStack() as mem:
        raw = mem.enter_context(sb("raw", [P, 6, T + 3]))
        pack = mem.enter_context(sb("pack", [P, GROUP_COLS]))
        sel = mem.enter_context(sb("sel", [P, GH, P]))
        x = mem.enter_context(sb("x", [P, 6, T]))
        z = mem.enter_context(sb("z", [P, 4, T]))
        tab = mem.enter_context(sb("tab", [P, 5, SNC, GH]))
        cb = mem.enter_context(sb("cb", [P, SNC, SCH]))
        xdt = mem.enter_context(sb("xdt", [P, SNC, W]))
        xw = mem.enter_context(sb("xw", [P, SNC, W]))
        bt = mem.enter_context(sb("bt", [P, SNC, P]))
        e = mem.enter_context(sb("e", [P, 2, SNC, SCH]))
        m = mem.enter_context(sb("m", [P, 2, SNC, SCH]))
        state = mem.enter_context(sb("state", [P, SNC, W]))
        off = mem.enter_context(sb("off", [P, 2, W]))
        ytok = mem.enter_context(sb("ytok", [P, SNC, W]))
        y = mem.enter_context(sb("y", [P, 4, T]))
        sq = mem.enter_context(sb("sq", [P, 2, T]))
        rstd = mem.enter_context(sb("rstd", [P, 2, T]))
        ps = mem.enter_context(nc.psum_tensor("s_psum", [P, 8, T], F32))
        block = mem.enter_context(nc.Block())
        p1 = lambda c: pack[:, c:c + 1]
        per_head = lambda n, c: tab[:, n, c].unsqueeze(2).broadcast_to([P, GH, 64])
        by_head = lambda a: a.rearrange("p (h n) -> p h n", h=GH)
        tiles = lambda n: [X0 + 4 * g + n] if n < 4 else [B0 + g] if n == 4 else [C0 + g]

        @block.sync
        def _(sp):
            for n in (4, 5, 0, 1, 2, 3):
                sp.dma_start(raw[:, n, 3:], projected[tiles(n)[0]]).then_inc(S["raw_loaded"], 16)

        @block.scalar
        def _(act):
            act.dma_start(pack[:], dram["group_pack"][l * SSD_GROUPS + g]).then_inc(S["pack_loaded"], 16)
            act.dma_start(sel[32:64].rearrange("p h n -> p (h n)"), dram["select"][g]).then_inc(S["select_loaded"], 16)
            for n in range(4):
                act.dma_start(z[:, n], projected[Z0 + 4 * g + n]).then_inc(S["z_loaded"], 16)
            for i, n in enumerate((4, 5, 0, 1, 2, 3)):
                act.wait_ge(S["conv_done"], i + 1)
                nc.scalar.activation(x[:, n], x[:, n], ACT.Silu).then_inc(S["silu_ready"], 1)
            act.wait_ge(S["z_loaded"], 64)
            for n in range(4):
                nc.scalar.activation(z[:, n], z[:, n], ACT.Silu).then_inc(S["z_ready"], 1)
            act.wait_ge(S["cb_psum"], 1)
            nc.scalar.activation(cb[:].rearrange("p c n -> p (c n)"), ps[:, 6], ACT.Copy).then_inc(S["cb_ready"], 1)
            act.wait_ge(S["bt_psum"], 1)
            nc.scalar.activation(bt[:].rearrange("p c n -> p (c n)"), ps[:, 7], ACT.Copy).then_inc(S["bt_ready"], 1)
            act.wait_ge(S["tab_ready"], 1)
            for h in range(GH):
                act.wait_ge(S["seg_psum"], h + 1)
                if h >= 2:
                    act.wait_ge(S["scored"], h - 1)
                for c in range(SNC):
                    last = nc.scalar.activation(e[:, h % 2, c], ps[:, 4 + h % 2, c * SCH:(c + 1) * SCH], ACT.Exp,
                                                bias=tab[:, T_NEG, c, h:h + 1])
                last.then_inc(S["seg_exp"], 1)
            for n in range(4):
                act.wait_ge(S["gated"], n + 1)
                if n >= 2:
                    act.wait_ge(S["norm_psum"], n - 1)
                nc.scalar.activation(sq[:, n % 2], y[:, n], ACT.Square).then_inc(S["squared"], 1)
            act.wait_ge(S["norm_psum"], 4)
            nc.scalar.activation(rstd[:, 0], ps[:, 7], ACT.Sqrt, scale=float(D) / W, bias=con("eps", 3)[:, 0:1]).then_inc(S["root_ready"], 1)
            for n in range(4):
                act.wait_ge(S["normed"], n + 1)
                nc.scalar.activation(mixed_hi[:, ds(8 + 4 * g + n, 1)].rearrange("p a t -> p (a t)"), ytok[:, n], ACT.Copy).then_inc(S["high_done"], 1)

        @block.gpsimd
        def _(pool):
            nc.gpsimd.memset(raw[:, :, 0:3], 0.0).then_inc(S["zeroed"], 1)
            nc.gpsimd.memset(state[:, 0], 0.0).then_inc(S["state_zero"], 1)

        @block.vector
        def _(dve):
            V = nc.vector
            V.tensor_copy(tab[:].rearrange("p k c h -> p (k c h)"), table[:, ds(g, 1)].rearrange("p a k c h -> p (a k c h)")).then_inc(S["tab_ready"], 1)
            dve.wait_ge(S["zeroed"], 1)
            dve.wait_ge(S["pack_loaded"], 16)
            dve.wait_ge(S["raw_loaded"], 96)
            done = 0
            for n in (4, 5, 0, 1, 2, 3):
                V.tensor_scalar(x[:, n], raw[:, n, 0:T], p1(G_CONV + 4 * n), p1(G_BIAS + n), ALU.mult, ALU.add).then_inc(S["tapped"], 1)
                for j in range(1, 4):
                    done += 1
                    dve.wait_ge(S["tapped"], done)
                    V.scalar_tensor_tensor(x[:, n], raw[:, n, j:j + T], p1(G_CONV + 4 * n + j), x[:, n], ALU.mult, ALU.add).then_inc(
                        S["tapped"] if j < 3 else S["conv_done"], 1)
            dve.wait_ge(S["tab_ready"], 1)
            for c in range(SNC):
                dve.wait_ge(S["xt_psum"], c + 1)
                V.tensor_tensor(by_head(xdt[:, c]), by_head(ps[:, c]), per_head(T_DT, c), ALU.mult).then_inc(S["xt_read"], 1)
                V.tensor_tensor(by_head(xw[:, c]), by_head(ps[:, c]), per_head(T_END_DT, c), ALU.mult).then_inc(S["xt_read"], 1)
            dve.wait_ge(S["cb_ready"], 1)
            for h in range(GH):
                dve.wait_ge(S["seg_exp"], h + 1)
                if h >= 2:
                    dve.wait_ge(S["diag_psum"], h - 1)
                V.tensor_tensor(m[:, h % 2], e[:, h % 2], cb[:], ALU.mult).then_inc(S["scored"], 1)
            dve.wait_ge(S["state_zero"], 1)
            for c in range(SNC - 1):
                if c:
                    dve.wait_ge(S["state_ready"], c)
                V.tensor_tensor(by_head(off[:, 0]), by_head(state[:, c]), per_head(T_END, c), ALU.mult).then_inc(S["state_decayed"], 1)
                dve.wait_ge(S["state_decayed"], c + 1)
                dve.wait_ge(S["state_psum"], c + 1)
                V.tensor_tensor(state[:, c + 1], off[:, 0], ps[:, 6], ALU.add).then_inc(S["state_ready"], 1)
            dve.wait_ge(S["diag_psum"], GH)
            for c in range(SNC):
                dve.wait_ge(S["off_psum"], c + 1)
                V.tensor_tensor(by_head(off[:, c % 2]), by_head(ps[:, 4 + c % 2]), per_head(T_EXP, c), ALU.mult).then_inc(S["off_scaled"], 1)
                dve.wait_ge(S["off_scaled"], c + 1)
                V.tensor_tensor(ytok[:, c], off[:, c % 2], ps[:, c], ALU.add).then_inc(S["y_ready"], 1)
            dve.wait_ge(S["z_ready"], 4)
            for n in range(4):
                dve.wait_ge(S["back_psum"], n + 1)
                V.scalar_tensor_tensor(y[:, n], x[:, n], p1(G_D + n), ps[:, n], ALU.mult, ALU.add).then_inc(S["skipped"], 1)
                dve.wait_ge(S["skipped"], n + 1)
                V.tensor_tensor(y[:, n], y[:, n], z[:, n], ALU.mult).then_inc(S["gated"], 1)
            dve.wait_ge(S["root_ready"], 1)
            V.reciprocal(rstd[:, 1], rstd[:, 0]).then_inc(S["rstd_ready"], 1)
            dve.wait_ge(S["rstd_ready"], 1)
            for n in range(4):
                V.scalar_tensor_tensor(ytok[:, n], y[:, n], p1(G_GAIN + n), rstd[:, 1], ALU.mult, ALU.mult).then_inc(S["normed"], 1)
            for n in range(4):
                dve.wait_ge(S["high_done"], n + 1)
                V.tensor_tensor(mixed_lo[:, ds(8 + 4 * g + n, 1)].rearrange("p a t -> p (a t)"), ytok[:, n],
                                mixed_hi[:, ds(8 + 4 * g + n, 1)].rearrange("p a t -> p (a t)"), ALU.subtract).then_inc(S["low_done"], 1)

        @block.tensor
        def _(pe):
            mm = nc.tensor.matmul
            cut = lambda c: slice(c * SCH, (c + 1) * SCH)
            pe.wait_ge(S["silu_ready"], 2)
            for c in range(SNC):
                last = mm(ps[:, 6, cut(c)], x[:, 4, cut(c)], x[:, 5, cut(c)], start=True, stop=True)
            last.then_inc(S["cb_psum"], 1)
            for c in range(SNC):
                last = nc.tensor.transpose(ps[:, 7, cut(c)], x[:, 4, cut(c)], ident)
            last.then_inc(S["bt_psum"], 1)
            pe.wait_ge(S["silu_ready"], 6)
            for c in range(SNC):
                for n in range(4):
                    last = nc.tensor.transpose(ps[:, c, n * P:(n + 1) * P], x[:, n, cut(c)], ident)
                last.then_inc(S["xt_psum"], 1)
            pe.wait_ge(S["select_loaded"], 16)
            pe.wait_ge(S["xt_read"], 8)

            def segment(h):
                if h >= 2:
                    pe.wait_ge(S["seg_exp"], h - 1)
                mm(ps[:, 4 + h % 2], sel[32:64, h], acs[32:64, :], start=True, stop=False)
                mm(ps[:, 4 + h % 2], ident, mask.unsqueeze(1).broadcast_to([P, SNC, SCH]), start=False, stop=True).then_inc(S["seg_psum"], 1)

            segment(0)
            for h in range(GH):
                if h + 1 < GH:
                    segment(h + 1)
                pe.wait_ge(S["scored"], h + 1)
                for c in range(SNC):
                    last = mm(ps[:, c, h * 64:(h + 1) * 64], m[:, h % 2, c], xdt[:, c, h * 64:(h + 1) * 64], start=True, stop=True)
                last.then_inc(S["diag_psum"], 1)
            pe.wait_ge(S["cb_ready"], 1)
            pe.wait_ge(S["bt_ready"], 1)
            for c in range(SNC - 1):
                if c:
                    pe.wait_ge(S["state_ready"], c)
                mm(ps[:, 6], bt[:, c], xw[:, c], start=True, stop=True).then_inc(S["state_psum"], 1)
            pe.wait_ge(S["state_zero"], 1)
            pe.wait_ge(S["state_ready"], SNC - 1)
            pe.wait_ge(S["seg_exp"], GH)
            for c in range(SNC):
                if c >= 2:
                    pe.wait_ge(S["off_scaled"], c - 1)
                mm(ps[:, 4 + c % 2], x[:, 5, cut(c)], state[:, c], start=True, stop=True).then_inc(S["off_psum"], 1)
            pe.wait_ge(S["y_ready"], 4)
            for n in range(4):
                for c in range(SNC):
                    last = nc.tensor.transpose(ps[:, n, cut(c)], ytok[:, c, n * P:(n + 1) * P], ident)
                last.then_inc(S["back_psum"], 1)
            for n in range(4):
                pe.wait_ge(S["squared"], n + 1)
                mm(ps[:, 7], mean, sq[:, n % 2], start=n == 0, stop=n == 3).then_inc(S["norm_psum"], 1)
    end_phase(nc, S)


MIX = 3


def mix_phase(nc, bufs, l, dram, mixed_hi, mixed_lo, act_hi, act_lo):
    projected, weights = dram["projected"], dram["w_branches"]
    S = phase_sems(nc, "mix", "w_loaded*6 high_ready*6 low_ready*6 product_done*6 gates_loaded*2 gates_ready*2 "
                       "rwkv_gated*2 ssd_gated*2 summed*2 high_done*2 low_done*2")
    steps = KT // 2
    with nc.sbuf_tensor("m_w", [P, 6, KT, P], F32) as w, nc.sbuf_tensor("m_whi", [P, 6, KT, P], F16) as w_hi, \
            nc.sbuf_tensor("m_wlo", [P, 6, KT, P], F16) as w_lo, nc.sbuf_tensor("m_gate", [P, 2, 2, T], F32) as gate, \
            nc.sbuf_tensor("m_part", [P, 2, 2, T], F32) as part, nc.sbuf_tensor("m_sum", [P, 2, T], F32) as total, \
            nc.psum_tensor("m_acc", [P, 4, T], F32) as acc, nc.Block() as block:
        flat = lambda a: a.rearrange("p a t -> p (a t)")

        @block.sync
        def _(sp):
            def load(i, s):
                sp.dma_start(w[:, s].rearrange("p k n -> p (k n)"), weights[l * KT * MIX + i * 6 + s]).then_inc(S["w_loaded"][s], 16)

            for s in range(6):
                load(0, s)
            with sp.Fori(1, steps) as i:
                for s in range(6):
                    sp.wait_ge(S["low_ready"][s], i)
                    load(i, s)

        @block.scalar
        def _(act):
            def half_step(i, x, first):
                if not first:
                    act.wait_ge(S["rwkv_gated"][x], i)
                    act.wait_ge(S["ssd_gated"][x], i)
                act.dma_start(gate[:, x, 0], projected[GA + 2 * i + x]).then_inc(S["gates_loaded"][x], 16)
                act.dma_start(gate[:, x, 1], projected[GB + 2 * i + x]).then_inc(S["gates_loaded"][x], 16)
                for s in range(3 * x, 3 * x + 3):
                    act.wait_ge(S["w_loaded"][s], 16 * i + 16)
                    if not first:
                        act.wait_ge(S["product_done"][s], i)
                    nc.scalar.activation(w_hi[:, s], w[:, s], ACT.Copy, scale=W_SCALE).then_inc(S["high_ready"][s], 1)
                act.wait_ge(S["gates_loaded"][x], 32 * i + 32)
                nc.scalar.activation(gate[:, x].rearrange("p a t -> p (a t)"), gate[:, x].rearrange("p a t -> p (a t)"), ACT.Sigmoid).then_inc(S["gates_ready"][x], 1)

            def split(i, x):
                act.wait_ge(S["summed"][x], i + 1)
                nc.scalar.activation(flat(act_hi[:, ds(2 * i + x, 1)]), total[:, x], ACT.Copy).then_inc(S["high_done"][x], 1)

            half_step(0, 0, True)
            half_step(0, 1, True)
            with act.Fori(1, steps) as i:
                for x in range(2):
                    split(i - 1, x)
                    half_step(i, x, False)
            for x in range(2):
                split(steps - 1, x)

        @block.tensor
        def _(pe):
            def products(i, first):
                for s in range(6):
                    x, n = divmod(s, 3)
                    pe.wait_ge(S["low_ready"][s], i + 1)
                    if not first and n == 0:
                        pe.wait_ge(S["rwkv_gated"][x], i)
                    if not first and n == 1:
                        pe.wait_ge(S["ssd_gated"][x], i)
                    a = acc[:, 2 * x + (n > 0)]
                    for k in range(KT):
                        z = KT * n + k
                        nc.tensor.matmul(a, w_hi[:, s, k], mixed_hi[:, z], start=k == 0 and n < 2, stop=False)
                        nc.tensor.matmul(a, w_hi[:, s, k], mixed_lo[:, z], start=False, stop=False)
                        last = nc.tensor.matmul(a, w_lo[:, s, k], mixed_hi[:, z], start=False, stop=k == KT - 1 and n != 1)
                    last.then_inc(S["product_done"][s], 1)

            products(0, True)
            with pe.Fori(1, steps) as i:
                products(i, False)

        @block.vector
        def _(dve):
            def gated(i, x):
                dve.wait_ge(S["gates_ready"][x], i + 1)
                dve.wait_ge(S["product_done"][3 * x], i + 1)
                nc.vector.scalar_tensor_tensor(part[:, x, 0], acc[:, 2 * x], 1.0 / W_SCALE, gate[:, x, 0], ALU.mult, ALU.mult).then_inc(S["rwkv_gated"][x], 1)
                dve.wait_ge(S["product_done"][3 * x + 2], i + 1)
                nc.vector.scalar_tensor_tensor(part[:, x, 1], acc[:, 2 * x + 1], 1.0 / W_SCALE, gate[:, x, 1], ALU.mult, ALU.mult).then_inc(S["ssd_gated"][x], 1)
                dve.wait_ge(S["rwkv_gated"][x], i + 1)
                dve.wait_ge(S["ssd_gated"][x], i + 1)
                nc.vector.tensor_tensor(total[:, x], part[:, x, 0], part[:, x, 1], ALU.add).then_inc(S["summed"][x], 1)
                dve.wait_ge(S["high_done"][x], i + 1)
                nc.vector.tensor_tensor(flat(act_lo[:, ds(2 * i + x, 1)]), total[:, x], flat(act_hi[:, ds(2 * i + x, 1)]), ALU.subtract).then_inc(S["low_done"][x], 1)

            def split_rest(i, x):
                for s in range(3 * x, 3 * x + 3):
                    dve.wait_ge(S["high_ready"][s], i + 1)
                    nc.vector.scalar_tensor_tensor(w_lo[:, s], w[:, s], W_SCALE, w_hi[:, s], ALU.mult, ALU.subtract).then_inc(S["low_ready"][s], 1)

            for x in range(2):
                split_rest(0, x)
            with dve.Fori(1, steps) as i:
                for x in range(2):
                    gated(i - 1, x)
                    split_rest(i, x)
            for x in range(2):
                gated(steps - 1, x)
    end_phase(nc, S)


def residual_phase(nc, bufs, l, weights, act_hi, act_lo):
    hT = bufs["hT"]
    S = phase_sems(nc, "residual", "w_loaded*4 high_ready*4 low_ready*4 product_done*4 added*4")
    steps = KT // SLOTS
    with nc.sbuf_tensor("o_w", [P, SLOTS, KT, P], F32) as w, nc.sbuf_tensor("o_whi", [P, SLOTS, KT, P], F16) as w_hi, \
            nc.sbuf_tensor("o_wlo", [P, SLOTS, KT, P], F16) as w_lo, \
            nc.psum_tensor("o_acc", [P, SLOTS, T], F32) as acc, nc.Block() as block:

        @block.sync
        def _(sp):
            for i in range(steps):
                for s in range(SLOTS):
                    if i:
                        sp.wait_ge(S["low_ready"][s], i)
                    sp.dma_start(w[:, s].rearrange("p k n -> p (k n)"), weights[l * KT + i * SLOTS + s]).then_inc(S["w_loaded"][s], 16)

        @block.scalar
        def _(act):
            for i in range(steps):
                for s in range(SLOTS):
                    act.wait_ge(S["w_loaded"][s], i * 16 + 16)
                    if i:
                        act.wait_ge(S["product_done"][s], i)
                    nc.scalar.activation(w_hi[:, s], w[:, s], ACT.Copy, scale=W_SCALE).then_inc(S["high_ready"][s], 1)

        @block.tensor
        def _(pe):
            for i in range(steps):
                for s in range(SLOTS):
                    pe.wait_ge(S["low_ready"][s], i + 1)
                    if i:
                        pe.wait_ge(S["added"][s], i)
                    for k in range(KT):
                        nc.tensor.matmul(acc[:, s], w_hi[:, s, k], act_hi[:, k], start=k == 0, stop=False)
                        nc.tensor.matmul(acc[:, s], w_hi[:, s, k], act_lo[:, k], start=False, stop=False)
                        last = nc.tensor.matmul(acc[:, s], w_lo[:, s, k], act_hi[:, k], start=False, stop=k == KT - 1)
                    last.then_inc(S["product_done"][s], 1)

        @block.vector
        def _(dve):
            def split_rest(i, s):
                dve.wait_ge(S["high_ready"][s], i + 1)
                nc.vector.scalar_tensor_tensor(w_lo[:, s], w[:, s], W_SCALE, w_hi[:, s], ALU.mult, ALU.subtract).then_inc(S["low_ready"][s], 1)

            for s in range(SLOTS):
                split_rest(0, s)
            for i in range(steps):
                for s in range(SLOTS):
                    n = i * SLOTS + s
                    if i + 1 < steps:
                        split_rest(i + 1, s)
                    dve.wait_ge(S["product_done"][s], i + 1)
                    nc.vector.scalar_tensor_tensor(hT[:, n], acc[:, s], 1.0 / W_SCALE, hT[:, n], ALU.mult, ALU.add).then_inc(S["added"][s], 1)
    end_phase(nc, S)


LOWEST = -3.0e38


def route_phase(nc, bufs, l, tb, dram, routes):
    consts = bufs["consts"]
    queries, keys = dram["queries"], dram["keys"]
    ident = consts[:, CONSTS["ident"]:CONSTS["ident"] + P]
    iota16 = consts[:, CONSTS["iota16"]:CONSTS["iota16"] + TOPK]
    H2 = 2 * HEADS
    S = phase_sems(nc, "route", "q_loaded keys_loaded scores_psum scores_ready top first_index rest second rest_index pairs_ready "
                       "best best_index pair_rest best_second pair_index shifted exp_ready summed inverse gated "
                       "position_row position_col float_ready one_hot picked chosen turned routes_ready")
    sb = lambda name, shape, dt=F32: nc.sbuf_tensor("t_" + name, shape, dt)
    with ExitStack() as mem:
        q = mem.enter_context(sb("q", [P, H2, P]))
        key = mem.enter_context(sb("keys", [P, H2, NKEYS]))
        s = mem.enter_context(sb("s", [P, H2, NKEYS]))
        s2 = mem.enter_context(sb("s2", [P, H2, NKEYS]))
        top = mem.enter_context(sb("top", [P, H2, TOPK]))
        topi = mem.enter_context(sb("topi", [P, H2, TOPK], U32))
        pair = mem.enter_context(sb("pair", [P, HEADS, TOPK, TOPK]))
        pair2 = mem.enter_context(sb("pair2", [P, HEADS, TOPK, TOPK]))
        best = mem.enter_context(sb("best", [P, HEADS, TOPK]))
        bpos = mem.enter_context(sb("bpos", [P, HEADS, TOPK], U32))
        pos = mem.enter_context(sb("pos", [P, 2, HEADS, TOPK], U32))
        posf = mem.enter_context(sb("posf", [P, 2, HEADS, TOPK]))
        topf = mem.enter_context(sb("topf", [P, H2, TOPK]))
        ex = mem.enter_context(sb("ex", [P, HEADS, TOPK]))
        total = mem.enter_context(sb("sum", [P, HEADS]))
        inv = mem.enter_context(sb("inv", [P, HEADS]))
        hot = mem.enter_context(sb("hot", [P, 2, HEADS, TOPK, TOPK]))
        out = mem.enter_context(sb("out", [P, 3, HEADS, TOPK]))
        ps = mem.enter_context(nc.psum_tensor("t_ps", [P, 4, T], F32))
        turn = mem.enter_context(nc.psum_tensor("t_turn", [P, 3, P], F32))
        block = mem.enter_context(nc.Block())

        @block.sync
        def _(sp):
            sp.dma_start(q[:], queries.rearrange("n p t -> p n t")[:, :, ds(tb * P, P)]).then_inc(S["q_loaded"], 16)

        @block.scalar
        def _(act):
            act.dma_start(key[:].rearrange("p n k -> p (n k)"), keys[l]).then_inc(S["keys_loaded"], 16)
            for n in range(4):
                act.wait_ge(S["scores_psum"], n + 1)
                nc.scalar.activation(s[:, 4 * n:4 * n + 4].rearrange("p n k -> p (n k)"), ps[:, n], ACT.Copy).then_inc(S["scores_ready"], 1)
            act.wait_ge(S["shifted"], 1)
            nc.scalar.activation(ex[:], ex[:], ACT.Exp).then_inc(S["exp_ready"], 1)
            act.wait_ge(S["turned"], 1)
            nc.scalar.activation(routes[:, :, ds(tb * P, P)], turn[:], ACT.Copy).then_inc(S["routes_ready"], 1)

        @block.tensor
        def _(pe):
            pe.wait_ge(S["q_loaded"], 16)
            pe.wait_ge(S["keys_loaded"], 16)
            for n in range(4):
                for x in range(4):
                    last = nc.tensor.matmul(ps[:, n, x * P:(x + 1) * P], q[:, 4 * n + x], key[:, 4 * n + x], start=True, stop=True)
                last.then_inc(S["scores_psum"], 1)
            pe.wait_ge(S["gated"], 1)
            pe.wait_ge(S["chosen"], 2)
            for n in range(3):
                last = nc.tensor.transpose(turn[:, n], out[:, n].rearrange("p h k -> p (h k)"), ident)
            last.then_inc(S["turned"], 1)

        @block.vector
        def _(dve):
            V = nc.vector
            for n in range(H2):
                if n % 4 == 0:
                    dve.wait_ge(S["scores_ready"], n // 4 + 1)
                V.max(top[:, n, 0:8], s[:, n]).then_inc(S["top"], 1)
            for n in range(H2):
                dve.wait_ge(S["top"], n + 1)
                V.max_index(topi[:, n, 0:8], top[:, n, 0:8], s[:, n]).then_inc(S["first_index"], 1)
                V.match_replace(s2[:, n], top[:, n, 0:8], s[:, n], LOWEST).then_inc(S["rest"], 1)
            for n in range(H2):
                dve.wait_ge(S["rest"], n + 1)
                V.max(top[:, n, 8:16], s2[:, n]).then_inc(S["second"], 1)
            for n in range(H2):
                dve.wait_ge(S["second"], n + 1)
                V.max_index(topi[:, n, 8:16], top[:, n, 8:16], s2[:, n]).then_inc(S["rest_index"], 1)
            dve.wait_ge(S["top"], H2)
            halves = top[:].rearrange("p (h c) k -> p h c k", c=2)
            V.tensor_tensor(pair[:], halves[:, :, 0].unsqueeze(3).broadcast_to([P, HEADS, TOPK, TOPK]),
                            halves[:, :, 1].unsqueeze(2).broadcast_to([P, HEADS, TOPK, TOPK]), ALU.add).then_inc(S["pairs_ready"], 1)
            dve.wait_ge(S["pairs_ready"], 1)
            flat = lambda a, h: a[:, h].rearrange("p a b -> p (a b)")
            for h in range(HEADS):
                V.max(best[:, h, 0:8], flat(pair, h)).then_inc(S["best"], 1)
            for h in range(HEADS):
                dve.wait_ge(S["best"], h + 1)
                V.max_index(bpos[:, h, 0:8], best[:, h, 0:8], flat(pair, h)).then_inc(S["best_index"], 1)
                V.match_replace(flat(pair2, h), best[:, h, 0:8], flat(pair, h), LOWEST).then_inc(S["pair_rest"], 1)
            for h in range(HEADS):
                dve.wait_ge(S["pair_rest"], h + 1)
                V.max(best[:, h, 8:16], flat(pair2, h)).then_inc(S["best_second"], 1)
            for h in range(HEADS):
                dve.wait_ge(S["best_second"], h + 1)
                V.max_index(bpos[:, h, 8:16], best[:, h, 8:16], flat(pair2, h)).then_inc(S["pair_index"], 1)
            V.tensor_tensor(ex[:], best[:], best[:, :, 0:1].broadcast_to([P, HEADS, TOPK]), ALU.subtract).then_inc(S["shifted"], 1)
            dve.wait_ge(S["exp_ready"], 1)
            V.tensor_reduce(total[:], ex[:], AX.X, ALU.add).then_inc(S["summed"], 1)
            dve.wait_ge(S["summed"], 1)
            V.reciprocal(inv[:], total[:]).then_inc(S["inverse"], 1)
            dve.wait_ge(S["inverse"], 1)
            V.tensor_tensor(out[:, 2], ex[:], inv[:].unsqueeze(2).broadcast_to([P, HEADS, TOPK]), ALU.mult).then_inc(S["gated"], 1)
            dve.wait_ge(S["pair_index"], HEADS)
            dve.wait_ge(S["best_index"], HEADS)
            V.tensor_scalar(pos[:, 0], bpos[:], 4, None, ALU.logical_shift_right).then_inc(S["position_row"], 1)
            V.tensor_scalar(pos[:, 1], bpos[:], 15, None, ALU.bitwise_and).then_inc(S["position_col"], 1)
            dve.wait_ge(S["first_index"], H2)
            dve.wait_ge(S["rest_index"], H2)
            V.tensor_copy(topf[:], topi[:]).then_inc(S["float_ready"], 1)
            dve.wait_ge(S["position_row"], 1)
            dve.wait_ge(S["position_col"], 1)
            V.tensor_copy(posf[:], pos[:]).then_inc(S["float_ready"], 1)
            dve.wait_ge(S["float_ready"], 2)
            index = topf[:].rearrange("p (h c) k -> p h c k", c=2)
            for c in range(2):
                for h in range(HEADS):
                    V.tensor_tensor(hot[:, c, h], posf[:, c, h].unsqueeze(2).broadcast_to([P, TOPK, TOPK]),
                                    iota16.unsqueeze(1).broadcast_to([P, TOPK, TOPK]), ALU.is_equal).then_inc(S["one_hot"], 1)
            for c in range(2):
                dve.wait_ge(S["one_hot"], HEADS * (c + 1))
                V.tensor_tensor(hot[:, c], hot[:, c], index[:, :, c].unsqueeze(2).broadcast_to([P, HEADS, TOPK, TOPK]), ALU.mult).then_inc(S["picked"], 1)
                dve.wait_ge(S["picked"], c + 1)
                V.tensor_reduce(out[:, c], hot[:, c], AX.X, ALU.add).then_inc(S["chosen"], 1)
    end_phase(nc, S)


GT = 8


def gates_phase(nc, bufs, l, tb, dram, routes):
    consts = bufs["consts"]
    iota = consts[:, CONSTS["iota128"]:CONSTS["iota128"] + P]
    S = phase_sems(nc, "gates", "rows_ready*2 built*2 copied*2 stored")
    steps = P // (2 * GT)
    with nc.sbuf_tensor("g_rows", [P, 2, GT, P], F32) as rows, nc.sbuf_tensor("g_cols", [P, 2, GT, P], F32) as cols, \
            nc.sbuf_tensor("g_dense", [P, NKEYS, P], F32) as dense, \
            nc.psum_tensor("g_ps", [P, 4, T], F32) as ps, nc.Block() as block:

        @block.sync
        def _(sp):
            for x in range(2):
                sp.wait_ge(S["copied"][x], 2 * steps)
            sp.dma_start(dram["gates"].rearrange("j p t -> p j t")[:, :, ds(tb * P, P)], dense[:]).then_inc(S["stored"], 16)
            sp.wait_ge(S["stored"], 16)

        @block.vector
        def _(dve):
            def build(i, x):
                for t in range(GT):
                    at = tb * P + (2 * i + x) * GT + t
                    nc.vector.tensor_scalar(rows[:, x, t], iota, routes[:, 0, ds(at, 1)], routes[:, 2, ds(at, 1)], ALU.is_equal, ALU.mult)
                    last = nc.vector.tensor_scalar(cols[:, x, t], iota, routes[:, 1, ds(at, 1)], None, ALU.is_equal)
                last.then_inc(S["rows_ready"][x], 1)

            for x in range(2):
                build(0, x)
            with dve.Fori(1, steps) as i:
                for x in range(2):
                    dve.wait_ge(S["built"][x], i)
                    build(i, x)

        @block.tensor
        def _(pe):
            def products(i, x):
                pe.wait_ge(S["rows_ready"][x], i + 1)
                for t in range(GT):
                    last = nc.tensor.matmul(ps[:, 2 * x + t // 4, (t % 4) * P:(t % 4 + 1) * P], rows[:, x, t], cols[:, x, t], start=True, stop=True)
                last.then_inc(S["built"][x], 1)

            for x in range(2):
                products(0, x)
            with pe.Fori(1, steps) as i:
                for x in range(2):
                    pe.wait_ge(S["copied"][x], 2 * i)
                    products(i, x)

        @block.scalar
        def _(act):
            with act.Fori(0, steps) as i:
                for x in range(2):
                    act.wait_ge(S["built"][x], i + 1)
                    for b in range(2):
                        nc.scalar.activation(dense[:, :, ds((2 * i + x) * GT + 4 * b, 4)], ps[:, 2 * x + b].rearrange("p (t j) -> p j t", t=4),
                                             ACT.Copy).then_inc(S["copied"][x], 1)
    end_phase(nc, S)


EG = 8


def experts_phase(nc, bufs, l, dram, act_hi, act_lo):
    hT = bufs["hT"]
    down, gates = dram["down"], dram["gates"]
    up_tiles = dram["up"].rearrange("l (i j) d -> l j i d", j=NKEYS)
    S = phase_sems(nc, "experts", "down_loaded*2 down_high*2 down_low*2 hidden_psum*2 gelu_done*2 gate_loaded*2 weighted*2 "
                       "share_high*8 share_low*8 up_loaded*2 up_high*8 up_low*8 out_psum*2 added*2")
    groups = NKEYS // EG
    sb = lambda name, shape, dt=F32: nc.sbuf_tensor("x_" + name, shape, dt)
    with ExitStack() as mem:
        dn = mem.enter_context(sb("down", [P, 2, D]))
        d_hi = mem.enter_context(sb("dhi", [P, 2, KT, P], F16))
        d_lo = mem.enter_context(sb("dlo", [P, 2, KT, P], F16))
        u = mem.enter_context(sb("up", [P, 2, D]))
        u_hi = mem.enter_context(sb("uhi", [P, EG, D], F16))
        u_lo = mem.enter_context(sb("ulo", [P, EG, D], F16))
        gate = mem.enter_context(sb("gate", [P, 2, T]))
        gelu = mem.enter_context(sb("gelu", [P, 2, T]))
        share = mem.enter_context(sb("share", [P, 2, T]))
        s_hi = mem.enter_context(sb("shi", [P, EG, T], F16))
        s_lo = mem.enter_context(sb("slo", [P, EG, T], F16))
        ps = mem.enter_context(nc.psum_tensor("x_ps", [P, 4, T], F32))
        block = mem.enter_context(nc.Block())
        flat = lambda a: a.rearrange("p k n -> p (k n)")
        use = lambda g, e: (e % 2, 4 * g + e // 2)

        def ahead(g, e, last):
            return None if last and e + 2 >= EG else (g + (e + 2) // EG, (e + 2) % EG)

        @block.sync
        def _(sp):
            def loads(g, e, first):
                x, n = use(g, e)
                if not (first and e < 2):
                    sp.wait_ge(S["down_low"][x], n)
                sp.dma_start(dn[:, x], down[l * NKEYS + g * EG + e]).then_inc(S["down_loaded"][x], 16)
                if not (first and e < 2):
                    sp.wait_ge(S["weighted"][x], n)
                sp.dma_start(gate[:, x], gates[g * EG + e]).then_inc(S["gate_loaded"][x], 16)
                if not (first and e < 2):
                    sp.wait_ge(S["up_low"][(e - 2) % EG], g + (e >= 2))
                sp.dma_start(u[:, x], up_tiles[ds(l, 1), ds(g * EG + e, 1)].rearrange("a b i d -> i (a b d)")).then_inc(S["up_loaded"][x], 16)

            for e in range(EG):
                loads(0, e, True)
            with sp.Fori(1, groups) as g:
                for e in range(EG):
                    loads(g, e, False)

        @block.scalar
        def _(act):
            def split_down(g, e, first):
                x, n = use(g, e)
                act.wait_ge(S["down_loaded"][x], 16 * n + 16)
                if not first:
                    act.wait_ge(S["hidden_psum"][x], n)
                nc.scalar.activation(flat(d_hi[:, x]), dn[:, x], ACT.Copy, scale=W_SCALE).then_inc(S["down_high"][x], 1)

            def group(g, first, last):
                for e in range(EG):
                    x, n = use(g, e)
                    if not first:
                        act.wait_ge(S["out_psum"][1], 4 * g)
                    act.wait_ge(S["up_loaded"][x], 16 * n + 16)
                    nc.scalar.activation(u_hi[:, e], u[:, x], ACT.Copy, scale=W_SCALE).then_inc(S["up_high"][e], 1)
                    if not (first and e < 2):
                        act.wait_ge(S["weighted"][x], n)
                    act.wait_ge(S["hidden_psum"][x], n + 1)
                    nc.scalar.activation(gelu[:, x], ps[:, x], ACT.Gelu_apprx_tanh, scale=1.0 / W_SCALE).then_inc(S["gelu_done"][x], 1)
                    if ahead(g, e, last):
                        split_down(*ahead(g, e, last), False)
                    act.wait_ge(S["weighted"][x], n + 1)
                    nc.scalar.activation(s_hi[:, e], share[:, x], ACT.Copy).then_inc(S["share_high"][e], 1)

            split_down(0, 0, True)
            split_down(0, 1, True)
            group(0, True, False)
            with act.Fori(1, groups - 1) as g:
                group(g, False, False)
            group(groups - 1, False, True)

        @block.vector
        def _(dve):
            V = nc.vector

            def split_down(g, e):
                x, n = use(g, e)
                dve.wait_ge(S["down_high"][x], n + 1)
                V.scalar_tensor_tensor(flat(d_lo[:, x]), dn[:, x], W_SCALE, flat(d_hi[:, x]), ALU.mult, ALU.subtract).then_inc(S["down_low"][x], 1)

            def group(g, last):
                for e in range(EG):
                    x, n = use(g, e)
                    dve.wait_ge(S["up_high"][e], g + 1)
                    V.scalar_tensor_tensor(u_lo[:, e], u[:, x], W_SCALE, u_hi[:, e], ALU.mult, ALU.subtract).then_inc(S["up_low"][e], 1)
                    dve.wait_ge(S["gate_loaded"][x], 16 * n + 16)
                    dve.wait_ge(S["gelu_done"][x], n + 1)
                    V.tensor_tensor(share[:, x], gelu[:, x], gate[:, x], ALU.mult).then_inc(S["weighted"][x], 1)
                    if ahead(g, e, last):
                        split_down(*ahead(g, e, last))
                    dve.wait_ge(S["share_high"][e], g + 1)
                    V.tensor_tensor(s_lo[:, e], share[:, x], s_hi[:, e], ALU.subtract).then_inc(S["share_low"][e], 1)
                for k in range(KT):
                    x, n = use(g, k)
                    dve.wait_ge(S["out_psum"][x], n + 1)
                    V.scalar_tensor_tensor(hT[:, k], ps[:, 2 + x], 1.0 / W_SCALE, hT[:, k], ALU.mult, ALU.add).then_inc(S["added"][x], 1)

            split_down(0, 0)
            split_down(0, 1)
            group(0, False)
            with dve.Fori(1, groups - 1) as g:
                group(g, False)
            group(groups - 1, True)

        @block.tensor
        def _(pe):
            mm = nc.tensor.matmul

            def hidden(g, e, first):
                x, n = use(g, e)
                pe.wait_ge(S["down_low"][x], n + 1)
                if not first:
                    pe.wait_ge(S["gelu_done"][x], n)
                for k in range(KT):
                    mm(ps[:, x], d_hi[:, x, k], act_hi[:, k], start=k == 0, stop=False)
                    mm(ps[:, x], d_hi[:, x, k], act_lo[:, k], start=False, stop=False)
                    last = mm(ps[:, x], d_lo[:, x, k], act_hi[:, k], start=False, stop=k == KT - 1)
                last.then_inc(S["hidden_psum"][x], 1)

            def output(g, k, first):
                x, n = use(g, k)
                if not first:
                    pe.wait_ge(S["added"][x], n)
                cut = slice(k * P, (k + 1) * P)
                for e in range(EG):
                    if k == 0:
                        pe.wait_ge(S["share_low"][e], g + 1)
                        pe.wait_ge(S["up_low"][e], g + 1)
                    mm(ps[:, 2 + x], u_hi[:, e, cut], s_hi[:, e], start=e == 0, stop=False)
                    mm(ps[:, 2 + x], u_hi[:, e, cut], s_lo[:, e], start=False, stop=False)
                    last = mm(ps[:, 2 + x], u_lo[:, e, cut], s_hi[:, e], start=False, stop=e == EG - 1)
                last.then_inc(S["out_psum"][x], 1)

            def group(g, first, last):
                for e in range(1, EG):
                    hidden(g, e, first and e < 2)
                if not last:
                    hidden(g + 1, 0, False)
                for k in range(KT):
                    output(g, k, first and k < 2)

            hidden(0, 0, True)
            group(0, True, False)
            with pe.Fori(1, groups - 1) as g:
                group(g, False, False)
            group(groups - 1, False, True)
    end_phase(nc, S)


def load_phase(nc, bufs, dram):
    S = phase_sems(nc, "load", "loaded")
    with nc.Block() as block:

        @block.sync
        def _(sp):
            sp.dma_start(bufs["consts"][:], dram["consts"]).then_inc(S["loaded"], 16)
            sp.dma_start(bufs["hT"][:].rearrange("p k t -> p (k t)"), dram["x"]).then_inc(S["loaded"], 16)
            sp.wait_ge(S["loaded"], 32)
    end_phase(nc, S)


def params_phase(nc, bufs, l, dram):
    S = phase_sems(nc, "params", "loaded")
    with nc.Block() as block:

        @block.sync
        def _(sp):
            sp.dma_start(bufs["params"][:], dram["params"][l]).then_inc(S["loaded"], 16)
            sp.wait_ge(S["loaded"], 16)
    end_phase(nc, S)


def trunk(nc, dram, out):
    internal = lambda name, shape: nc.dram_tensor(name, shape, F32, kind="Internal").ap()
    dram = dict(dram)
    dram["projected"] = internal("projected", [IN_TILES, P, T])
    dram["v_mixed"] = internal("v_mixed", [LAYERS * KT, P, T])
    dram["queries"] = internal("queries", [2 * HEADS, P, T])
    dram["gates"] = internal("gates", [NKEYS, P, T])
    sb = lambda name, shape, dt=F32: nc.sbuf_tensor(name, shape, dt)
    split = lambda name, n: (sb(name + "_hi", [P, n, T], F16), sb(name + "_lo", [P, n, T], F16))
    with sb("hT", [P, KT, T]) as hT, sb("consts", [P, N_CONSTS]) as consts, sb("params", [P, N_PARAMS]) as params:
        bufs = {"hT": hT, "consts": consts, "params": params}
        load_phase(nc, bufs, dram)
        with nc.Fori(0, LAYERS) as l:
            params_phase(nc, bufs, l, dram)
            with sb("u_hi", [P, KT, T], F16) as act_hi, sb("u_lo", [P, KT, T], F16) as act_lo:
                norm_phase(nc, bufs, "norm_mix", PARAMS["norm_mix"], act_hi, act_lo)
                project_phase(nc, bufs, l, dram["w_in"], IN_TILES, act_hi, act_lo, dram["projected"], "in")
            with sb("mixed_hi", [P, 24, T], F16) as mixed_hi, sb("mixed_lo", [P, 24, T], F16) as mixed_lo:
                with sb("low_wa", [P, T]) as low_wa, sb("low_g", [P, T]) as low_g, sb("low_gv", [P, T]) as low_gv:
                    lora = low_wa, low_g, low_gv
                    lora_phase(nc, bufs, l, lora, dram)
                    with nc.Fori(0, RWKV_TILES) as hp:
                        rwkv_pair_phase(nc, bufs, l, hp, lora, dram, mixed_hi, mixed_lo)
                with sb("acs", [P, T]) as acs, sb("table", [P, SSD_GROUPS, 5, SNC, GROUP_HEADS]) as table:
                    dt_phase(nc, bufs, l, dram, acs, table)
                    with nc.Fori(0, SSD_GROUPS) as g:
                        ssd_group_phase(nc, bufs, l, g, dram, acs, table, mixed_hi, mixed_lo)
                with sb("o_hi", [P, KT, T], F16) as act_hi, sb("o_lo", [P, KT, T], F16) as act_lo:
                    mix_phase(nc, bufs, l, dram, mixed_hi, mixed_lo, act_hi, act_lo)
                    residual_phase(nc, bufs, l, dram["w_out"], act_hi, act_lo)
            with sb("f_hi", [P, KT, T], F16) as act_hi, sb("f_lo", [P, KT, T], F16) as act_lo:
                norm_phase(nc, bufs, "norm_ffn", PARAMS["norm_ffn"], act_hi, act_lo)
                project_phase(nc, bufs, l, dram["w_q"], 2 * HEADS, act_hi, act_lo, dram["queries"], "q")
                with sb("routes", [P, 3, T]) as routes:
                    with nc.Fori(0, TB) as tb:
                        route_phase(nc, bufs, l, tb, dram, routes)
                        gates_phase(nc, bufs, l, tb, dram, routes)
                experts_phase(nc, bufs, l, dram, act_hi, act_lo)
        norm_phase(nc, bufs, "norm_final", PARAMS["norm_final"], None, None, out)


def kernel(**inputs):
    import concourse.bacc as bacc
    from concourse.bass_utils import run_bass_kernel_spmd

    a = {k: np.asarray(v) for k, v in inputs.items()}
    f = np.float32
    L = LAYERS

    def zeros(*shape):
        return np.zeros(shape, f)

    def tiles(w):
        n = w.shape[2] // P
        return np.ascontiguousarray(w.reshape(L, w.shape[1] // P, P, n, P).transpose(0, 3, 2, 1, 4)).reshape(L * n, P, -1)

    def columns(v):
        return v.reshape(L, -1, P).transpose(0, 2, 1)

    def in_order(v):
        pad = zeros(*v.shape[:-1], P)
        rwkv, gd = v[..., 0:3200], v[..., 3200:3360]
        z, xbc, dt, gates = v[..., 3360:5408], v[..., 5408:8480], v[..., 8480:8512], v[..., 8512:10560]
        return np.concatenate([rwkv, gd, dt, pad[..., 0:64], z, xbc, gates, pad], axis=-1)

    first = lambda v: np.concatenate([zeros(1, *v.shape[1:]), v])
    v0, v1, v2 = first(a["rwkv_v0"]), first(a["rwkv_v1"]), first(a["rwkv_v2"])
    mu = np.concatenate([a["rwkv_mu"], zeros(L, 96)], axis=-1)
    at_dt = lambda v: np.concatenate([zeros(L, 32), v, zeros(L, 64)], axis=-1)
    final = np.broadcast_to(a["norm_final_g"], (L, D))
    conv_w = np.concatenate([columns(a["ssd_conv_w"][:, j]) for j in range(4)], axis=-1)
    per_feature = np.repeat(a["ssd_D"], 64, axis=-1)
    params = np.concatenate([columns(v) for v in (
        a["norm_mix_g"], mu, a["rwkv_w0"], a["rwkv_a0"], v0, a["rwkv_k_k"], a["rwkv_k_a"],
        a["rwkv_r_k"].reshape(L, -1), a["rwkv_ln_w"], a["rwkv_ln_b"])] + [conv_w] + [columns(v) for v in (
            a["ssd_conv_b"], a["ssd_norm_g"], per_feature, at_dt(a["ssd_dt_bias"]), at_dt(a["ssd_A_log"]),
            a["norm_ffn_g"], final)], axis=-1)
    p = PARAMS
    pair_pack = zeros(L, RWKV_TILES, P, PACK_COLS)
    for n in range(RWKV_TILES):
        cut = slice(n * P, (n + 1) * P)
        pair_pack[:, n, 0:64, 0:P] = a["rwkv_w2"][:, :, cut]
        pair_pack[:, n, 64:128, 0:P] = a["rwkv_a2"][:, :, cut]
        pair_pack[:, n, :, P:2 * P] = a["rwkv_g2"][:, 0:P, cut]
        pair_pack[:, n, 0:32, 2 * P:3 * P] = a["rwkv_g2"][:, P:160, cut]
        pair_pack[:, n, 32:64, 2 * P:3 * P] = v2[:, :, cut]
        for col, at in ((MU_R, p["mu"] + R0), (MU_K, p["mu"] + K0), (W0, p["w0"]), (A0, p["a0"]), (V0P, p["v0"]),
                        (K_K, p["k_k"]), (K_A, p["k_a"]), (R_K, p["r_k"]), (LN_W, p["ln_w"]), (LN_B, p["ln_b"])):
            pair_pack[:, n, :, col] = params[:, :, at + n]
    group_pack = zeros(L, SSD_GROUPS, P, GROUP_COLS)
    for g in range(SSD_GROUPS):
        for n, t in enumerate([4 * g, 4 * g + 1, 4 * g + 2, 4 * g + 3, 16 + g, 20 + g]):
            for j in range(4):
                group_pack[:, g, :, G_CONV + 4 * n + j] = params[:, :, p["conv_w"] + 24 * j + t]
            group_pack[:, g, :, G_BIAS + n] = params[:, :, p["conv_b"] + t]
        for n in range(4):
            group_pack[:, g, :, G_GAIN + n] = params[:, :, p["ssd_norm"] + 4 * g + n]
            group_pack[:, g, :, G_D + n] = params[:, :, p["D"] + 4 * g + n]
    select = zeros(SSD_GROUPS, 32, GROUP_HEADS, P)
    for h in range(SSD_HEADS):
        select[h // GROUP_HEADS, h, h % GROUP_HEADS] = 1.0
    branches = np.stack([tiles(a["w_rwkv_branch"]).reshape(L, KT, P, D),
                         tiles(a["w_ssd_branch"][:, 0:D]).reshape(L, KT, P, D),
                         tiles(a["w_ssd_branch"][:, D:]).reshape(L, KT, P, D)], axis=2).reshape(L * KT * MIX, P, D)
    down = a["peer_down"].reshape(L, NKEYS, NKEYS, KT, P).transpose(0, 2, 4, 3, 1)
    arrays = {
        "x": np.ascontiguousarray(a["x"][0].T.reshape(KT, P, T).transpose(1, 0, 2)).reshape(P, KT * T),
        "consts": make_consts(), "select": select.reshape(SSD_GROUPS, 32, -1), "params": params,
        "w_in": tiles(in_order(a["w_in"])), "w_branches": branches, "w_out": tiles(a["w_out"]),
        "w_q": tiles(a["peer_w_q"]), "pair_pack": pair_pack.reshape(L * RWKV_TILES, P, PACK_COLS),
        "group_pack": group_pack.reshape(L * SSD_GROUPS, P, GROUP_COLS),
        "v1": v1.reshape(L, KT, P, 32).transpose(0, 2, 1, 3).reshape(L, P, KT * 32),
        "keys": a["peer_sub_keys"].reshape(L, 2 * HEADS, NKEYS, P).transpose(0, 3, 1, 2).reshape(L, P, -1),
        "down": down.reshape(L * NKEYS, P, D), "up": a["peer_up"],
    }
    nc = bacc.Bacc("TRN2", target_bir_lowering=False, num_devices=1)
    data, dram = {}, {}
    for name, v in arrays.items():
        data["in_" + name] = np.ascontiguousarray(v)
        dram[name] = nc.dram_tensor("in_" + name, v.shape, F32, kind="ExternalInput").ap()
    out = nc.dram_tensor("out_t", (P, KT, T), F32, kind="ExternalOutput").ap()
    trunk(nc, dram, out)
    r = run_bass_kernel_spmd(nc, [data], core_ids=[0])
    got = np.asarray(r.results[0]["out_t"])
    return np.ascontiguousarray(got.transpose(1, 0, 2).reshape(D, T).T)[None]
```

```python
from contextlib import ExitStack

import numpy as np
import concourse.bass as bass
from concourse import mybir

F32 = mybir.dt.float32
F16 = mybir.dt.float16
U32 = mybir.dt.uint32
ALU = mybir.AluOpType
ACT = mybir.ActivationFunctionType
AX = mybir.AxisListType
ds = bass.ds

P = 128
LAYERS, T, D = 2, 512, 1024
KT = D // P
HS = 64
RWKV_TILES = D // P
CH = 64
NC = T // CH
SSD_HEADS, SSD_GROUPS, GROUP_HEADS = 32, 4, 8
SCH = 128
SNC = T // SCH
TB = T // P
HEADS, NKEYS, TOPK = 8, 128, 16
HK = HEADS * TOPK
NORM_EPS, GN_EPS, KK_EPS = 1e-6, 64e-5, 1e-12
DECAY_SCALE = float(np.exp(np.float64(-0.5)))

R0, K0, V0, WA, GD, GDT, Z0, X0, B0, C0, GA, GB = 0, 8, 16, 24, 25, 26, 27, 43, 59, 63, 67, 75
IN_TILES = 84
SLOTS = 4
W_SCALE = 64.0

PARAMS = {}
_at = 0
for _name, _n in (("norm_mix", 8), ("mu", 27), ("w0", 8), ("a0", 8), ("v0", 8), ("k_k", 8), ("k_a", 8),
                  ("r_k", 8), ("ln_w", 8), ("ln_b", 8), ("conv_w", 96), ("conv_b", 24), ("ssd_norm", 16),
                  ("D", 16), ("dt_bias", 1), ("A_log", 1), ("norm_ffn", 8), ("norm_final", 8)):
    PARAMS[_name] = _at
    _at += _n
N_PARAMS = _at

CONSTS = {}
_at = 0
for _name, _n in (("ident", 128), ("mean", 128), ("head_ones", 128), ("head_mean", 128), ("scores", 128),
                  ("levels_q", 6 * 64), ("level0_n", 64), ("eye64", 64), ("ssd_mask", 128),
                  ("chunk_start", 512), ("ssd_start", 512), ("iota128", 128), ("iota16", 16), ("eps", 3)):
    CONSTS[_name] = _at
    _at += _n
N_CONSTS = _at


def make_consts():
    c = np.zeros((P, N_CONSTS), np.float32)

    def put(name, a):
        c[:a.shape[0], CONSTS[name]:CONSTS[name] + a.shape[1]] = a

    i = np.arange(P)
    put("ident", np.eye(P, dtype=np.float32))
    put("mean", np.full((P, P), 1.0 / D, np.float32))
    same_head = (i[:, None] // HS == i[None, :] // HS).astype(np.float32)
    put("head_ones", same_head)
    put("head_mean", same_head / HS)
    j, q = i[:, None] % CH, i[None, :] % CH
    put("scores", np.where(i[None, :] < CH, j < q, j <= q).astype(np.float32))
    j, q = i[:, None] % CH, np.arange(CH)[None, :]
    for s in range(6):
        b = 1 << s
        m = (j // (2 * b) == q // (2 * b)) & (j % (2 * b) < b) & (q % (2 * b) >= b)
        c[:, CONSTS["levels_q"] + s * 64:CONSTS["levels_q"] + (s + 1) * 64] = m
    put("level0_n", ((j // 2 == q // 2) & (j % 2 == 1) & (q % 2 == 0)).astype(np.float32))
    put("eye64", (j == q).astype(np.float32))
    put("ssd_mask", (i[:, None] <= i[None, :]).astype(np.float32))
    t = np.arange(T)
    put("chunk_start", np.broadcast_to((t % CH != 0).astype(np.float32), (P, T)))
    put("ssd_start", np.broadcast_to((t % SCH != 0).astype(np.float32), (P, T)))
    put("iota128", np.broadcast_to(i.astype(np.float32), (P, P)))
    put("eps", np.broadcast_to(np.array([NORM_EPS, GN_EPS, KK_EPS], np.float32), (P, 3)))
    put("iota16", np.broadcast_to(np.arange(16, dtype=np.float32), (P, 16)))
    return c


def phase_sems(nc, phase, names):
    out = {}
    for name in names.split():
        name, _, n = name.partition("*")
        out[name] = [nc.alloc_semaphore(f"{phase}_{name}{i}") for i in range(int(n))] if n else nc.alloc_semaphore(f"{phase}_{name}")
    return out


def end_phase(nc, sems):
    flat = [s for v in sems.values() for s in (v if isinstance(v, list) else [v])]
    nc.clear_and_free_semaphores(flat)
    nc.all_engine_barrier()


def norm_phase(nc, bufs, name, gain_column, act_hi, act_lo, to_dram=None):
    hT, consts, params = bufs["hT"], bufs["consts"], bufs["params"]
    mean = consts[:, CONSTS["mean"]:CONSTS["mean"] + P]
    S = phase_sems(nc, name, "squared summed log_ready inverse_ready scaled high_done low_done stored")
    with nc.sbuf_tensor(name + "_sq", [P, 2, T], F32) as sq, nc.sbuf_tensor(name + "_inverse", [P, T], F32) as inverse, \
            nc.sbuf_tensor(name + "_u", [P, KT, T], F32) as u, nc.psum_tensor(name + "_ss", [P, 2, T], F32) as ss, \
            nc.Block() as block:

        @block.scalar
        def _(act):
            for k in range(KT):
                if k >= 2:
                    act.wait_ge(S["summed"], k - 1)
                nc.scalar.activation(sq[:, k % 2, :], hT[:, k, :], ACT.Square).then_inc(S["squared"], 1)
            act.wait_ge(S["summed"], KT)
            nc.scalar.activation(inverse[:], ss[:, 0, :], ACT.Ln, bias=consts[:, CONSTS["eps"]:CONSTS["eps"] + 1]).then_inc(S["log_ready"], 1)
            act.wait_ge(S["log_ready"], 1)
            nc.scalar.activation(inverse[:], inverse[:], ACT.Exp, scale=-0.5).then_inc(S["inverse_ready"], 1)
            if to_dram is None:
                for k in range(KT):
                    act.wait_ge(S["scaled"], k + 1)
                    nc.scalar.activation(act_hi[:, k, :], u[:, k, :], ACT.Copy).then_inc(S["high_done"], 1)

        @block.tensor
        def _(pe):
            for k in range(KT):
                pe.wait_ge(S["squared"], k + 1)
                nc.tensor.matmul(ss[:, 0, :], mean, sq[:, k % 2, :], start=k == 0, stop=k == KT - 1).then_inc(S["summed"], 1)

        @block.vector
        def _(dve):
            dve.wait_ge(S["inverse_ready"], 1)
            for k in range(KT):
                nc.vector.scalar_tensor_tensor(u[:, k, :], hT[:, k, :], params[:, gain_column + k:gain_column + k + 1],
                                               inverse[:], ALU.mult, ALU.mult).then_inc(S["scaled"], 1)
            if to_dram is None:
                for k in range(KT):
                    dve.wait_ge(S["high_done"], k + 1)
                    dve.wait_ge(S["scaled"], k + 1)
                    nc.vector.tensor_tensor(act_lo[:, k, :], u[:, k, :], act_hi[:, k, :], ALU.subtract).then_inc(S["low_done"], 1)

        @block.sync
        def _(sp):
            if to_dram is not None:
                for k in range(KT):
                    sp.wait_ge(S["scaled"], k + 1)
                    sp.dma_start(to_dram[:, k, :], u[:, k, :]).then_inc(S["stored"], 16)
                sp.wait_ge(S["stored"], 16 * KT)
    end_phase(nc, S)


def project_phase(nc, bufs, l, weights, tiles, act_hi, act_lo, out, name):
    S = phase_sems(nc, name, "w_loaded*4 high_ready*4 low_ready*4 product_done*4 copied*4 stored*4")
    steps = tiles // SLOTS
    with nc.sbuf_tensor(name + "_w", [P, SLOTS, KT, P], F32) as w, nc.sbuf_tensor(name + "_whi", [P, SLOTS, KT, P], F16) as w_hi, \
            nc.sbuf_tensor(name + "_wlo", [P, SLOTS, KT, P], F16) as w_lo, nc.sbuf_tensor(name + "_o", [P, SLOTS, T], F32) as o, \
            nc.psum_tensor(name + "_acc", [P, SLOTS, T], F32) as acc, nc.Block() as block:

        @block.sync
        def _(sp):
            for s in range(SLOTS):
                sp.dma_start(w[:, s].rearrange("p k n -> p (k n)"), weights[l * tiles + s]).then_inc(S["w_loaded"][s], 16)
            with sp.Fori(1, steps) as i:
                for s in range(SLOTS):
                    sp.wait_ge(S["low_ready"][s], i)
                    sp.dma_start(w[:, s].rearrange("p k n -> p (k n)"), weights[l * tiles + i * SLOTS + s]).then_inc(S["w_loaded"][s], 16)
                    sp.wait_ge(S["copied"][s], i)
                    sp.dma_start(out[(i - 1) * SLOTS + s], o[:, s]).then_inc(S["stored"][s], 16)
            for s in range(SLOTS):
                sp.wait_ge(S["copied"][s], steps)
                sp.dma_start(out[(steps - 1) * SLOTS + s], o[:, s]).then_inc(S["stored"][s], 16)
            for s in range(SLOTS):
                sp.wait_ge(S["stored"][s], 16 * steps)

        @block.scalar
        def _(act):
            def split_high(s):
                nc.scalar.activation(w_hi[:, s], w[:, s], ACT.Copy, scale=W_SCALE).then_inc(S["high_ready"][s], 1)

            for s in range(SLOTS):
                act.wait_ge(S["w_loaded"][s], 16)
                split_high(s)
            with act.Fori(1, steps) as i:
                for s in range(SLOTS):
                    act.wait_ge(S["w_loaded"][s], i * 16 + 16)
                    act.wait_ge(S["product_done"][s], i)
                    split_high(s)

        @block.tensor
        def _(pe):
            def product(s):
                for k in range(KT):
                    nc.tensor.matmul(acc[:, s], w_hi[:, s, k], act_hi[:, k], start=k == 0, stop=False)
                    nc.tensor.matmul(acc[:, s], w_hi[:, s, k], act_lo[:, k], start=False, stop=False)
                    last = nc.tensor.matmul(acc[:, s], w_lo[:, s, k], act_hi[:, k], start=False, stop=k == KT - 1)
                last.then_inc(S["product_done"][s], 1)

            for s in range(SLOTS):
                pe.wait_ge(S["low_ready"][s], 1)
                product(s)
            with pe.Fori(1, steps) as i:
                for s in range(SLOTS):
                    pe.wait_ge(S["low_ready"][s], i + 1)
                    pe.wait_ge(S["copied"][s], i)
                    product(s)

        @block.vector
        def _(dve):
            def split_rest(i, s):
                dve.wait_ge(S["high_ready"][s], i + 1)
                nc.vector.scalar_tensor_tensor(w_lo[:, s], w[:, s], W_SCALE, w_hi[:, s], ALU.mult, ALU.subtract).then_inc(S["low_ready"][s], 1)

            def copy_out(s):
                nc.vector.tensor_scalar(o[:, s], acc[:, s], 1.0 / W_SCALE, None, ALU.mult).then_inc(S["copied"][s], 1)

            for s in range(SLOTS):
                split_rest(0, s)
            for s in range(SLOTS):
                dve.wait_ge(S["product_done"][s], 1)
                copy_out(s)
                split_rest(1, s)
            with dve.Fori(2, steps) as i:
                for s in range(SLOTS):
                    dve.wait_ge(S["stored"][s], i * 16 - 16)
                    dve.wait_ge(S["product_done"][s], i)
                    copy_out(s)
                    split_rest(i, s)
            for s in range(SLOTS):
                dve.wait_ge(S["product_done"][s], steps)
                dve.wait_ge(S["stored"][s], steps * 16 - 16)
                copy_out(s)
    end_phase(nc, S)


PACK_COLS = 3 * P + 12
MU_R, MU_K, W0, A0, V0P, K_K, K_A, R_K, LN_W, LN_B = range(3 * P, 3 * P + 10)


def lora_phase(nc, bufs, l, lora, dram):
    params = bufs["params"]
    projected, v_mixed, v1 = dram["projected"], dram["v_mixed"], dram["v1"]
    low_wa, low_g, low_gv = lora
    S = phase_sems(nc, "lora", "zeroed raw_loaded*11 v1_loaded diffed mixed ready vlow_done vlow_copied stored")
    mu = PARAMS["mu"]
    tiles = [WA, GD, GDT] + [V0 + k for k in range(KT)]
    n = len(tiles)
    with nc.sbuf_tensor("l_raw", [P, n, T + 1], F32) as raw, nc.sbuf_tensor("l_diff", [P, 2, T], F32) as diff, \
            nc.sbuf_tensor("l_mix", [P, n, T], F32) as mix, nc.sbuf_tensor("l_v1", [P, KT, 32], F32) as v1s, \
            nc.psum_tensor("l_vlow", [P, T], F32) as vlow, nc.Block() as block:

        @block.sync
        def _(sp):
            sp.dma_start(v1s[:].rearrange("p k n -> p (k n)"), v1[l]).then_inc(S["v1_loaded"], 16)
            for k in range(KT):
                sp.wait_ge(S["mixed"], 4 + k)
                sp.dma_start(v_mixed[l * KT + k], mix[:, 3 + k]).then_inc(S["stored"], 16)
            sp.wait_ge(S["stored"], 16 * KT)

        @block.scalar
        def _(act):
            for k, t in enumerate(tiles):
                act.dma_start(raw[:, k, 1:], projected[t]).then_inc(S["raw_loaded"][k], 16)
            act.wait_ge(S["mixed"], 3)
            nc.scalar.activation(low_wa[0:64, :], mix[0:64, 0], ACT.Tanh).then_inc(S["ready"], 1)
            nc.scalar.activation(low_wa[64:128, :], mix[64:128, 0], ACT.Copy).then_inc(S["ready"], 1)
            nc.scalar.activation(low_g[:], mix[:, 1], ACT.Sigmoid).then_inc(S["ready"], 1)
            nc.scalar.activation(low_gv[0:32, :], mix[0:32, 2], ACT.Sigmoid).then_inc(S["ready"], 1)
            act.wait_ge(S["vlow_done"], 1)
            nc.scalar.activation(low_gv[32:64, :], vlow[32:64, :], ACT.Copy).then_inc(S["vlow_copied"], 1)

        @block.gpsimd
        def _(pool):
            nc.gpsimd.memset(raw[:, :, 0:1], 0.0).then_inc(S["zeroed"], 1)

        @block.vector
        def _(dve):
            dve.wait_ge(S["zeroed"], 1)
            for k, t in enumerate(tiles):
                dve.wait_ge(S["raw_loaded"][k], 16)
                if k >= 2:
                    dve.wait_ge(S["mixed"], k - 1)
                nc.vector.tensor_tensor(diff[:, k % 2], raw[:, k, 0:T], raw[:, k, 1:], ALU.subtract).then_inc(S["diffed"], 1)
                dve.wait_ge(S["diffed"], k + 1)
                nc.vector.scalar_tensor_tensor(mix[:, k], diff[:, k % 2], params[:, mu + t:mu + t + 1], raw[:, k, 1:],
                                               ALU.mult, ALU.add).then_inc(S["mixed"], 1)

        @block.tensor
        def _(pe):
            pe.wait_ge(S["v1_loaded"], 16)
            for k in range(KT):
                pe.wait_ge(S["mixed"], 4 + k)
                last = nc.tensor.matmul(vlow[32:64, :], v1s[:, k, :], mix[:, 3 + k], start=k == 0, stop=k == KT - 1)
            last.then_inc(S["vlow_done"], 1)
    end_phase(nc, S)


def rwkv_memory(nc, mem, mixed_lo):
    sb = lambda name, shape: mem.enter_context(nc.sbuf_tensor("r_" + name, shape, F32))
    line, chunked = [P, T], [P, NC, CH]
    sets = []
    for x in range(2):
        of = lambda name, shape, x=x: sb(f"{name}{x}", shape)
        sets.append(dict(
            ar=of("ar", [P, NC, 2, CH]), bonus=of("bonus", line), g=of("g", line), scm=of("scm", [P, 2, NC, P]), q=of("q", chunked),
            tri=of("tri", chunked), trit=of("trit", chunked), bkt=of("bkt", [P, NC, P]), uv=of("uv", [P, NC, 2, CH]),
            at=of("at", chunked), end=of("end", [P, NC]), pack=of("pack", [P, PACK_COLS])))
    prep = {name: sb(name, line) for name in "r kx sw a cs lp eout kk rn am".split()}
    prep.update(raw=sb("raw", [P, 2, T + 1]), vin=sb("vin", [P, 2, T]), v=sb("v", [P, CH + T]), bk=sb("bk", [P, NC, 2, CH]), bke=sb("bke", [P, NC, 2, CH]))
    chain = dict(left=sb("left", chunked), level=sb("level", [P, 2, NC, CH]), w1=sb("w1", chunked), ta=sb("ta", chunked),
                 state=sb("state", [P, NC + 1, CH]), y=sb("y", line), ln=sb("ln", [P, 2]))
    spare = mixed_lo[:, RWKV_TILES:RWKV_TILES + 8].rearrange("p a t -> p (a t)").bitcast(F32).rearrange("p (n t) -> p n t", n=4)
    chain.update(yc=spare[:, 0], ysq=spare[:, 1], y_bonus=spare[:, 2], y_gate=spare[:, 3])
    return sets, prep, chain, mem.enter_context(nc.psum_tensor("r_psum", [P, 8, T], F32))


def rwkv_phase(nc, bufs, phase, l, hp_prep, hp_chain, hp_norm, parity, lora, dram, memory, mixed_hi, mixed_lo):
    consts = bufs["consts"]
    projected, v_mixed, pair_pack = dram["projected"], dram["v_mixed"], dram["pair_pack"]
    low_wa, low_g, low_gv = lora
    con = lambda name, n: consts[:, CONSTS[name]:CONSTS[name] + n]
    ident, head_ones, head_mean = con("ident", P), con("head_ones", P), con("head_mean", P)
    S = phase_sems(nc, phase, "zeroed pad_zeroed r_loaded k_loaded v_loaded v_first_loaded pack_loaded r_diff r_mix k_diff k_mix "
                       "gates_psum sigmoid_w a_ready sigmoid_v g_ready v_diff v_scaled v_ready log_decay decay_sum "
                       "decay_before exp_in exp_out exp_before kk_scaled kk_squared kk_norm kk_log kk_inverse kk_ready "
                       "a_less_one k_ready b_ready ar_ready bk_ready bk_end ends_ready rk bonus_sum bonus_ready scores_psum "
                       "scores_masked n_psum n_masked tri_start q_psum q_copied q_first trit_start bkt_psum bkt_copied vt_psum "
                       "vt_copied at_psum at_copied level_ready left_psum left_copied tri_psum trit_psum tri_joined trit_joined "
                       "w1_psum w1_copied ta_psum ta_copied state_zero u_psum u_copied state_psum state_ready y_psum y_copied "
                       "y_mean y_centered y_squared y_variance y_log y_inverse y_scaled y_bonus y_gated high_done low_done "
                       "kept")
    sets, tmp, work, ps = memory
    new, old = sets[parity], sets[1 - parity]
    half = lambda t, h: t[64 * h:64 * h + 64]
    cols = lambda pack: (lambda c: pack[:, c:c + 1])
    p_new, p_old = cols(new["pack"]), cols(old["pack"])
    chunks = lambda x: x.rearrange("p (c t) -> p c t", c=NC)
    flat = lambda x: x.rearrange("p c n -> p (c n)")
    line = lambda x: x.rearrange("p a t -> p (a t)")
    raw, vin, bk, bke, ar = tmp["raw"], tmp["vin"], tmp["bk"], tmp["bke"], new["ar"]
    r, kx, sw, a, cs, lp, eout, kk, rn, am = (tmp[n] for n in "r kx sw a cs lp eout kk rn am".split())
    v = tmp["v"][:, CH:]
    k, b, sv, ein, ebef, kksq, rk = kx, a, v, cs, lp, rn, am
    left, levels, w1, ta, state = (work[n] for n in ("left", "level", "w1", "ta", "state"))
    y, yc, ysq, y_bonus, y_gate, ln = (work[n] for n in "y yc ysq y_bonus y_gate ln".split())
    prepares, chains, norms = (hp is not None for hp in (hp_prep, hp_chain, hp_norm))

    def take_turns(norm, prep, join, form, chunk, finish):
        parts = iter(range(64))
        def prepare():
            n = next(parts)
            if norms:
                norm(n)
            if prepares and n < PREP_PARTS:
                prep(n)
        for s in range(1, 6):
            for second in range(2):
                if chains:
                    join(s, second)
                prepare()
        for n in range(2):
            if chains:
                form(n)
            prepare()
        for c in range(NC):
            if chains:
                chunk(c, False)
            prepare()
            if chains:
                chunk(c, True)
        for n in range(3):
            if chains:
                finish(n)
            prepare()

    with nc.Block() as block:
        @block.sync
        def _(sp):
            if prepares:
                sp.dma_start(raw[:, 1, 1:], projected[K0 + hp_prep]).then_inc(S["k_loaded"], 16)
                sp.dma_start(raw[:, 0, 1:], projected[R0 + hp_prep]).then_inc(S["r_loaded"], 16)
                sp.dma_start(vin[:, 0], v_mixed[l * KT + hp_prep]).then_inc(S["v_loaded"], 16)
                sp.dma_start(new["pack"][:], pair_pack[l * RWKV_TILES + hp_prep]).then_inc(S["pack_loaded"], 16)
                sp.dma_start(vin[:, 1], v_mixed[hp_prep]).then_inc(S["v_first_loaded"], 16)

        @block.scalar
        def _(act):
            A = nc.scalar.activation

            def prep(n):
                if n == 0:
                    act.wait_ge(S["pack_loaded"], 16)
                    act.wait_ge(S["gates_psum"], 1)
                    A(sw[:], ps[:, 0], ACT.Sigmoid, bias=p_new(W0)).then_inc(S["sigmoid_w"], 1)
                    act.wait_ge(S["gates_psum"], 2)
                    A(a[:], ps[:, 1], ACT.Sigmoid, bias=p_new(A0)).then_inc(S["a_ready"], 1)
                elif n == 1:
                    act.wait_ge(S["gates_psum"], 4)
                    A(sv[:], ps[:, 3], ACT.Sigmoid, bias=p_new(V0P)).then_inc(S["sigmoid_v"], 1)
                    A(new["g"][:], ps[:, 2], ACT.Copy).then_inc(S["g_ready"], 1)
                elif n == 2:
                    act.wait_ge(S["kk_scaled"], 1)
                    A(kksq[:], kk[:], ACT.Square).then_inc(S["kk_squared"], 1)
                    act.wait_ge(S["kk_norm"], 1)
                    A(rn[:], ps[:, 4], ACT.Ln, bias=con("eps", 3)[:, 2:3]).then_inc(S["kk_log"], 1)
                elif n == 3:
                    act.wait_ge(S["kk_log"], 1)
                    A(rn[:], rn[:], ACT.Exp, scale=-0.5).then_inc(S["kk_inverse"], 1)
                    act.wait_ge(S["decay_sum"], 1)
                    A(eout[:], cs[:], ACT.Exp, scale=-1.0).then_inc(S["exp_out"], 1)
                    act.wait_ge(S["decay_before"], 1)
                    A(ein[:], cs[:], ACT.Exp).then_inc(S["exp_in"], 1)
                    A(ebef[:], lp[:], ACT.Exp).then_inc(S["exp_before"], 1)
                elif n == 8:
                    act.wait_ge(S["q_psum"], 1)
                    A(flat(new["q"][:]), ps[:, 3], ACT.Copy).then_inc(S["q_copied"], 1)
                elif n == 21:
                    act.wait_ge(S["at_psum"], 1)
                    A(flat(new["at"][:]), ps[:, 0], ACT.Copy).then_inc(S["at_copied"], 1)
                elif n == 17:
                    act.wait_ge(S["bkt_psum"], 1)
                    A(flat(new["bkt"][:]), ps[:, 1:3].rearrange("p b n -> p (b n)"), ACT.Copy).then_inc(S["bkt_copied"], 1)
                elif n == 18:
                    act.wait_ge(S["vt_psum"], 1)
                    A(new["uv"][64:128].rearrange("p c h n -> p (c h n)"), ps[64:128, 3:5].rearrange("p b n -> p (b n)"),
                      ACT.Copy).then_inc(S["vt_copied"], 1)

            def join(s, second):
                if not second:
                    act.wait_ge(S["left_psum"], s)
                    A(flat(left[:]), ps[:, 5], ACT.Copy).then_inc(S["left_copied"], 1)

            def form(n):
                if n == 0:
                    act.wait_ge(S["w1_psum"], 1)
                    A(flat(w1[:]), ps[:, 5], ACT.Copy).then_inc(S["w1_copied"], 1)
                else:
                    act.wait_ge(S["ta_psum"], 1)
                    A(flat(ta[:]), ps[:, 6], ACT.Copy).then_inc(S["ta_copied"], 1)

            def finish(n):
                if n == 0:
                    act.wait_ge(S["y_psum"], 1)
                    A(y[:], ps[:, 5], ACT.Copy).then_inc(S["y_copied"], 1)

            def norm(n):
                if n == 0:
                    A(ysq, yc, ACT.Square).then_inc(S["y_squared"], 1)
                elif n == 2:
                    act.wait_ge(S["y_variance"], 1)
                    A(ysq, ps[:, 4], ACT.Ln, bias=con("eps", 3)[:, 1:2]).then_inc(S["y_log"], 1)
                elif n == 3:
                    act.wait_ge(S["y_log"], 1)
                    A(ysq, ysq, ACT.Exp, scale=-0.5).then_inc(S["y_inverse"], 1)
                elif n == 5:
                    act.wait_ge(S["y_gated"], 1)
                    A(line(mixed_hi[:, ds(hp_norm, 1)]), yc, ACT.Copy).then_inc(S["high_done"], 1)

            take_turns(norm, prep, join, form, lambda c, second: None, finish)

        @block.gpsimd
        def _(pool):
            if prepares:
                nc.gpsimd.memset(raw[:, :, 0:1], 0.0).then_inc(S["zeroed"], 1)
                nc.gpsimd.memset(tmp["v"][:, 0:CH], 0.0).then_inc(S["pad_zeroed"], 1)
            def mask_level(q, s):
                at = CONSTS["levels_q"] + CH * s
                return nc.gpsimd.tensor_tensor(levels[:, s % 2], q[:], consts[:, at:at + CH].unsqueeze(1).broadcast_to([P, NC, CH]), ALU.mult)

            if chains:
                nc.gpsimd.memset(state[:, 0], 0.0).then_inc(S["state_zero"], 1)
                for s in range(2, 6):
                    if s > 2:
                        pool.wait_ge(S["left_psum"], s - 2)
                    mask_level(old["q"], s).then_inc(S["level_ready"], 1)
                pool.wait_ge(S["left_psum"], 5)
                if norms:
                    pool.wait_ge(S["y_gated"], 1)
                nc.gpsimd.tensor_copy(y_bonus, old["bonus"][:]).then_inc(S["kept"], 1)
                nc.gpsimd.tensor_copy(y_gate, old["g"][:]).then_inc(S["kept"], 1)
                nc.gpsimd.tensor_copy(ln[:], old["pack"][:, LN_W:LN_W + 2]).then_inc(S["kept"], 1)
            if prepares:
                pool.wait_ge(S["q_copied"], 1)
                mask_level(new["q"], 1).then_inc(S["level_ready"], 1)

        @block.vector
        def _(dve):
            V = nc.vector
            level = lambda n, w=CH: consts[:, n:n + w].unsqueeze(1).broadcast_to([P, NC, w])

            def mask_scores(n):
                dve.wait_ge(S["scores_psum"], n % 2 + 1)
                mask = con("scores", P).unsqueeze(1).broadcast_to([P, 4, P])
                V.tensor_tensor(new["scm"][:, n // 2, 4 * (n % 2):4 * (n % 2) + 4], ps[:, n].rearrange("p (x q) -> p x q", x=4),
                                mask, ALU.mult).then_inc(S["scores_masked"], 1)

            def prep(n):
                if n == 0:
                    dve.wait_ge(S["zeroed"], 1)
                    dve.wait_ge(S["k_loaded"], 16)
                    V.tensor_tensor(kx[:], raw[:, 1, 0:T], raw[:, 1, 1:], ALU.subtract).then_inc(S["k_diff"], 1)
                    dve.wait_ge(S["pack_loaded"], 16)
                    dve.wait_ge(S["k_diff"], 1)
                    V.scalar_tensor_tensor(kx[:], kx[:], p_new(MU_K), raw[:, 1, 1:], ALU.mult, ALU.add).then_inc(S["k_mix"], 1)
                    dve.wait_ge(S["k_mix"], 1)
                    V.tensor_scalar(kk[:], kx[:], p_new(K_K), None, ALU.mult).then_inc(S["kk_scaled"], 1)
                elif n == 1:
                    dve.wait_ge(S["sigmoid_w"], 1)
                    V.tensor_scalar(sw[:], sw[:], -DECAY_SCALE, None, ALU.mult).then_inc(S["log_decay"], 1)
                    dve.wait_ge(S["log_decay"], 1)
                    V.tensor_tensor_scan(cs[:], con("chunk_start", T), sw[:], 0.0, ALU.mult, ALU.add).then_inc(S["decay_sum"], 1)
                    dve.wait_ge(S["decay_sum"], 1)
                    V.tensor_tensor(lp[:], cs[:], sw[:], ALU.subtract).then_inc(S["decay_before"], 1)
                elif n == 2:
                    dve.wait_ge(S["r_loaded"], 16)
                    V.tensor_tensor(r[:], raw[:, 0, 0:T], raw[:, 0, 1:], ALU.subtract).then_inc(S["r_diff"], 1)
                    dve.wait_ge(S["a_ready"], 1)
                    V.tensor_scalar(am[:], a[:], -1.0, p_new(K_A), ALU.add, ALU.mult).then_inc(S["a_less_one"], 1)
                    dve.wait_ge(S["r_diff"], 1)
                    V.scalar_tensor_tensor(r[:], r[:], p_new(MU_R), raw[:, 0, 1:], ALU.mult, ALU.add).then_inc(S["r_mix"], 1)
                    dve.wait_ge(S["a_less_one"], 1)
                    V.scalar_tensor_tensor(k[:], am[:], 1.0, kx[:], ALU.add, ALU.mult).then_inc(S["k_ready"], 1)
                elif n == 3:
                    dve.wait_ge(S["v_loaded"], 16)
                    dve.wait_ge(S["v_first_loaded"], 16)
                    V.tensor_tensor(vin[:, 1], vin[:, 1], vin[:, 0], ALU.subtract).then_inc(S["v_diff"], 1)
                    dve.wait_ge(S["sigmoid_v"], 1)
                    dve.wait_ge(S["v_diff"], 1)
                    V.tensor_tensor(sv[:], vin[:, 1], sv[:], ALU.mult).then_inc(S["v_scaled"], 1)
                    dve.wait_ge(S["v_scaled"], 1)
                    V.tensor_tensor(v[:], sv[:], vin[:, 0], ALU.add).then_inc(S["v_ready"], 1)
                elif n == 4:
                    dve.wait_ge(S["kk_inverse"], 1)
                    V.tensor_tensor(kk[:], kk[:], rn[:], ALU.mult).then_inc(S["kk_ready"], 1)
                    dve.wait_ge(S["exp_in"], 1)
                    V.tensor_copy(new["end"][:], chunks(ein[:])[:, :, CH - 1]).then_inc(S["ends_ready"], 1)
                    dve.wait_ge(S["kk_ready"], 1)
                    V.tensor_tensor(b[:], kk[:], a[:], ALU.mult).then_inc(S["b_ready"], 1)
                    dve.wait_ge(S["exp_before"], 1)
                    V.scalar_tensor_tensor(ar[:, :, 0], chunks(kk[:]), -1.0, chunks(ebef[:]), ALU.mult, ALU.mult).then_inc(S["ar_ready"], 1)
                    dve.wait_ge(S["exp_out"], 1)
                    dve.wait_ge(S["b_ready"], 1)
                    V.tensor_tensor(bk[:, :, 0], chunks(b[:]), chunks(eout[:]), ALU.mult).then_inc(S["bk_ready"], 1)
                elif n == 5:
                    dve.wait_ge(S["k_ready"], 1)
                    V.tensor_tensor(bk[:, :, 1], chunks(k[:]), chunks(eout[:]), ALU.mult).then_inc(S["bk_ready"], 1)
                    dve.wait_ge(S["r_mix"], 1)
                    V.tensor_tensor(ar[:, :, 1], chunks(r[:]), chunks(ein[:]), ALU.mult).then_inc(S["ar_ready"], 1)
                    V.scalar_tensor_tensor(rk[:], r[:], p_new(R_K), k[:], ALU.mult, ALU.mult).then_inc(S["rk"], 1)
                elif n == 6:
                    dve.wait_ge(S["n_psum"], 1)
                    V.tensor_tensor(new["tri"][:], ps[:, 4].rearrange("p (c t) -> p c t", c=NC), level(CONSTS["level0_n"]), ALU.mult).then_inc(S["n_masked"], 1)
                    dve.wait_ge(S["n_masked"], 1)
                    V.tensor_tensor(new["tri"][:], new["tri"][:], level(CONSTS["eye64"]), ALU.add).then_inc(S["tri_start"], 1)
                elif n == 7:
                    dve.wait_ge(S["bk_ready"], 2)
                    dve.wait_ge(S["ends_ready"], 1)
                    V.tensor_tensor(bke[:], bk[:], new["end"][:].unsqueeze(2).unsqueeze(3).broadcast_to([P, NC, 2, CH]), ALU.mult).then_inc(S["bk_end"], 1)
                elif n == 9:
                    dve.wait_ge(S["q_copied"], 1)
                    V.tensor_tensor(new["trit"][:], new["q"][:], level(CONSTS["levels_q"]), ALU.mult).then_inc(S["q_first"], 1)
                    dve.wait_ge(S["q_first"], 1)
                    V.tensor_tensor(new["trit"][:], new["trit"][:], level(CONSTS["eye64"]), ALU.add).then_inc(S["trit_start"], 1)
                elif n in (13, 15):
                    mask_scores((n - 13) // 2)
                    mask_scores((n - 13) // 2 + 2)
                elif n == 20:
                    dve.wait_ge(S["v_ready"], 1)
                    dve.wait_ge(S["bonus_sum"], 1)
                    V.tensor_tensor(new["bonus"][:], ps[:, 4], v[:], ALU.mult).then_inc(S["bonus_ready"], 1)

            def join(s, second):
                if second:
                    if s < 5:
                        dve.wait_ge(S["tri_psum"], s)
                        if s > 1:
                            dve.wait_ge(S["tri_joined"], s - 1)
                        V.tensor_tensor(old["tri"][:], old["tri"][:], ps[:, 6].rearrange("p (c t) -> p c t", c=NC), ALU.add).then_inc(S["tri_joined"], 1)
                    dve.wait_ge(S["trit_psum"], s)
                    if s > 1:
                        dve.wait_ge(S["trit_joined"], s - 1)
                    V.tensor_tensor(old["trit"][:], old["trit"][:], ps[:, 7].rearrange("p (c t) -> p c t", c=NC), ALU.add).then_inc(S["trit_joined"], 1)

            def chunk(c, second):
                if not second:
                    dve.wait_ge(S["u_psum"], c + 1)
                    V.tensor_copy(old["uv"][0:64, c], ps[0:64, 5:7, 0:CH]).then_inc(S["u_copied"], 1)
                    return
                dve.wait_ge(S["state_psum"], c + 1)
                if c:
                    dve.wait_ge(S["state_ready"], c)
                else:
                    dve.wait_ge(S["state_zero"], 1)
                if c < NC - 1:
                    V.scalar_tensor_tensor(state[:, c + 1], state[:, c], old["end"][:, c:c + 1], ps[:, 7, 0:CH],
                                           ALU.mult, ALU.add).then_inc(S["state_ready"], 1)

            def finish(n):
                if n == 1:
                    dve.wait_ge(S["y_mean"], 1)
                    dve.wait_ge(S["y_copied"], 1)
                    if norms:
                        dve.wait_ge(S["low_done"], 1)
                    V.tensor_tensor(yc, y[:], ps[:, 6], ALU.subtract).then_inc(S["y_centered"], 1)

            def norm(n):
                if n == 4:
                    dve.wait_ge(S["y_inverse"], 1)
                    V.scalar_tensor_tensor(yc, yc, ln[:, 0:1], ysq, ALU.mult, ALU.mult).then_inc(S["y_scaled"], 1)
                    dve.wait_ge(S["y_scaled"], 1)
                    V.scalar_tensor_tensor(yc, yc, ln[:, 1:2], y_bonus, ALU.add, ALU.add).then_inc(S["y_bonus"], 1)
                    dve.wait_ge(S["y_bonus"], 1)
                    V.tensor_tensor(yc, yc, y_gate, ALU.mult).then_inc(S["y_gated"], 1)
                elif n == 6:
                    dve.wait_ge(S["high_done"], 1)
                    V.tensor_tensor(line(mixed_lo[:, ds(hp_norm, 1)]), yc, line(mixed_hi[:, ds(hp_norm, 1)]), ALU.subtract).then_inc(S["low_done"], 1)

            take_turns(norm, prep, join, lambda n: None, chunk, finish)

        @block.tensor
        def _(pe):
            mm = nc.tensor.matmul
            pack = new["pack"]

            def each(out, lhs, rhs):
                for c in range(NC):
                    for h in range(2):
                        last = mm(half(ps, h)[:, out, c * CH:(c + 1) * CH], lhs(c, h), rhs(c, h), start=True, stop=True)
                return last

            def score(n):
                for c in range(2 * n, 2 * n + 2):
                    for h in range(2):
                        last = mm(ps[:, 2 * h + c // 4, (c % 4) * P:(c % 4 + 1) * P], line(half(bk, h)[:, c]), line(half(ar, h)[:, c]), start=True, stop=True)
                if n % 2:
                    last.then_inc(S["scores_psum"], 1)

            def prep(n):
                if n == 0:
                    pe.wait_ge(S["pack_loaded"], 16)
                    mm(ps[:, 0], pack[0:64, 0:P], low_wa[0:64, :], start=True, stop=True).then_inc(S["gates_psum"], 1)
                    mm(ps[:, 1], pack[64:128, 0:P], low_wa[64:128, :], start=True, stop=True).then_inc(S["gates_psum"], 1)
                elif n == 1:
                    mm(ps[:, 3], pack[32:64, 2 * P:3 * P], low_gv[32:64, :], start=True, stop=True).then_inc(S["gates_psum"], 1)
                    mm(ps[:, 2], pack[:, P:2 * P], low_g[:], start=True, stop=False)
                    mm(ps[:, 2], pack[0:32, 2 * P:3 * P], low_gv[0:32, :], start=False, stop=True).then_inc(S["gates_psum"], 1)
                elif n == 2:
                    pe.wait_ge(S["kk_squared"], 1)
                    mm(ps[:, 4], head_ones, kksq[:], start=True, stop=True).then_inc(S["kk_norm"], 1)
                elif n == 6:
                    pe.wait_ge(S["ar_ready"], 1)
                    pe.wait_ge(S["bk_ready"], 1)
                    pe.wait_ge(S["kk_inverse"], 1)
                    each(4, lambda c, h: half(ar, h)[:, c, 0], lambda c, h: half(bk, h)[:, c, 0]).then_inc(S["n_psum"], 1)
                elif n == 8:
                    pe.wait_ge(S["sigmoid_v"], 1)
                    each(3, lambda c, h: half(bk, h)[:, c, 0], lambda c, h: half(ar, h)[:, c, 0]).then_inc(S["q_psum"], 1)
                elif 12 <= n < 16:
                    if n == 12:
                        pe.wait_ge(S["ar_ready"], 2)
                        pe.wait_ge(S["bk_ready"], 2)
                        pe.wait_ge(S["a_ready"], 1)
                        pe.wait_ge(S["g_ready"], 1)
                        pe.wait_ge(S["q_copied"], 1)
                    score(n - 12)
                elif n == 17:
                    pe.wait_ge(S["bk_end"], 1)
                    pe.wait_ge(S["scores_masked"], 4)
                    for c in range(NC):
                        last = nc.tensor.transpose(ps[:, 1 + c // 4, (c % 4) * P:(c % 4 + 1) * P], line(bke[:, c]), ident)
                    last.then_inc(S["bkt_psum"], 1)
                elif n == 18:
                    pe.wait_ge(S["v_ready"], 1)
                    pe.wait_ge(S["pad_zeroed"], 1)
                    pe.wait_ge(S["n_masked"], 1)
                    for c in range(NC):
                        last = nc.tensor.transpose(ps[:, 3 + c // 4, (c % 4) * P:(c % 4 + 1) * P], tmp["v"][:, c * CH:c * CH + P], ident)
                    last.then_inc(S["vt_psum"], 1)
                elif n == 19:
                    each(0, lambda c, h: half(ar, h)[:, c, 0], lambda c, h: half(ident, h)[:, 64 * h:64 * h + 64]).then_inc(S["at_psum"], 1)
                elif n == 20:
                    pe.wait_ge(S["rk"], 1)
                    pe.wait_ge(S["vt_copied"], 1)
                    mm(ps[:, 4], head_ones, rk[:], start=True, stop=True).then_inc(S["bonus_sum"], 1)

            def join(s, second):
                tri, trit = old["tri"], old["trit"]
                if not second:
                    if s > 1:
                        pe.wait_ge(S["level_ready"], s - 1)
                        pe.wait_ge(S["tri_joined"], s - 1)
                    each(5, lambda c, h: half(levels, h)[:, s % 2, c], lambda c, h: half(tri, h)[:, c]).then_inc(S["left_psum"], 1)
                else:
                    pe.wait_ge(S["left_copied"], s)
                    if s > 1:
                        pe.wait_ge(S["trit_joined"], s - 1)
                    if s < 5:
                        each(6, lambda c, h: half(trit, h)[:, c], lambda c, h: half(left, h)[:, c]).then_inc(S["tri_psum"], 1)
                    each(7, lambda c, h: half(left, h)[:, c], lambda c, h: half(trit, h)[:, c]).then_inc(S["trit_psum"], 1)

            def form(n):
                if n == 0:
                    each(5, lambda c, h: old["scm"][64:128, h, c, 0:CH], lambda c, h: old["uv"][64:128, c, h]).then_inc(S["w1_psum"], 1)
                else:
                    pe.wait_ge(S["tri_joined"], 4)
                    pe.wait_ge(S["trit_joined"], 5)
                    each(6, lambda c, h: half(old["at"], h)[:, c], lambda c, h: half(old["trit"], h)[:, c]).then_inc(S["ta_psum"], 1)

            def chunk(c, second):
                if second:
                    pe.wait_ge(S["u_copied"], c + 1)
                    for h in range(2):
                        last = mm(half(ps, h)[:, 7, 0:CH], old["bkt"][:, c, 64 * h:64 * h + 64], old["uv"][:, c, h], start=True, stop=True)
                    last.then_inc(S["state_psum"], 1)
                    return
                if c == 0:
                    pe.wait_ge(S["w1_copied"], 1)
                    pe.wait_ge(S["ta_copied"], 1)
                    pe.wait_ge(S["state_zero"], 1)
                for h in range(2):
                    mm(ps[0:64, 5 + h, 0:CH], half(old["trit"], h)[:, c], half(w1, h)[:, c], start=True, stop=False)
                if c:
                    pe.wait_ge(S["state_ready"], c)
                for h in range(2):
                    last = mm(ps[0:64, 5 + h, 0:CH], half(ta, h)[:, c], half(state, h)[:, c], start=False, stop=True)
                last.then_inc(S["u_psum"], 1)

            def finish(n):
                if n == 0:
                    for c in range(NC):
                        for h in range(2):
                            out = half(ps, h)[:, 5, c * CH:(c + 1) * CH]
                            mm(out, old["uv"][:, c, h], old["scm"][:, h, c, CH:P], start=True, stop=False)
                            last = mm(out, half(state, h)[:, c], half(old["ar"], h)[:, c, 1], start=False, stop=True)
                    last.then_inc(S["y_psum"], 1)
                elif n == 1:
                    pe.wait_ge(S["y_copied"], 1)
                    mm(ps[:, 6], head_mean, y[:], start=True, stop=True).then_inc(S["y_mean"], 1)

            def norm(n):
                if n == 0:
                    pe.wait_ge(S["y_squared"], 1)
                    mm(ps[:, 4], head_mean, ysq, start=True, stop=True).then_inc(S["y_variance"], 1)

            take_turns(norm, prep, join, form, chunk, finish)
    end_phase(nc, S)


PREP_PARTS = 23


def rwkv_pairs(nc, bufs, l, lora, dram, mixed_hi, mixed_lo):
    with ExitStack() as mem:
        memory = rwkv_memory(nc, mem, mixed_lo)

        def step(name, prepared, chained, normed, parity):
            rwkv_phase(nc, bufs, "rwkv_" + name, l, prepared, chained, normed, parity, lora, dram, memory, mixed_hi, mixed_lo)

        n = RWKV_TILES
        step("first", 0, None, None, 0)
        step("second", 1, 0, None, 1)
        with nc.Fori(0, (n - 2) // 2) as u:
            step("even", 2 * u + 2, 2 * u + 1, 2 * u, 0)
            step("odd", 2 * u + 3, 2 * u + 2, 2 * u + 1, 1)
        step("last", None, n - 1, n - 2, 0)
        step("end", None, None, n - 1, 1)


T_DT, T_NEG, T_EXP, T_END_DT, T_END = range(5)
G_CONV, G_BIAS, G_GAIN, G_D = 0, 24, 30, 34
GROUP_COLS = 38


def dt_phase(nc, bufs, l, dram, acs, table):
    consts, params = bufs["consts"], bufs["params"]
    projected = dram["projected"]
    S = phase_sems(nc, "dt", "loaded biased negative exponent one_plus less_one is_zero log_ready log_masked den_masked "
                       "inverse ratio log1p dt_ready rate_ready decay acs_ready diagonal transposed tables_ready "
                       "end_diff end_exp")
    R = slice(32, 64)
    with nc.sbuf_tensor("d_t", [P, 14, T], F32) as t, nc.sbuf_tensor("d_diag", [P, SNC, 32], F32) as diag, \
            nc.sbuf_tensor("d_rate", [P, 1], F32) as rate, nc.sbuf_tensor("d_end", [P, SNC, 32], F32) as end_diff, \
            nc.psum_tensor("d_ps", [P, 3, SNC, 32], F32) as ps, nc.Block() as block:
        raw, x, neg, e, u, less, zero, logu, num, den, inv, ratio, lp, dt = (t[R, n] for n in range(14))
        bias = params[R, PARAMS["dt_bias"]:PARAMS["dt_bias"] + 1]
        a_log = params[R, PARAMS["A_log"]:PARAMS["A_log"] + 1]
        ident = consts[:, CONSTS["ident"]:CONSTS["ident"] + P]
        heads = lambda n: table[:, :, n].rearrange("p g c h -> p c g h")
        psum = lambda n: ps[:, n].rearrange("p c (g h) -> p c g h", g=SSD_GROUPS)

        @block.sync
        def _(sp):
            sp.dma_start(raw, projected[GDT, 32:64]).then_inc(S["loaded"], 16)

        @block.scalar
        def _(act):
            nc.scalar.activation(rate[R], a_log, ACT.Exp).then_inc(S["rate_ready"], 1)
            act.wait_ge(S["negative"], 1)
            nc.scalar.activation(e, neg, ACT.Exp).then_inc(S["exponent"], 1)
            act.wait_ge(S["one_plus"], 1)
            nc.scalar.activation(logu, u, ACT.Ln).then_inc(S["log_ready"], 1)
            act.wait_ge(S["transposed"], 1)
            nc.scalar.activation(heads(T_DT), psum(0), ACT.Copy).then_inc(S["tables_ready"], 1)
            nc.scalar.activation(heads(T_NEG), psum(1), ACT.Copy, scale=-1.0).then_inc(S["tables_ready"], 1)
            nc.scalar.activation(heads(T_EXP), psum(1), ACT.Exp).then_inc(S["tables_ready"], 1)
            nc.scalar.activation(heads(T_END), psum(2), ACT.Exp).then_inc(S["tables_ready"], 1)
            act.wait_ge(S["end_diff"], 1)
            nc.scalar.activation(end_diff[:], end_diff[:], ACT.Exp).then_inc(S["end_exp"], 1)

        @block.vector
        def _(dve):
            V = nc.vector
            dve.wait_ge(S["loaded"], 16)
            V.tensor_scalar(x, raw, bias, None, ALU.add).then_inc(S["biased"], 1)
            dve.wait_ge(S["biased"], 1)
            V.scalar_tensor_tensor(neg, x, -1.0, x, ALU.mult, ALU.min).then_inc(S["negative"], 1)
            dve.wait_ge(S["exponent"], 1)
            V.tensor_scalar(u, e, 1.0, None, ALU.add).then_inc(S["one_plus"], 1)
            dve.wait_ge(S["one_plus"], 1)
            V.tensor_scalar(less, u, -1.0, None, ALU.add).then_inc(S["less_one"], 1)
            dve.wait_ge(S["less_one"], 1)
            V.tensor_scalar(zero, less, 0.0, None, ALU.is_equal).then_inc(S["is_zero"], 1)
            dve.wait_ge(S["is_zero"], 1)
            V.tensor_tensor(den, less, zero, ALU.add).then_inc(S["den_masked"], 1)
            dve.wait_ge(S["den_masked"], 1)
            V.reciprocal(inv, den).then_inc(S["inverse"], 1)
            dve.wait_ge(S["log_ready"], 1)
            V.tensor_tensor(num, logu, zero, ALU.add).then_inc(S["log_masked"], 1)
            dve.wait_ge(S["log_masked"], 1)
            dve.wait_ge(S["inverse"], 1)
            V.tensor_tensor(ratio, num, inv, ALU.mult).then_inc(S["ratio"], 1)
            dve.wait_ge(S["ratio"], 1)
            V.tensor_tensor(lp, ratio, e, ALU.mult).then_inc(S["log1p"], 1)
            dve.wait_ge(S["log1p"], 1)
            V.scalar_tensor_tensor(dt, x, 0.0, lp, ALU.max, ALU.add).then_inc(S["dt_ready"], 1)
            dve.wait_ge(S["dt_ready"], 1)
            dve.wait_ge(S["rate_ready"], 1)
            V.tensor_scalar(raw, dt, rate[R], -1.0, ALU.mult, ALU.mult).then_inc(S["decay"], 1)
            dve.wait_ge(S["decay"], 1)
            V.tensor_tensor_scan(acs[R], consts[R, CONSTS["ssd_start"]:CONSTS["ssd_start"] + T], raw, 0.0, ALU.mult, ALU.add).then_inc(S["acs_ready"], 1)
            dve.wait_ge(S["acs_ready"], 1)
            for c in range(SNC):
                V.tensor_scalar(diag[R, c], ident[R, 32:64], acs[R, (c + 1) * SCH - 1:(c + 1) * SCH], float(D), ALU.mult, ALU.mult).then_inc(S["diagonal"], 1)
            dve.wait_ge(S["transposed"], 1)
            dve.wait_ge(S["tables_ready"], 4)
            V.tensor_tensor(end_diff[:].rearrange("p c (g h) -> p c g h", g=SSD_GROUPS), psum(2), heads(T_NEG), ALU.add).then_inc(S["end_diff"], 1)
            dve.wait_ge(S["end_exp"], 1)
            V.tensor_tensor(heads(T_END_DT), end_diff[:].rearrange("p c (g h) -> p c g h", g=SSD_GROUPS), heads(T_DT), ALU.mult).then_inc(S["tables_ready"], 1)

        @block.tensor
        def _(pe):
            mean = consts[:, CONSTS["mean"]:CONSTS["mean"] + P]
            pe.wait_ge(S["diagonal"], SNC)
            for c in range(SNC):
                cut = slice(c * SCH, (c + 1) * SCH)
                nc.tensor.matmul(ps[:, 0, c], dt[:, cut], ident[R, 32:64], start=True, stop=True)
                nc.tensor.matmul(ps[:, 1, c], acs[R, cut], ident[R, 32:64], start=True, stop=True)
                last = nc.tensor.matmul(ps[:, 2, c], mean[R, :], diag[R, c], start=True, stop=True)
            last.then_inc(S["transposed"], 1)
    end_phase(nc, S)


POOL_TILE = 3


def ssd_group_phase(nc, bufs, l, g, dram, acs, table, mixed_hi, mixed_lo):
    consts = bufs["consts"]
    projected = dram["projected"]
    con = lambda name, n: consts[:, CONSTS[name]:CONSTS[name] + n]
    ident, mean, mask = con("ident", P), con("mean", P), con("ssd_mask", P)
    GH, W = GROUP_HEADS, GROUP_HEADS * 64
    S = phase_sems(nc, "ssd_group", "zeroed state_zero pack_loaded raw_loaded*6 z_loaded select_loaded tab_ready tapped conv_done tap_ready pool_tapped pool_done "
                       "silu_ready z_ready cb_psum cb_ready xt_psum xt_read bt_psum bt_ready seg_psum seg_bounded seg_exp scored "
                       "diag_psum off_psum off_scaled y_ready state_psum state_decayed state_ready back_psum "
                       "skipped gated squared norm_psum log_ready inverse_ready normed high_done low_done")
    sb = lambda name, shape, dt=F32: nc.sbuf_tensor("s_" + name, shape, dt)
    with ExitStack() as mem:
        raw = mem.enter_context(sb("raw", [P, 6, T + 3]))
        pack = mem.enter_context(sb("pack", [P, GROUP_COLS]))
        sel = mem.enter_context(sb("sel", [P, GH, P]))
        x = mem.enter_context(sb("x", [P, 6, T]))
        z = mem.enter_context(sb("z", [P, 4, T]))
        tab = mem.enter_context(sb("tab", [P, 5, SNC, GH]))
        cb = mem.enter_context(sb("cb", [P, SNC, SCH]))
        xdt = mem.enter_context(sb("xdt", [P, SNC, W]))
        xw = mem.enter_context(sb("xw", [P, SNC, W]))
        bt = mem.enter_context(sb("bt", [P, SNC, P]))
        e = mem.enter_context(sb("e", [P, 2, SNC, SCH]))
        m = mem.enter_context(sb("m", [P, 2, SNC, SCH]))
        state = mem.enter_context(sb("state", [P, SNC, W]))
        off = mem.enter_context(sb("off", [P, 2, W]))
        taps = mem.enter_context(sb("taps", [P, 3, T]))
        ytok = mem.enter_context(sb("ytok", [P, SNC, W]))
        y = mem.enter_context(sb("y", [P, 4, T]))
        sq = mem.enter_context(sb("sq", [P, 2, T]))
        inverse = mem.enter_context(sb("inverse", [P, T]))
        ps = mem.enter_context(nc.psum_tensor("s_psum", [P, 8, T], F32))
        block = mem.enter_context(nc.Block())
        p1 = lambda c: pack[:, c:c + 1]
        per_head = lambda n, c: tab[:, n, c].unsqueeze(2).broadcast_to([P, GH, 64])
        by_head = lambda a: a.rearrange("p (h n) -> p h n", h=GH)
        seg_bank = lambda h: (4, 5, 7)[h % 3]
        state_bank, off_bank = (6, 7, 4), (None, 5, 6, 7)
        tiles = lambda n: [X0 + 4 * g + n] if n < 4 else [B0 + g] if n == 4 else [C0 + g]

        @block.sync
        def _(sp):
            for n in (4, POOL_TILE, 5, 0, 1, 2):
                sp.dma_start(raw[:, n, 3:], projected[tiles(n)[0]]).then_inc(S["raw_loaded"][n], 16)

        @block.scalar
        def _(act):
            act.dma_start(pack[:], dram["group_pack"][l * SSD_GROUPS + g]).then_inc(S["pack_loaded"], 16)
            act.dma_start(sel[32:64].rearrange("p h n -> p (h n)"), dram["select"][g]).then_inc(S["select_loaded"], 16)
            for n in range(4):
                act.dma_start(z[:, n], projected[Z0 + 4 * g + n]).then_inc(S["z_loaded"], 16)
            for i, n in enumerate((4, 5, 0, 1, 2, 3)):
                if n == POOL_TILE:
                    act.wait_ge(S["pool_done"], 1)
                else:
                    act.wait_ge(S["conv_done"], i + 1)
                nc.scalar.activation(x[:, n], x[:, n], ACT.Silu).then_inc(S["silu_ready"], 1)
            act.wait_ge(S["z_loaded"], 64)
            for n in range(4):
                nc.scalar.activation(z[:, n], z[:, n], ACT.Silu).then_inc(S["z_ready"], 1)
            act.wait_ge(S["bt_psum"], 1)
            nc.scalar.activation(bt[:].rearrange("p c n -> p (c n)"), ps[:, 7], ACT.Copy).then_inc(S["bt_ready"], 1)
            for h in range(GH):
                act.wait_ge(S["seg_bounded"], SNC * (h + 1))
                nc.scalar.activation(e[:, h % 2], e[:, h % 2], ACT.Exp).then_inc(S["seg_exp"], 1)
            for n in range(4):
                act.wait_ge(S["gated"], n + 1)
                if n >= 2:
                    act.wait_ge(S["norm_psum"], n - 1)
                nc.scalar.activation(sq[:, n % 2], y[:, n], ACT.Square).then_inc(S["squared"], 1)
            act.wait_ge(S["norm_psum"], 4)
            nc.scalar.activation(inverse[:], ps[:, 7], ACT.Ln, scale=float(D) / W, bias=con("eps", 3)[:, 0:1]).then_inc(S["log_ready"], 1)
            act.wait_ge(S["log_ready"], 1)
            nc.scalar.activation(inverse[:], inverse[:], ACT.Exp, scale=-0.5).then_inc(S["inverse_ready"], 1)
            for n in range(4):
                act.wait_ge(S["normed"], n + 1)
                nc.scalar.activation(mixed_hi[:, ds(8 + 4 * g + n, 1)].rearrange("p a t -> p (a t)"), ytok[:, n], ACT.Copy).then_inc(S["high_done"], 1)

        @block.gpsimd
        def _(pool):
            nc.gpsimd.memset(raw[:, :, 0:3], 0.0).then_inc(S["zeroed"], 1)
            nc.gpsimd.memset(state[:, 0], 0.0).then_inc(S["state_zero"], 1)
            n = POOL_TILE
            pool.wait_ge(S["zeroed"], 1)
            pool.wait_ge(S["pack_loaded"], 16)
            pool.wait_ge(S["raw_loaded"][n], 16)
            nc.gpsimd.tensor_scalar(x[:, n], raw[:, n, 0:T], p1(G_CONV + 4 * n), p1(G_BIAS + n), ALU.mult, ALU.add).then_inc(S["pool_tapped"], 1)
            for j in range(1, 4):
                nc.gpsimd.tensor_scalar(taps[:, j - 1], raw[:, n, j:j + T], p1(G_CONV + 4 * n + j), None, ALU.mult).then_inc(S["tap_ready"], 1)
            for j in range(1, 4):
                pool.wait_ge(S["tap_ready"], j)
                pool.wait_ge(S["pool_tapped"], j)
                nc.gpsimd.tensor_tensor(x[:, n], taps[:, j - 1], x[:, n], ALU.add).then_inc(S["pool_tapped"] if j < 3 else S["pool_done"], 1)

        @block.vector
        def _(dve):
            V = nc.vector
            V.tensor_copy(tab[:].rearrange("p k c h -> p (k c h)"), table[:, ds(g, 1)].rearrange("p a k c h -> p (a k c h)")).then_inc(S["tab_ready"], 1)
            dve.wait_ge(S["zeroed"], 1)
            dve.wait_ge(S["pack_loaded"], 16)
            done = 0
            for n in (4, 5, 0, 1, 2):
                dve.wait_ge(S["raw_loaded"][n], 16)
                V.tensor_scalar(x[:, n], raw[:, n, 0:T], p1(G_CONV + 4 * n), p1(G_BIAS + n), ALU.mult, ALU.add).then_inc(S["tapped"], 1)
                for j in range(1, 4):
                    done += 1
                    dve.wait_ge(S["tapped"], done)
                    V.scalar_tensor_tensor(x[:, n], raw[:, n, j:j + T], p1(G_CONV + 4 * n + j), x[:, n], ALU.mult, ALU.add).then_inc(
                        S["tapped"] if j < 3 else S["conv_done"], 1)
            dve.wait_ge(S["tab_ready"], 1)
            for c in range(SNC):
                dve.wait_ge(S["xt_psum"], c + 1)
                V.tensor_tensor(by_head(xdt[:, c]), by_head(ps[:, c]), per_head(T_DT, c), ALU.mult).then_inc(S["xt_read"], 1)
                V.tensor_tensor(by_head(xw[:, c]), by_head(ps[:, c]), per_head(T_END_DT, c), ALU.mult).then_inc(S["xt_read"], 1)
            dve.wait_ge(S["cb_psum"], 1)
            V.tensor_tensor(cb[:], ps[:, 6].rearrange("p (c t) -> p c t", c=SNC), mask.unsqueeze(1).broadcast_to([P, SNC, SCH]), ALU.mult).then_inc(S["cb_ready"], 1)
            dve.wait_ge(S["cb_ready"], 1)

            def bound(h):
                dve.wait_ge(S["seg_psum"], h + 1)
                if h >= 2:
                    dve.wait_ge(S["scored"], h - 1)
                for c in range(SNC):
                    V.tensor_scalar(e[:, h % 2, c], ps[:, seg_bank(h), c * SCH:(c + 1) * SCH], tab[:, T_NEG, c, h:h + 1], 0.0,
                                    ALU.add, ALU.min).then_inc(S["seg_bounded"], 1)

            bound(0)
            for h in range(GH):
                if h + 1 < GH:
                    bound(h + 1)
                dve.wait_ge(S["seg_exp"], h + 1)
                if h >= 2:
                    dve.wait_ge(S["diag_psum"], h - 1)
                V.tensor_tensor(m[:, h % 2], e[:, h % 2], cb[:], ALU.mult).then_inc(S["scored"], 1)
            dve.wait_ge(S["state_zero"], 1)
            for c in range(SNC - 1):
                if c:
                    dve.wait_ge(S["state_ready"], c)
                V.tensor_tensor(by_head(off[:, 0]), by_head(state[:, c]), per_head(T_END, c), ALU.mult).then_inc(S["state_decayed"], 1)
                dve.wait_ge(S["state_decayed"], c + 1)
                dve.wait_ge(S["state_psum"], c + 1)
                V.tensor_tensor(state[:, c + 1], off[:, 0], ps[:, state_bank[c]], ALU.add).then_inc(S["state_ready"], 1)
            dve.wait_ge(S["diag_psum"], GH)
            V.tensor_copy(ytok[:, 0], ps[:, 0]).then_inc(S["y_ready"], 1)
            for c in range(1, SNC):
                dve.wait_ge(S["off_psum"], c)
                V.tensor_tensor(by_head(off[:, c % 2]), by_head(ps[:, off_bank[c]]), per_head(T_EXP, c), ALU.mult).then_inc(S["off_scaled"], 1)
                dve.wait_ge(S["off_scaled"], c)
                V.tensor_tensor(ytok[:, c], off[:, c % 2], ps[:, c], ALU.add).then_inc(S["y_ready"], 1)
            dve.wait_ge(S["z_ready"], 4)
            for n in range(4):
                dve.wait_ge(S["back_psum"], n + 1)
                V.scalar_tensor_tensor(y[:, n], x[:, n], p1(G_D + n), ps[:, n], ALU.mult, ALU.add).then_inc(S["skipped"], 1)
                dve.wait_ge(S["skipped"], n + 1)
                V.tensor_tensor(y[:, n], y[:, n], z[:, n], ALU.mult).then_inc(S["gated"], 1)
            dve.wait_ge(S["inverse_ready"], 1)
            for n in range(4):
                V.scalar_tensor_tensor(ytok[:, n], y[:, n], p1(G_GAIN + n), inverse[:], ALU.mult, ALU.mult).then_inc(S["normed"], 1)
            for n in range(4):
                dve.wait_ge(S["high_done"], n + 1)
                V.tensor_tensor(mixed_lo[:, ds(8 + 4 * g + n, 1)].rearrange("p a t -> p (a t)"), ytok[:, n],
                                mixed_hi[:, ds(8 + 4 * g + n, 1)].rearrange("p a t -> p (a t)"), ALU.subtract).then_inc(S["low_done"], 1)

        @block.tensor
        def _(pe):
            mm = nc.tensor.matmul
            cut = lambda c: slice(c * SCH, (c + 1) * SCH)
            pe.wait_ge(S["silu_ready"], 2)
            for c in range(SNC):
                last = mm(ps[:, 6, cut(c)], x[:, 4, cut(c)], x[:, 5, cut(c)], start=True, stop=True)
            last.then_inc(S["cb_psum"], 1)
            for c in range(SNC):
                last = nc.tensor.transpose(ps[:, 7, cut(c)], x[:, 4, cut(c)], ident)
            last.then_inc(S["bt_psum"], 1)
            pe.wait_ge(S["silu_ready"], 6)
            for c in range(SNC):
                for n in range(4):
                    last = nc.tensor.transpose(ps[:, c, n * P:(n + 1) * P], x[:, n, cut(c)], ident)
                last.then_inc(S["xt_psum"], 1)
            pe.wait_ge(S["select_loaded"], 16)
            pe.wait_ge(S["xt_read"], 8)

            def segment(h):
                if h >= 3:
                    pe.wait_ge(S["seg_bounded"], SNC * (h - 2))
                mm(ps[:, seg_bank(h)], sel[32:64, h], acs[32:64, :], start=True, stop=True).then_inc(S["seg_psum"], 1)

            segment(0)
            segment(1)
            pe.wait_ge(S["bt_ready"], 1)
            pe.wait_ge(S["cb_ready"], 1)
            mm(ps[:, state_bank[0]], bt[:, 0], xw[:, 0], start=True, stop=True).then_inc(S["state_psum"], 1)
            for h in range(GH):
                if h + 2 < GH:
                    segment(h + 2)
                pe.wait_ge(S["scored"], h + 1)
                for c in range(SNC):
                    last = mm(ps[:, c, h * 64:(h + 1) * 64], m[:, h % 2, c], xdt[:, c, h * 64:(h + 1) * 64], start=True, stop=True)
                last.then_inc(S["diag_psum"], 1)
            pe.wait_ge(S["seg_bounded"], SNC * GH)
            for c in range(1, SNC - 1):
                mm(ps[:, state_bank[c]], bt[:, c], xw[:, c], start=True, stop=True).then_inc(S["state_psum"], 1)
            for c in range(1, SNC):
                pe.wait_ge(S["state_ready"], c)
                mm(ps[:, off_bank[c]], x[:, 5, cut(c)], state[:, c], start=True, stop=True).then_inc(S["off_psum"], 1)
            pe.wait_ge(S["y_ready"], 4)
            for n in range(4):
                for c in range(SNC):
                    last = nc.tensor.transpose(ps[:, n, cut(c)], ytok[:, c, n * P:(n + 1) * P], ident)
                last.then_inc(S["back_psum"], 1)
            for n in range(4):
                pe.wait_ge(S["squared"], n + 1)
                mm(ps[:, 7], mean, sq[:, n % 2], start=n == 0, stop=n == 3).then_inc(S["norm_psum"], 1)
    end_phase(nc, S)


MIX = 3


def mix_phase(nc, bufs, l, dram, mixed_hi, mixed_lo, act_hi, act_lo):
    projected, weights = dram["projected"], dram["w_branches"]
    S = phase_sems(nc, "mix", "w_loaded*6 high_ready*6 low_ready*6 product_done*6 gates_loaded*2 gates_ready*2 "
                       "rwkv_gated*2 ssd_gated*2 summed*2 high_done*2 low_done*2")
    steps = KT // 2
    with nc.sbuf_tensor("m_w", [P, 6, KT, P], F32) as w, nc.sbuf_tensor("m_whi", [P, 6, KT, P], F16) as w_hi, \
            nc.sbuf_tensor("m_wlo", [P, 6, KT, P], F16) as w_lo, nc.sbuf_tensor("m_gate", [P, 2, 2, T], F32) as gate, \
            nc.sbuf_tensor("m_part", [P, 2, 2, T], F32) as part, nc.sbuf_tensor("m_sum", [P, 2, T], F32) as total, \
            nc.psum_tensor("m_acc", [P, 4, T], F32) as acc, nc.Block() as block:
        flat = lambda a: a.rearrange("p a t -> p (a t)")

        @block.sync
        def _(sp):
            def load(i, s):
                sp.dma_start(w[:, s].rearrange("p k n -> p (k n)"), weights[l * KT * MIX + i * 6 + s]).then_inc(S["w_loaded"][s], 16)

            for s in range(6):
                load(0, s)
            with sp.Fori(1, steps) as i:
                for s in range(6):
                    sp.wait_ge(S["low_ready"][s], i)
                    load(i, s)

        @block.scalar
        def _(act):
            def half_step(i, x, first):
                if not first:
                    act.wait_ge(S["rwkv_gated"][x], i)
                    act.wait_ge(S["ssd_gated"][x], i)
                act.dma_start(gate[:, x, 0], projected[GA + 2 * i + x]).then_inc(S["gates_loaded"][x], 16)
                act.dma_start(gate[:, x, 1], projected[GB + 2 * i + x]).then_inc(S["gates_loaded"][x], 16)
                for s in range(3 * x, 3 * x + 3):
                    act.wait_ge(S["w_loaded"][s], 16 * i + 16)
                    if not first:
                        act.wait_ge(S["product_done"][s], i)
                    nc.scalar.activation(w_hi[:, s], w[:, s], ACT.Copy, scale=W_SCALE).then_inc(S["high_ready"][s], 1)
                act.wait_ge(S["gates_loaded"][x], 32 * i + 32)
                nc.scalar.activation(gate[:, x].rearrange("p a t -> p (a t)"), gate[:, x].rearrange("p a t -> p (a t)"), ACT.Sigmoid).then_inc(S["gates_ready"][x], 1)

            def split(i, x):
                act.wait_ge(S["summed"][x], i + 1)
                nc.scalar.activation(flat(act_hi[:, ds(2 * i + x, 1)]), total[:, x], ACT.Copy).then_inc(S["high_done"][x], 1)

            half_step(0, 0, True)
            half_step(0, 1, True)
            with act.Fori(1, steps) as i:
                for x in range(2):
                    split(i - 1, x)
                    half_step(i, x, False)
            for x in range(2):
                split(steps - 1, x)

        @block.tensor
        def _(pe):
            def products(i, first):
                for s in range(6):
                    x, n = divmod(s, 3)
                    pe.wait_ge(S["low_ready"][s], i + 1)
                    if not first and n == 0:
                        pe.wait_ge(S["rwkv_gated"][x], i)
                    if not first and n == 1:
                        pe.wait_ge(S["ssd_gated"][x], i)
                    a = acc[:, 2 * x + (n > 0)]
                    for k in range(KT):
                        z = KT * n + k
                        nc.tensor.matmul(a, w_hi[:, s, k], mixed_hi[:, z], start=k == 0 and n < 2, stop=False)
                        nc.tensor.matmul(a, w_hi[:, s, k], mixed_lo[:, z], start=False, stop=False)
                        last = nc.tensor.matmul(a, w_lo[:, s, k], mixed_hi[:, z], start=False, stop=k == KT - 1 and n != 1)
                    last.then_inc(S["product_done"][s], 1)

            products(0, True)
            with pe.Fori(1, steps) as i:
                products(i, False)

        @block.vector
        def _(dve):
            def gated(i, x):
                dve.wait_ge(S["gates_ready"][x], i + 1)
                dve.wait_ge(S["product_done"][3 * x], i + 1)
                nc.vector.scalar_tensor_tensor(part[:, x, 0], acc[:, 2 * x], 1.0 / W_SCALE, gate[:, x, 0], ALU.mult, ALU.mult).then_inc(S["rwkv_gated"][x], 1)
                dve.wait_ge(S["product_done"][3 * x + 2], i + 1)
                nc.vector.scalar_tensor_tensor(part[:, x, 1], acc[:, 2 * x + 1], 1.0 / W_SCALE, gate[:, x, 1], ALU.mult, ALU.mult).then_inc(S["ssd_gated"][x], 1)
                dve.wait_ge(S["rwkv_gated"][x], i + 1)
                dve.wait_ge(S["ssd_gated"][x], i + 1)
                nc.vector.tensor_tensor(total[:, x], part[:, x, 0], part[:, x, 1], ALU.add).then_inc(S["summed"][x], 1)
                dve.wait_ge(S["high_done"][x], i + 1)
                nc.vector.tensor_tensor(flat(act_lo[:, ds(2 * i + x, 1)]), total[:, x], flat(act_hi[:, ds(2 * i + x, 1)]), ALU.subtract).then_inc(S["low_done"][x], 1)

            def split_rest(i, x):
                for s in range(3 * x, 3 * x + 3):
                    dve.wait_ge(S["high_ready"][s], i + 1)
                    nc.vector.scalar_tensor_tensor(w_lo[:, s], w[:, s], W_SCALE, w_hi[:, s], ALU.mult, ALU.subtract).then_inc(S["low_ready"][s], 1)

            for x in range(2):
                split_rest(0, x)
            with dve.Fori(1, steps) as i:
                for x in range(2):
                    gated(i - 1, x)
                    split_rest(i, x)
            for x in range(2):
                gated(steps - 1, x)
    end_phase(nc, S)


def residual_phase(nc, bufs, l, weights, act_hi, act_lo):
    hT = bufs["hT"]
    S = phase_sems(nc, "residual", "w_loaded*4 high_ready*4 low_ready*4 product_done*4 added*4")
    steps = KT // SLOTS
    with nc.sbuf_tensor("o_w", [P, SLOTS, KT, P], F32) as w, nc.sbuf_tensor("o_whi", [P, SLOTS, KT, P], F16) as w_hi, \
            nc.sbuf_tensor("o_wlo", [P, SLOTS, KT, P], F16) as w_lo, \
            nc.psum_tensor("o_acc", [P, SLOTS, T], F32) as acc, nc.Block() as block:

        @block.sync
        def _(sp):
            for i in range(steps):
                for s in range(SLOTS):
                    if i:
                        sp.wait_ge(S["low_ready"][s], i)
                    sp.dma_start(w[:, s].rearrange("p k n -> p (k n)"), weights[l * KT + i * SLOTS + s]).then_inc(S["w_loaded"][s], 16)

        @block.scalar
        def _(act):
            for i in range(steps):
                for s in range(SLOTS):
                    act.wait_ge(S["w_loaded"][s], i * 16 + 16)
                    if i:
                        act.wait_ge(S["product_done"][s], i)
                    nc.scalar.activation(w_hi[:, s], w[:, s], ACT.Copy, scale=W_SCALE).then_inc(S["high_ready"][s], 1)

        @block.tensor
        def _(pe):
            for i in range(steps):
                for s in range(SLOTS):
                    pe.wait_ge(S["low_ready"][s], i + 1)
                    if i:
                        pe.wait_ge(S["added"][s], i)
                    for k in range(KT):
                        nc.tensor.matmul(acc[:, s], w_hi[:, s, k], act_hi[:, k], start=k == 0, stop=False)
                        nc.tensor.matmul(acc[:, s], w_hi[:, s, k], act_lo[:, k], start=False, stop=False)
                        last = nc.tensor.matmul(acc[:, s], w_lo[:, s, k], act_hi[:, k], start=False, stop=k == KT - 1)
                    last.then_inc(S["product_done"][s], 1)

        @block.vector
        def _(dve):
            def split_rest(i, s):
                dve.wait_ge(S["high_ready"][s], i + 1)
                nc.vector.scalar_tensor_tensor(w_lo[:, s], w[:, s], W_SCALE, w_hi[:, s], ALU.mult, ALU.subtract).then_inc(S["low_ready"][s], 1)

            for s in range(SLOTS):
                split_rest(0, s)
            for i in range(steps):
                for s in range(SLOTS):
                    n = i * SLOTS + s
                    dve.wait_ge(S["product_done"][s], i + 1)
                    nc.vector.scalar_tensor_tensor(hT[:, n], acc[:, s], 1.0 / W_SCALE, hT[:, n], ALU.mult, ALU.add).then_inc(S["added"][s], 1)
                    if i + 1 < steps:
                        split_rest(i + 1, s)
    end_phase(nc, S)


LOWEST = -3.0e38
GT = 8
BEFORE, BESIDE, BEHIND = 3, 4, 1
BLOCK_TILES = SLOTS * (BEFORE + BESIDE + BEHIND)


def route_phase(nc, bufs, l, tb, dram, routes, act_hi, act_lo):
    consts = bufs["consts"]
    queries, keys, down, hidden = dram["queries"], dram["keys"], dram["down"], dram["hidden"]
    con = lambda name, n: consts[:, CONSTS[name]:CONSTS[name] + n]
    ident, iota16, iota = con("ident", P), con("iota16", TOPK), con("iota128", P)
    H2 = 2 * HEADS
    S = phase_sems(nc, "route", "q_loaded keys_loaded scores_psum scores_ready top first_index rest second rest_index "
                       "pairs_ready best best_index pair_rest best_second pair_index shifted exp_ready summed inverse "
                       "gated position_row position_col float_ready one_hot picked chosen turned routes_ready "
                       "rows_ready*2 built*2 copied*2 gates_stored "
                       "down_loaded*4 down_high*4 down_low*4 hidden_psum*4 gelu_done*2 stored*2")
    with ExitStack() as mem:
        sb = lambda name, shape, dt=F32: mem.enter_context(nc.sbuf_tensor("t_" + name, shape, dt))
        dense = sb("dense", [P, NKEYS, P])
        arena = dense[:].rearrange("p j t -> p (j t)")
        q, key, scores, scores2, pair, pair2 = (arena[:, 2048 * n:2048 * (n + 1)] for n in range(6))
        q, key, scores, scores2 = (a.rearrange("p (n k) -> p n k", n=H2) for a in (q, key, scores, scores2))
        hot = arena[:, 4 * 2048:6 * 2048].rearrange("p (c h k m) -> p c h k m", c=2, h=HEADS, k=TOPK)
        pair, pair2 = (a.rearrange("p (h m) -> p h m", h=HEADS) for a in (pair, pair2))
        top, topi, topf = sb("top", [P, H2, TOPK]), sb("topi", [P, H2, TOPK], U32), sb("topf", [P, H2, TOPK])
        best, bpos = sb("best", [P, HEADS, TOPK]), sb("bpos", [P, HEADS, TOPK], U32)
        pos, posf = sb("pos", [P, 2, HEADS, TOPK], U32), sb("posf", [P, 2, HEADS, TOPK])
        ex, total, inv = sb("ex", [P, HEADS, TOPK]), sb("sum", [P, HEADS]), sb("inv", [P, HEADS])
        out = sb("out", [P, 3, HEADS, TOPK])
        rows, cols = sb("rows", [P, 2, GT, P]), sb("cols", [P, 2, GT, P])
        dn, d_hi, d_lo = sb("down", [P, SLOTS, D]), sb("dhi", [P, SLOTS, KT, P], F16), sb("dlo", [P, SLOTS, KT, P], F16)
        gelu = sb("gelu", [P, 2, T])
        ps = mem.enter_context(nc.psum_tensor("t_ps", [P, 4, T], F32))
        turn = mem.enter_context(nc.psum_tensor("t_turn", [P, 4, P], F32))
        acc = mem.enter_context(nc.psum_tensor("t_acc", [P, 2, T], F32))
        block = mem.enter_context(nc.Block())
        flat = lambda a: a.rearrange("p k n -> p (k n)")
        bank = lambda i, s: (s % 2, 2 * i + s // 2)
        steps = BLOCK_TILES // SLOTS

        @block.sync
        def _(sp):
            def load(i, s, first=False):
                if not first:
                    sp.wait_ge(S["down_low"][s], i)
                sp.dma_start(dn[:, s], down[l * NKEYS + tb * BLOCK_TILES + i * SLOTS + s]).then_inc(S["down_loaded"][s], 16)

            def store(i, s):
                x, n = bank(i, s)
                sp.wait_ge(S["gelu_done"][x], n + 1)
                sp.dma_start(hidden[tb * BLOCK_TILES + i * SLOTS + s], gelu[:, x]).then_inc(S["stored"][x], 16)

            sp.dma_start(q, queries.rearrange("n p t -> p n t")[:, :, ds(tb * P, P)]).then_inc(S["q_loaded"], 16)
            for s in range(SLOTS):
                load(0, s, True)
            with sp.Fori(1, steps) as i:
                for s in range(SLOTS):
                    load(i, s)
                    store(i - 1, s)
            for x in range(2):
                sp.wait_ge(S["copied"][x], 2 * P // (2 * GT))
            sp.dma_start(dram["gates"].rearrange("j p t -> p j t")[:, :, ds(tb * P, P)], dense[:]).then_inc(S["gates_stored"], 16)
            for s in range(SLOTS):
                store(steps - 1, s)
            for x in range(2):
                sp.wait_ge(S["stored"][x], 16 * BLOCK_TILES // 2)
            sp.wait_ge(S["gates_stored"], 16)

        @block.scalar
        def _(act):
            def split_down(i, s, first=False):
                act.wait_ge(S["down_loaded"][s], 16 * i + 16)
                if not first:
                    act.wait_ge(S["hidden_psum"][s], i)
                nc.scalar.activation(flat(d_hi[:, s]), dn[:, s], ACT.Copy, scale=W_SCALE).then_inc(S["down_high"][s], 1)

            def activate(i, s, first=False):
                x, n = bank(i, s)
                if not first:
                    act.wait_ge(S["stored"][x], 16 * n)
                act.wait_ge(S["hidden_psum"][s], i + 1)
                nc.scalar.activation(gelu[:, x], acc[:, x], ACT.Gelu_apprx_tanh, scale=1.0 / W_SCALE).then_inc(S["gelu_done"][x], 1)

            def copy_gates(i, h):
                x, n = h % 2, 2 * i + h // 2
                act.wait_ge(S["built"][x], n + 1)
                for b in range(2):
                    nc.scalar.activation(dense[:, :, ds((4 * i + h) * GT + 4 * b, 4)], ps[:, 2 * x + b].rearrange("p (t j) -> p j t", t=4),
                                         ACT.Copy).then_inc(S["copied"][x], 1)

            act.dma_start(flat(key), keys[l]).then_inc(S["keys_loaded"], 16)
            for s in range(SLOTS):
                split_down(0, s, True)
            for n in range(4):
                act.wait_ge(S["scores_psum"], n + 1)
                nc.scalar.activation(flat(scores[:, 4 * n:4 * n + 4]), ps[:, n], ACT.Copy).then_inc(S["scores_ready"], 1)
            for i in range(BEFORE):
                for z in range(SLOTS):
                    activate(i, z, i == 0 and z < 2)
                    if i < BEFORE - 1:
                        split_down(i + 1, z)
            act.wait_ge(S["shifted"], 1)
            nc.scalar.activation(ex[:], ex[:], ACT.Exp).then_inc(S["exp_ready"], 1)
            for z in range(SLOTS):
                split_down(BEFORE, z)
            act.wait_ge(S["turned"], 1)
            nc.scalar.activation(routes[:, :, ds(tb * P, P)], turn[:, 0:3], ACT.Copy).then_inc(S["routes_ready"], 1)
            with act.Fori(0, BESIDE) as i:
                for h in range(SLOTS):
                    activate(i + BEFORE, h)
                    split_down(i + BEFORE + 1, h)
                    copy_gates(i, h)
            for z in range(SLOTS):
                activate(steps - 1, z)

        @block.tensor
        def _(pe):
            mm = nc.tensor.matmul

            def hidden_products(i, s, first=False):
                x, n = bank(i, s)
                pe.wait_ge(S["down_low"][s], i + 1)
                if not first:
                    pe.wait_ge(S["gelu_done"][x], n)
                for k in range(KT):
                    mm(acc[:, x], d_hi[:, s, k], act_hi[:, k], start=k == 0, stop=False)
                    mm(acc[:, x], d_hi[:, s, k], act_lo[:, k], start=False, stop=False)
                    last = mm(acc[:, x], d_lo[:, s, k], act_hi[:, k], start=False, stop=k == KT - 1)
                last.then_inc(S["hidden_psum"][s], 1)

            def gate_products(i, h, first=False):
                x, n = h % 2, 2 * i + h // 2
                pe.wait_ge(S["rows_ready"][x], n + 1)
                if not first:
                    pe.wait_ge(S["copied"][x], 2 * n)
                for t in range(GT):
                    last = mm(ps[:, 2 * x + t // 4, (t % 4) * P:(t % 4 + 1) * P], rows[:, x, t], cols[:, x, t], start=True, stop=True)
                last.then_inc(S["built"][x], 1)

            pe.wait_ge(S["q_loaded"], 16)
            pe.wait_ge(S["keys_loaded"], 16)
            for n in range(4):
                for x in range(4):
                    last = mm(ps[:, n, x * P:(x + 1) * P], q[:, 4 * n + x], key[:, 4 * n + x], start=True, stop=True)
                last.then_inc(S["scores_psum"], 1)
            for i in range(BEFORE):
                for z in range(SLOTS):
                    hidden_products(i, z, i == 0 and z < 2)
            pe.wait_ge(S["gated"], 1)
            pe.wait_ge(S["chosen"], 2)
            for n in range(3):
                last = nc.tensor.transpose(turn[:, n], out[:, n].rearrange("p h k -> p (h k)"), ident)
            last.then_inc(S["turned"], 1)
            for h in range(SLOTS):
                hidden_products(BEFORE, h)
                gate_products(0, h, h < 2)
            with pe.Fori(1, BESIDE) as i:
                for h in range(SLOTS):
                    hidden_products(i + BEFORE, h)
                    gate_products(i, h)
            for z in range(SLOTS):
                hidden_products(steps - 1, z)

        @block.vector
        def _(dve):
            V = nc.vector

            def split_down(i, s):
                dve.wait_ge(S["down_high"][s], i + 1)
                V.scalar_tensor_tensor(flat(d_lo[:, s]), dn[:, s], W_SCALE, flat(d_hi[:, s]), ALU.mult, ALU.subtract).then_inc(S["down_low"][s], 1)

            def build(i, h, first=False):
                x, n = h % 2, 2 * i + h // 2
                if not first:
                    dve.wait_ge(S["built"][x], n)
                for t in range(GT):
                    at = tb * P + (4 * i + h) * GT + t
                    V.tensor_scalar(rows[:, x, t], iota, routes[:, 0, ds(at, 1)], routes[:, 2, ds(at, 1)], ALU.is_equal, ALU.mult)
                    last = V.tensor_scalar(cols[:, x, t], iota, routes[:, 1, ds(at, 1)], None, ALU.is_equal)
                last.then_inc(S["rows_ready"][x], 1)

            for z in range(SLOTS):
                split_down(0, z)
            for n in range(H2):
                if n % 4 == 0:
                    dve.wait_ge(S["scores_ready"], n // 4 + 1)
                V.max(top[:, n, 0:8], scores[:, n]).then_inc(S["top"], 1)
            split_down(1, 0)
            for n in range(H2):
                if n == H2 // 2:
                    split_down(1, 1)
                dve.wait_ge(S["top"], n + 1)
                V.max_index(topi[:, n, 0:8], top[:, n, 0:8], scores[:, n]).then_inc(S["first_index"], 1)
                V.match_replace(scores2[:, n], top[:, n, 0:8], scores[:, n], LOWEST).then_inc(S["rest"], 1)
            for n in range(H2):
                dve.wait_ge(S["rest"], n + 1)
                V.max(top[:, n, 8:16], scores2[:, n]).then_inc(S["second"], 1)
            split_down(1, 2)
            for n in range(H2):
                dve.wait_ge(S["second"], n + 1)
                V.max_index(topi[:, n, 8:16], top[:, n, 8:16], scores2[:, n]).then_inc(S["rest_index"], 1)
            dve.wait_ge(S["top"], H2)
            halves = top[:].rearrange("p (h c) k -> p h c k", c=2)
            V.tensor_tensor(pair.rearrange("p h (a b) -> p h a b", a=TOPK), halves[:, :, 0].unsqueeze(3).broadcast_to([P, HEADS, TOPK, TOPK]),
                            halves[:, :, 1].unsqueeze(2).broadcast_to([P, HEADS, TOPK, TOPK]), ALU.add).then_inc(S["pairs_ready"], 1)
            split_down(1, 3)
            dve.wait_ge(S["pairs_ready"], 1)
            for h in range(HEADS):
                V.max(best[:, h, 0:8], pair[:, h]).then_inc(S["best"], 1)
            for h in range(HEADS):
                dve.wait_ge(S["best"], h + 1)
                V.max_index(bpos[:, h, 0:8], best[:, h, 0:8], pair[:, h]).then_inc(S["best_index"], 1)
                V.match_replace(pair2[:, h], best[:, h, 0:8], pair[:, h], LOWEST).then_inc(S["pair_rest"], 1)
            split_down(2, 0)
            for h in range(HEADS):
                dve.wait_ge(S["pair_rest"], h + 1)
                V.max(best[:, h, 8:16], pair2[:, h]).then_inc(S["best_second"], 1)
            for h in range(HEADS):
                dve.wait_ge(S["best_second"], h + 1)
                V.max_index(bpos[:, h, 8:16], best[:, h, 8:16], pair2[:, h]).then_inc(S["pair_index"], 1)
            split_down(2, 1)
            V.tensor_tensor(ex[:], best[:], best[:, :, 0:1].broadcast_to([P, HEADS, TOPK]), ALU.subtract).then_inc(S["shifted"], 1)
            dve.wait_ge(S["pair_index"], HEADS)
            dve.wait_ge(S["best_index"], HEADS)
            V.tensor_scalar(pos[:, 0], bpos[:], 4, None, ALU.logical_shift_right).then_inc(S["position_row"], 1)
            V.tensor_scalar(pos[:, 1], bpos[:], 15, None, ALU.bitwise_and).then_inc(S["position_col"], 1)
            dve.wait_ge(S["first_index"], H2)
            dve.wait_ge(S["rest_index"], H2)
            V.tensor_copy(topf[:], topi[:]).then_inc(S["float_ready"], 1)
            dve.wait_ge(S["position_row"], 1)
            dve.wait_ge(S["position_col"], 1)
            V.tensor_copy(posf[:], pos[:]).then_inc(S["float_ready"], 1)
            split_down(2, 2)
            dve.wait_ge(S["float_ready"], 2)
            index = topf[:].rearrange("p (h c) k -> p h c k", c=2)
            for c in range(2):
                for h in range(HEADS):
                    V.tensor_tensor(hot[:, c, h], posf[:, c, h].unsqueeze(2).broadcast_to([P, TOPK, TOPK]),
                                    iota16.unsqueeze(1).broadcast_to([P, TOPK, TOPK]), ALU.is_equal).then_inc(S["one_hot"], 1)
            split_down(2, 3)
            for c in range(2):
                dve.wait_ge(S["one_hot"], HEADS * (c + 1))
                V.tensor_tensor(hot[:, c], hot[:, c], index[:, :, c].unsqueeze(2).broadcast_to([P, HEADS, TOPK, TOPK]), ALU.mult).then_inc(S["picked"], 1)
                dve.wait_ge(S["picked"], c + 1)
                V.tensor_reduce(out[:, c], hot[:, c], AX.X, ALU.add).then_inc(S["chosen"], 1)
            dve.wait_ge(S["exp_ready"], 1)
            V.tensor_reduce(total[:], ex[:], AX.X, ALU.add).then_inc(S["summed"], 1)
            dve.wait_ge(S["summed"], 1)
            V.reciprocal(inv[:], total[:]).then_inc(S["inverse"], 1)
            dve.wait_ge(S["inverse"], 1)
            V.tensor_tensor(out[:, 2], ex[:], inv[:].unsqueeze(2).broadcast_to([P, HEADS, TOPK]), ALU.mult).then_inc(S["gated"], 1)
            for z in range(SLOTS):
                split_down(BEFORE, z)
            dve.wait_ge(S["routes_ready"], 1)
            for h in range(SLOTS):
                build(0, h, h < 2)
                split_down(BEFORE + 1, h)
            with dve.Fori(1, BESIDE) as i:
                for h in range(SLOTS):
                    build(i, h)
                    split_down(i + BEFORE + 1, h)
    end_phase(nc, S)


EG = 8
BANKS = 4


def output_phase(nc, bufs, l, dram):
    hT = bufs["hT"]
    gates, hidden = dram["gates"], dram["hidden"]
    up_tiles = dram["up"].rearrange("l (i j) d -> l j i d", j=NKEYS)
    S = phase_sems(nc, "output", "up_loaded*2 gate_loaded*2 hidden_loaded*2 up_high*2 up_low*2 weighted*2 share_high*2 "
                       "share_low*2 out_psum added")
    groups = NKEYS // EG
    with ExitStack() as mem:
        sb = lambda name, shape, dt=F32: mem.enter_context(nc.sbuf_tensor("x_" + name, shape, dt))
        u, u_hi, u_lo = sb("up", [P, 2, D]), sb("uhi", [P, 2, EG, D], F16), sb("ulo", [P, 2, EG, D], F16)
        gate, hid, share = sb("gate", [P, 2, T]), sb("hid", [P, 2, T]), sb("share", [P, 2, T])
        s_hi, s_lo = sb("shi", [P, 2, EG, T], F16), sb("slo", [P, 2, EG, T], F16)
        ps = mem.enter_context(nc.psum_tensor("x_ps", [P, BANKS, T], F32))
        block = mem.enter_context(nc.Block())
        count = lambda g, e: 4 * g + e // 2

        @block.sync
        def _(sp):
            def loads(g, e, first=False):
                x, n = e % 2, count(g, e)
                j = g * EG + e
                if not first:
                    sp.wait_ge(S["up_low"][x], n)
                sp.dma_start(u[:, x], up_tiles[ds(l, 1), ds(j, 1)].rearrange("a b i d -> i (a b d)")).then_inc(S["up_loaded"][x], 16)
                if not first:
                    sp.wait_ge(S["weighted"][x], n)
                sp.dma_start(gate[:, x], gates[j]).then_inc(S["gate_loaded"][x], 16)
                sp.dma_start(hid[:, x], hidden[j]).then_inc(S["hidden_loaded"][x], 16)

            for e in range(EG):
                loads(0, e, e < 2)
            with sp.Fori(1, groups) as g:
                for e in range(EG):
                    loads(g, e)

        @block.scalar
        def _(act):
            def split(g, half, e, first=False):
                x, n = e % 2, count(g, e)
                act.wait_ge(S["up_loaded"][x], 16 * n + 16)
                if not first:
                    act.wait_ge(S["out_psum"], KT * (g - 1))
                nc.scalar.activation(u_hi[:, half, e], u[:, x], ACT.Copy, scale=W_SCALE).then_inc(S["up_high"][x], 1)
                act.wait_ge(S["weighted"][x], n + 1)
                nc.scalar.activation(s_hi[:, half, e], share[:, x], ACT.Copy).then_inc(S["share_high"][x], 1)

            for g in range(2):
                for e in range(EG):
                    split(g, g, e, True)
            with act.Fori(1, groups // 2) as i:
                for half in range(2):
                    for e in range(EG):
                        split(2 * i + half, half, e)

        @block.vector
        def _(dve):
            V = nc.vector

            def weigh(g, half, e, first=False):
                x, n = e % 2, count(g, e)
                dve.wait_ge(S["gate_loaded"][x], 16 * n + 16)
                dve.wait_ge(S["hidden_loaded"][x], 16 * n + 16)
                if not first:
                    dve.wait_ge(S["share_high"][x], n)
                V.tensor_tensor(share[:, x], hid[:, x], gate[:, x], ALU.mult).then_inc(S["weighted"][x], 1)
                dve.wait_ge(S["up_high"][x], n + 1)
                V.scalar_tensor_tensor(u_lo[:, half, e], u[:, x], W_SCALE, u_hi[:, half, e], ALU.mult, ALU.subtract).then_inc(S["up_low"][x], 1)
                dve.wait_ge(S["share_high"][x], n + 1)
                V.tensor_tensor(s_lo[:, half, e], share[:, x], s_hi[:, half, e], ALU.subtract).then_inc(S["share_low"][x], 1)

            def add(g, k):
                dve.wait_ge(S["out_psum"], KT * g + k + 1)
                V.scalar_tensor_tensor(hT[:, k], ps[:, k % BANKS], 1.0 / W_SCALE, hT[:, k], ALU.mult, ALU.add).then_inc(S["added"], 1)

            for e in range(EG):
                weigh(0, 0, e, e < 2)
            for e in range(EG):
                weigh(1, 1, e)
                add(0, e)
            with dve.Fori(1, groups // 2) as i:
                for half in range(2):
                    for e in range(EG):
                        weigh(2 * i + half, half, e)
                        add(2 * i + half - 1, e)
            for k in range(KT):
                add(groups - 1, k)

        @block.tensor
        def _(pe):
            mm = nc.tensor.matmul

            def output(g, half, first=False):
                for k in range(KT):
                    if not (first and k < BANKS):
                        pe.wait_ge(S["added"], KT * g + k - BANKS + 1)
                    cut = slice(k * P, (k + 1) * P)
                    for e in range(EG):
                        if k == 0:
                            pe.wait_ge(S["up_low"][e % 2], count(g, e) + 1)
                            pe.wait_ge(S["share_low"][e % 2], count(g, e) + 1)
                        mm(ps[:, k % BANKS], u_hi[:, half, e, cut], s_hi[:, half, e], start=e == 0, stop=False)
                        mm(ps[:, k % BANKS], u_hi[:, half, e, cut], s_lo[:, half, e], start=False, stop=False)
                        last = mm(ps[:, k % BANKS], u_lo[:, half, e, cut], s_hi[:, half, e], start=False, stop=e == EG - 1)
                    last.then_inc(S["out_psum"], 1)

            output(0, 0, True)
            output(1, 1)
            with pe.Fori(1, groups // 2) as i:
                for half in range(2):
                    output(2 * i + half, half)
    end_phase(nc, S)


def load_phase(nc, bufs, dram):
    S = phase_sems(nc, "load", "loaded")
    with nc.Block() as block:

        @block.sync
        def _(sp):
            sp.dma_start(bufs["consts"][:], dram["consts"]).then_inc(S["loaded"], 16)
            sp.dma_start(bufs["hT"][:].rearrange("p k t -> p (k t)"), dram["x"]).then_inc(S["loaded"], 16)
            sp.wait_ge(S["loaded"], 32)
    end_phase(nc, S)


def params_phase(nc, bufs, l, dram):
    S = phase_sems(nc, "params", "loaded")
    with nc.Block() as block:

        @block.sync
        def _(sp):
            sp.dma_start(bufs["params"][:], dram["params"][l]).then_inc(S["loaded"], 16)
            sp.wait_ge(S["loaded"], 16)
    end_phase(nc, S)


def trunk(nc, dram, out):
    internal = lambda name, shape: nc.dram_tensor(name, shape, F32, kind="Internal").ap()
    dram = dict(dram)
    dram["projected"] = internal("projected", [IN_TILES, P, T])
    dram["v_mixed"] = internal("v_mixed", [LAYERS * KT, P, T])
    dram["queries"] = internal("queries", [2 * HEADS, P, T])
    dram["gates"] = internal("gates", [NKEYS, P, T])
    dram["hidden"] = internal("hidden", [NKEYS, P, T])
    sb = lambda name, shape, dt=F32: nc.sbuf_tensor(name, shape, dt)
    split = lambda name, n: (sb(name + "_hi", [P, n, T], F16), sb(name + "_lo", [P, n, T], F16))
    with sb("hT", [P, KT, T]) as hT, sb("consts", [P, N_CONSTS]) as consts, sb("params", [P, N_PARAMS]) as params:
        bufs = {"hT": hT, "consts": consts, "params": params}
        load_phase(nc, bufs, dram)
        with nc.Fori(0, LAYERS) as l:
            params_phase(nc, bufs, l, dram)
            with sb("u_hi", [P, KT, T], F16) as act_hi, sb("u_lo", [P, KT, T], F16) as act_lo:
                norm_phase(nc, bufs, "norm_mix", PARAMS["norm_mix"], act_hi, act_lo)
                project_phase(nc, bufs, l, dram["w_in"], IN_TILES, act_hi, act_lo, dram["projected"], "in")
            with sb("mixed_hi", [P, 24, T], F16) as mixed_hi, sb("mixed_lo", [P, 24, T], F16) as mixed_lo:
                with sb("low_wa", [P, T]) as low_wa, sb("low_g", [P, T]) as low_g, sb("low_gv", [P, T]) as low_gv:
                    lora = low_wa, low_g, low_gv
                    lora_phase(nc, bufs, l, lora, dram)
                    rwkv_pairs(nc, bufs, l, lora, dram, mixed_hi, mixed_lo)
                with sb("acs", [P, T]) as acs, sb("table", [P, SSD_GROUPS, 5, SNC, GROUP_HEADS]) as table:
                    dt_phase(nc, bufs, l, dram, acs, table)
                    with nc.Fori(0, SSD_GROUPS) as g:
                        ssd_group_phase(nc, bufs, l, g, dram, acs, table, mixed_hi, mixed_lo)
                with sb("o_hi", [P, KT, T], F16) as act_hi, sb("o_lo", [P, KT, T], F16) as act_lo:
                    mix_phase(nc, bufs, l, dram, mixed_hi, mixed_lo, act_hi, act_lo)
                    residual_phase(nc, bufs, l, dram["w_out"], act_hi, act_lo)
            with sb("f_hi", [P, KT, T], F16) as act_hi, sb("f_lo", [P, KT, T], F16) as act_lo:
                norm_phase(nc, bufs, "norm_ffn", PARAMS["norm_ffn"], act_hi, act_lo)
                project_phase(nc, bufs, l, dram["w_q"], 2 * HEADS, act_hi, act_lo, dram["queries"], "q")
                with sb("routes", [P, 3, T]) as routes:
                    with nc.Fori(0, TB) as tb:
                        route_phase(nc, bufs, l, tb, dram, routes, act_hi, act_lo)
            output_phase(nc, bufs, l, dram)
        norm_phase(nc, bufs, "norm_final", PARAMS["norm_final"], None, None, out)


def kernel(**inputs):
    import concourse.bacc as bacc
    from concourse.bass_utils import run_bass_kernel_spmd

    a = {k: np.asarray(v) for k, v in inputs.items()}
    f = np.float32
    L = LAYERS

    def zeros(*shape):
        return np.zeros(shape, f)

    def tiles(w):
        n = w.shape[2] // P
        return np.ascontiguousarray(w.reshape(L, w.shape[1] // P, P, n, P).transpose(0, 3, 2, 1, 4)).reshape(L * n, P, -1)

    def columns(v):
        return v.reshape(L, -1, P).transpose(0, 2, 1)

    def in_order(v):
        pad = zeros(*v.shape[:-1], P)
        rwkv, gd = v[..., 0:3200], v[..., 3200:3360]
        z, xbc, dt, gates = v[..., 3360:5408], v[..., 5408:8480], v[..., 8480:8512], v[..., 8512:10560]
        return np.concatenate([rwkv, gd, dt, pad[..., 0:64], z, xbc, gates, pad], axis=-1)

    first = lambda v: np.concatenate([zeros(1, *v.shape[1:]), v])
    v0, v1, v2 = first(a["rwkv_v0"]), first(a["rwkv_v1"]), first(a["rwkv_v2"])
    mu = np.concatenate([a["rwkv_mu"], zeros(L, 96)], axis=-1)
    at_dt = lambda v: np.concatenate([zeros(L, 32), v, zeros(L, 64)], axis=-1)
    final = np.broadcast_to(a["norm_final_g"], (L, D))
    conv_w = np.concatenate([columns(a["ssd_conv_w"][:, j]) for j in range(4)], axis=-1)
    per_feature = np.repeat(a["ssd_D"], 64, axis=-1)
    params = np.concatenate([columns(v) for v in (
        a["norm_mix_g"], mu, a["rwkv_w0"], a["rwkv_a0"], v0, a["rwkv_k_k"], a["rwkv_k_a"],
        a["rwkv_r_k"].reshape(L, -1), a["rwkv_ln_w"], a["rwkv_ln_b"])] + [conv_w] + [columns(v) for v in (
            a["ssd_conv_b"], a["ssd_norm_g"], per_feature, at_dt(a["ssd_dt_bias"]), at_dt(a["ssd_A_log"]),
            a["norm_ffn_g"], final)], axis=-1)
    p = PARAMS
    pair_pack = zeros(L, RWKV_TILES, P, PACK_COLS)
    for n in range(RWKV_TILES):
        cut = slice(n * P, (n + 1) * P)
        pair_pack[:, n, 0:64, 0:P] = a["rwkv_w2"][:, :, cut]
        pair_pack[:, n, 64:128, 0:P] = a["rwkv_a2"][:, :, cut]
        pair_pack[:, n, :, P:2 * P] = a["rwkv_g2"][:, 0:P, cut]
        pair_pack[:, n, 0:32, 2 * P:3 * P] = a["rwkv_g2"][:, P:160, cut]
        pair_pack[:, n, 32:64, 2 * P:3 * P] = v2[:, :, cut]
        for col, at in ((MU_R, p["mu"] + R0), (MU_K, p["mu"] + K0), (W0, p["w0"]), (A0, p["a0"]), (V0P, p["v0"]),
                        (K_K, p["k_k"]), (K_A, p["k_a"]), (R_K, p["r_k"]), (LN_W, p["ln_w"]), (LN_B, p["ln_b"])):
            pair_pack[:, n, :, col] = params[:, :, at + n]
    group_pack = zeros(L, SSD_GROUPS, P, GROUP_COLS)
    for g in range(SSD_GROUPS):
        for n, t in enumerate([4 * g, 4 * g + 1, 4 * g + 2, 4 * g + 3, 16 + g, 20 + g]):
            for j in range(4):
                group_pack[:, g, :, G_CONV + 4 * n + j] = params[:, :, p["conv_w"] + 24 * j + t]
            group_pack[:, g, :, G_BIAS + n] = params[:, :, p["conv_b"] + t]
        for n in range(4):
            group_pack[:, g, :, G_GAIN + n] = params[:, :, p["ssd_norm"] + 4 * g + n]
            group_pack[:, g, :, G_D + n] = params[:, :, p["D"] + 4 * g + n]
    select = zeros(SSD_GROUPS, 32, GROUP_HEADS, P)
    for h in range(SSD_HEADS):
        select[h // GROUP_HEADS, h, h % GROUP_HEADS] = 1.0
    branches = np.stack([tiles(a["w_rwkv_branch"]).reshape(L, KT, P, D),
                         tiles(a["w_ssd_branch"][:, 0:D]).reshape(L, KT, P, D),
                         tiles(a["w_ssd_branch"][:, D:]).reshape(L, KT, P, D)], axis=2).reshape(L * KT * MIX, P, D)
    down = a["peer_down"].reshape(L, NKEYS, NKEYS, KT, P).transpose(0, 2, 4, 3, 1)
    arrays = {
        "x": np.ascontiguousarray(a["x"][0].T.reshape(KT, P, T).transpose(1, 0, 2)).reshape(P, KT * T),
        "consts": make_consts(), "select": select.reshape(SSD_GROUPS, 32, -1), "params": params,
        "w_in": tiles(in_order(a["w_in"])), "w_branches": branches, "w_out": tiles(a["w_out"]),
        "w_q": tiles(a["peer_w_q"]), "pair_pack": pair_pack.reshape(L * RWKV_TILES, P, PACK_COLS),
        "group_pack": group_pack.reshape(L * SSD_GROUPS, P, GROUP_COLS),
        "v1": v1.reshape(L, KT, P, 32).transpose(0, 2, 1, 3).reshape(L, P, KT * 32),
        "keys": a["peer_sub_keys"].reshape(L, 2 * HEADS, NKEYS, P).transpose(0, 3, 1, 2).reshape(L, P, -1),
        "down": down.reshape(L * NKEYS, P, D), "up": a["peer_up"],
    }
    nc = bacc.Bacc("TRN2", target_bir_lowering=False, num_devices=1)
    data, dram = {}, {}
    for name, v in arrays.items():
        data["in_" + name] = np.ascontiguousarray(v)
        dram[name] = nc.dram_tensor("in_" + name, v.shape, F32, kind="ExternalInput").ap()
    out = nc.dram_tensor("out_t", (P, KT, T), F32, kind="ExternalOutput").ap()
    trunk(nc, dram, out)
    r = run_bass_kernel_spmd(nc, [data], core_ids=[0])
    got = np.asarray(r.results[0]["out_t"])
    return np.ascontiguousarray(got.transpose(1, 0, 2).reshape(D, T).T)[None]
```
